# Optimizing a Trainium2 kernel written in Bass

```python
import jax, jax.numpy as jnp
from jax import lax
import numpy as np
import math

D_MODEL = 1024
BATCH = 1
SEQ = 512
DEPTH = 1

A_HEADS = 8
A_KV_HEADS = 2
A_HEAD_DIM = 64
IDX_HEADS = 8
IDX_DIM = 64
TOPK_MAX = 256
B_HEADS = 8
B_HEAD_DIM = 64
A_WIDTH = A_HEADS * A_HEAD_DIM
B_WIDTH = B_HEADS * B_HEAD_DIM
MIX_WIDTH = A_WIDTH + B_WIDTH
A_KV_WIDTH = A_KV_HEADS * A_HEAD_DIM
IDX_Q_WIDTH = IDX_HEADS * IDX_DIM
IN_SPLITS = (A_WIDTH, A_KV_WIDTH, A_KV_WIDTH, IDX_Q_WIDTH, IDX_DIM, IDX_HEADS,
             B_WIDTH, B_WIDTH, B_WIDTH, B_HEADS)
IN_COLS = sum(IN_SPLITS)
Q_BLOCK = 128
N_GROUPS = 4
EXPERTS_PER_GROUP = 8
N_EXPERTS = N_GROUPS * EXPERTS_PER_GROUP
TOPK_EXPERT = 2
D_FF_EXPERT = D_MODEL // 4
N_MOD = 6
EPS = 1e-6


def rms_norm(x, g):
    xf = x.astype(jnp.float32)
    y = xf * lax.rsqrt(jnp.mean(xf * xf, axis=-1, keepdims=True) + EPS)
    return (y * g.astype(jnp.float32)).astype(x.dtype)

def alibi_slopes(n):
    return jnp.exp2(-8.0 * jnp.arange(1, n + 1, dtype=jnp.float32) / n)

def to_blocks(a, nb):
    return jnp.moveaxis(a.reshape(a.shape[0], nb, Q_BLOCK, *a.shape[2:]), 1, 0)

def dsa_attention(q, k, v, iq, ik, iw):
    bsz, L = q.shape[0], q.shape[1]
    n_top = min(TOPK_MAX, L // 4)
    nb = L // Q_BLOCK
    rep = A_HEADS // A_KV_HEADS
    slopes = alibi_slopes(A_HEADS).reshape(A_KV_HEADS, rep)
    scale = A_HEAD_DIM ** -0.5
    kpos = jnp.arange(L)
    ikf = ik.astype(jnp.float32)

    def block(args):
        qb, iqb, iwb, t0 = args
        tpos = t0 + jnp.arange(Q_BLOCK)
        dots = jnp.einsum('bqhd,bsd->bqhs', iqb.astype(jnp.float32), ikf)
        score = jnp.einsum('bqh,bqhs->bqs', iwb.astype(jnp.float32), jax.nn.relu(dots))
        causal = kpos[None, :] <= tpos[:, None]
        score = jnp.where(causal[None], score, -jnp.inf)
        _, idx = lax.top_k(score, n_top)
        valid = idx <= tpos[None, :, None]
        ksel = jax.vmap(lambda kb, ib: kb[ib])(k, idx)
        vsel = jax.vmap(lambda vb, ib: vb[ib])(v, idx)
        qg = qb.reshape(bsz, Q_BLOCK, A_KV_HEADS, rep, A_HEAD_DIM)
        logits = jnp.einsum('bqgrd,bqkgd->bqgrk', qg, ksel).astype(jnp.float32) * scale
        dist = (tpos[None, :, None] - idx).astype(jnp.float32)
        logits = logits - slopes[None, None, :, :, None] * dist[:, :, None, None, :]
        logits = jnp.where(valid[:, :, None, None, :], logits, -jnp.inf)
        p = jax.nn.softmax(logits, axis=-1).astype(v.dtype)
        o = jnp.einsum('bqgrk,bqkgd->bqgrd', p, vsel)
        return o.reshape(bsz, Q_BLOCK, A_WIDTH)

    out = lax.map(block, (to_blocks(q, nb), to_blocks(iq, nb), to_blocks(iw, nb),
                          jnp.arange(nb, dtype=jnp.int32) * Q_BLOCK))
    return jnp.moveaxis(out, 0, 1).reshape(bsz, L, A_WIDTH)

def forgetting_attention(q, k, v, log_f):
    bsz, L = q.shape[0], q.shape[1]
    nb = L // Q_BLOCK
    scale = B_HEAD_DIM ** -0.5
    cum = jnp.cumsum(log_f, axis=1)
    cum_k = jnp.transpose(cum, (0, 2, 1))
    kpos = jnp.arange(L)

    def block(args):
        qb, cb, t0 = args
        tpos = t0 + jnp.arange(Q_BLOCK)
        logits = jnp.einsum('bqhd,bshd->bhqs', qb, k).astype(jnp.float32) * scale
        logits = logits + jnp.transpose(cb, (0, 2, 1))[..., None] - cum_k[:, :, None, :]
        causal = kpos[None, :] <= tpos[:, None]
        logits = jnp.where(causal[None, None], logits, -jnp.inf)
        p = jax.nn.softmax(logits, axis=-1).astype(v.dtype)
        o = jnp.einsum('bhqs,bshd->bqhd', p, v)
        return o.reshape(bsz, Q_BLOCK, B_WIDTH)

    out = lax.map(block, (to_blocks(q, nb), to_blocks(cum, nb),
                          jnp.arange(nb, dtype=jnp.int32) * Q_BLOCK))
    return jnp.moveaxis(out, 0, 1).reshape(bsz, L, B_WIDTH)

def hybrid_mixer(h, w_in, b_forget, g_out_a, g_out_b, w_out):
    bsz, L, _ = h.shape
    proj = h @ w_in
    (aq, ak, av, iq, ik, iw, bq, bk, bv, bf) = jnp.split(
        proj, list(np.cumsum(IN_SPLITS)[:-1]), axis=-1)
    oa = dsa_attention(aq.reshape(bsz, L, A_HEADS, A_HEAD_DIM),
                       ak.reshape(bsz, L, A_KV_HEADS, A_HEAD_DIM),
                       av.reshape(bsz, L, A_KV_HEADS, A_HEAD_DIM),
                       iq.reshape(bsz, L, IDX_HEADS, IDX_DIM), ik, iw)
    log_f = jax.nn.log_sigmoid(bf.astype(jnp.float32) + b_forget.astype(jnp.float32))
    ob = forgetting_attention(bq.reshape(bsz, L, B_HEADS, B_HEAD_DIM),
                              bk.reshape(bsz, L, B_HEADS, B_HEAD_DIM),
                              bv.reshape(bsz, L, B_HEADS, B_HEAD_DIM), log_f)
    o = jnp.concatenate([rms_norm(oa, g_out_a), rms_norm(ob, g_out_b)], axis=-1)
    return o @ w_out

def hierarchical_moe(h, w_group, b_group, w_router, b_router, w_gate, w_up, w_down):
    bsz, L, d = h.shape
    t = h.reshape(-1, d)
    g_logits = (t @ w_group).astype(jnp.float32) + b_group.astype(jnp.float32)
    g_prob = jax.nn.softmax(g_logits, axis=-1)
    g_sel = jnp.argmax(g_logits, axis=-1)
    p_group = jnp.take_along_axis(g_prob, g_sel[:, None], axis=1)[:, 0]
    e_all = jnp.einsum('nd,gde->nge', t, w_router).astype(jnp.float32) + b_router.astype(jnp.float32)
    e_logits = jnp.take_along_axis(e_all, g_sel[:, None, None], axis=1)[:, 0]
    top_v, top_i = lax.top_k(e_logits, TOPK_EXPERT)
    w_top = jax.nn.softmax(top_v, axis=-1) * p_group[:, None]
    eid = g_sel[:, None] * EXPERTS_PER_GROUP + top_i
    comb = jnp.sum(jax.nn.one_hot(eid, N_EXPERTS, dtype=jnp.float32) * w_top[..., None], axis=1)
    hg = jnp.einsum('nd,edf->nef', t, w_gate)
    hu = jnp.einsum('nd,edf->nef', t, w_up)
    a = jax.nn.silu(hg) * hu * comb[:, :, None].astype(h.dtype)
    y = jnp.einsum('nef,efd->nd', a, w_down)
    return y.reshape(bsz, L, d)

def first_inputs(seed: int = 0) -> dict:
    key = jax.random.key(seed)
    ks = jax.random.split(key, 20)
    f32 = jnp.float32
    nrm = lambda k, shape, s: jax.random.normal(k, shape, f32) * s
    return {
        'x': nrm(ks[0], (BATCH, SEQ, D_MODEL), 1.0),
        'c': nrm(ks[1], (BATCH, D_MODEL), 1.0),
        'w_ada': nrm(ks[2], (DEPTH, D_MODEL, N_MOD * D_MODEL), 0.5 * D_MODEL ** -0.5),
        'b_ada': nrm(ks[3], (DEPTH, N_MOD * D_MODEL), 0.01),
        'g_mix': 1.0 + nrm(ks[4], (DEPTH, D_MODEL), 0.01),
        'w_in': nrm(ks[5], (DEPTH, D_MODEL, IN_COLS), D_MODEL ** -0.5),
        'b_forget': jax.random.uniform(ks[6], (DEPTH, B_HEADS), f32, 1.0, 4.0),
        'g_out_a': 1.0 + nrm(ks[7], (DEPTH, A_WIDTH), 0.01),
        'g_out_b': 1.0 + nrm(ks[8], (DEPTH, B_WIDTH), 0.01),
        'w_out': nrm(ks[9], (DEPTH, MIX_WIDTH, D_MODEL), MIX_WIDTH ** -0.5),
        'g_ffn': 1.0 + nrm(ks[10], (DEPTH, D_MODEL), 0.01),
        'w_group': nrm(ks[11], (DEPTH, D_MODEL, N_GROUPS), D_MODEL ** -0.5),
        'b_group': nrm(ks[12], (DEPTH, N_GROUPS), 0.01),
        'w_router': nrm(ks[13], (DEPTH, N_GROUPS, D_MODEL, EXPERTS_PER_GROUP), D_MODEL ** -0.5),
        'b_router': nrm(ks[14], (DEPTH, N_GROUPS, EXPERTS_PER_GROUP), 0.01),
        'w_gate': nrm(ks[15], (DEPTH, N_EXPERTS, D_MODEL, D_FF_EXPERT), D_MODEL ** -0.5),
        'w_up': nrm(ks[16], (DEPTH, N_EXPERTS, D_MODEL, D_FF_EXPERT), D_MODEL ** -0.5),
        'w_down': nrm(ks[17], (DEPTH, N_EXPERTS, D_FF_EXPERT, D_MODEL), D_FF_EXPERT ** -0.5),
        'g_final': 1.0 + nrm(ks[18], (D_MODEL,), 0.01),
    }

def first_block(x, c, w_ada, b_ada, g_mix, w_in, b_forget, g_out_a, g_out_b, w_out,
              g_ffn, w_group, b_group, w_router, b_router, w_gate, w_up, w_down, g_final):
    for l in range(DEPTH):
        mod = (jax.nn.silu(c) @ w_ada[l] + b_ada[l])[:, None, :]
        shift_m, scale_m, gate_m, shift_f, scale_f, gate_f = jnp.split(mod, N_MOD, axis=-1)
        h = rms_norm(x, g_mix[l]) * (1.0 + scale_m) + shift_m
        x = x + gate_m * hybrid_mixer(h, w_in[l], b_forget[l], g_out_a[l], g_out_b[l], w_out[l])
        h = rms_norm(x, g_ffn[l]) * (1.0 + scale_f) + shift_f
        x = x + gate_f * hierarchical_moe(h, w_group[l], b_group[l], w_router[l], b_router[l],
                                          w_gate[l], w_up[l], w_down[l])
    return rms_norm(x, g_final)


GRID_W = 64
CTX_LEN = 256
N_ADA = 6
DIFF_HEADS = 8
DIFF_DH = 64
Q_W = 2 * DIFF_HEADS * DIFF_DH
K_W = 2 * DIFF_HEADS * DIFF_DH
V_W = DIFF_HEADS * 2 * DIFF_DH
ATTN_OUT = V_W
Q_BLK = 128
ROPE_BASE = 10000.0
SGU_CHUNK = 128
SGU_GROUPS = 8
SGU_W = 1024
SGU_GROUP_W = SGU_W // SGU_GROUPS
Z_W = 2 * SGU_W
GATE_W = 2 * D_MODEL
IN_W = Q_W + K_W + V_W + Z_W + GATE_W
PEER_HEADS = 8
PEER_N_KEYS = 128
PEER_N_EXPERTS = PEER_N_KEYS * PEER_N_KEYS
PEER_TOPK = 16
PEER_PK_DIM = 128
PEER_Q_DIM = 2 * PEER_PK_DIM
PEER_BLK = 128
RMS_EPS = 1e-6


def rmsnorm(x, g=None, eps=RMS_EPS):
    xf = x.astype(jnp.float32)
    y = xf * lax.rsqrt(jnp.mean(xf * xf, axis=-1, keepdims=True) + eps)
    if g is not None:
        y = y * g.astype(jnp.float32)
    return y.astype(x.dtype)

def layernorm(x, g, b, eps=1e-5):
    xf = x.astype(jnp.float32)
    mu = jnp.mean(xf, axis=-1, keepdims=True)
    xc = xf - mu
    y = xc * lax.rsqrt(jnp.mean(xc * xc, axis=-1, keepdims=True) + eps)
    return (y * g.astype(jnp.float32) + b.astype(jnp.float32)).astype(x.dtype)

def modulate(h, shift, scale):
    return h * (1.0 + scale) + shift

def _rotate(xp, pos):
    nfreq = xp.shape[-1] // 2
    inv = ROPE_BASE ** (-jnp.arange(nfreq, dtype=jnp.float32) / nfreq)
    ang = pos.astype(jnp.float32)[:, None] * inv[None, :]
    cos = jnp.cos(ang)[None, :, None, :]
    sin = jnp.sin(ang)[None, :, None, :]
    x1 = xp[..., :nfreq].astype(jnp.float32)
    x2 = xp[..., nfreq:].astype(jnp.float32)
    return jnp.concatenate([x1 * cos - x2 * sin, x1 * sin + x2 * cos], axis=-1)

def axial_rope(x, rows, cols):
    half = x.shape[-1] // 2
    return jnp.concatenate([_rotate(x[..., :half], rows), _rotate(x[..., half:], cols)], axis=-1).astype(x.dtype)

def diff_attention(q, k, v, lam):
    B, L = q.shape[0], q.shape[1]
    Lk = k.shape[1]
    nb = L // Q_BLK
    qb = q.reshape(B, nb, Q_BLK, 2 * DIFF_HEADS, DIFF_DH).transpose(1, 0, 2, 3, 4)

    def one(qblk):
        s = jnp.einsum('bqhd,bkhd->bhqk', qblk, k).astype(jnp.float32) * (DIFF_DH ** -0.5)
        a = jax.nn.softmax(s, axis=-1).reshape(B, DIFF_HEADS, 2, Q_BLK, Lk)
        a = a[:, :, 0] - lam * a[:, :, 1]
        return jnp.einsum('bhqk,bkhe->bqhe', a.astype(v.dtype), v)

    o = lax.map(one, qb)
    return o.transpose(1, 0, 2, 3, 4).reshape(B, L, DIFF_HEADS, 2 * DIFF_DH)

def spatial_gating(z, ln_g, ln_b, w_s, b_s):
    u, v = jnp.split(z, 2, axis=-1)
    v = layernorm(v, ln_g, ln_b)
    B, L = v.shape[0], v.shape[1]
    vb = v.reshape(B, L // SGU_CHUNK, SGU_CHUNK, SGU_GROUPS, SGU_GROUP_W)
    mixed = jnp.einsum('gpq,bnqgc->bnpgc', w_s, vb) + jnp.transpose(b_s)[None, None, :, :, None]
    return u * mixed.reshape(B, L, SGU_W)

def split_proj(p):
    B, L = p.shape[0], p.shape[1]
    q, k, v, z, gl = jnp.split(p, [Q_W, Q_W + K_W, Q_W + K_W + V_W, Q_W + K_W + V_W + Z_W], axis=-1)
    q = q.reshape(B, L, 2 * DIFF_HEADS, DIFF_DH)
    k = k.reshape(B, L, 2 * DIFF_HEADS, DIFF_DH)
    v = v.reshape(B, L, DIFF_HEADS, 2 * DIFF_DH)
    return q, k, v, z, gl

def mix_branches(q, k_all, v_all, z, gate_logits, lam, lam_init, subln_g,
                 sgu_ln_g, sgu_ln_b, sgu_w, sgu_b, w_branch_attn, w_branch_sgu, w_out):
    B, L = q.shape[0], q.shape[1]
    o = diff_attention(q, k_all, v_all, lam)
    o = rmsnorm(o, subln_g) * (1.0 - lam_init)
    y_attn = o.reshape(B, L, ATTN_OUT) @ w_branch_attn
    y_sgu = spatial_gating(jax.nn.gelu(z, approximate=False), sgu_ln_g, sgu_ln_b, sgu_w, sgu_b) @ w_branch_sgu
    g_attn, g_sgu = jnp.split(jax.nn.sigmoid(gate_logits), 2, axis=-1)
    return (g_attn * y_attn + g_sgu * y_sgu) @ w_out

def peer(h, w_query, sub_keys, u_tab, v_tab):
    B, L, D = h.shape
    T = B * L
    xt = h.reshape(T, D)
    q = rmsnorm((xt @ w_query).reshape(T, PEER_HEADS, 2, PEER_PK_DIM))
    s = jnp.einsum('thpd,pnd->thpn', q, sub_keys).astype(jnp.float32)
    s1, i1 = lax.top_k(s[:, :, 0], PEER_TOPK)
    s2, i2 = lax.top_k(s[:, :, 1], PEER_TOPK)
    n_cand = PEER_TOPK * PEER_TOPK
    cand = (s1[..., :, None] + s2[..., None, :]).reshape(T, PEER_HEADS, n_cand)
    cidx = (i1[..., :, None] * PEER_N_KEYS + i2[..., None, :]).reshape(T, PEER_HEADS, n_cand)
    best, pos = lax.top_k(cand, PEER_TOPK)
    eidx = jnp.take_along_axis(cidx, pos, axis=-1)
    gate = jax.nn.softmax(best, axis=-1)
    nb = T // PEER_BLK

    def one(args):
        xb, ib, gb = args
        act = jax.nn.gelu(jnp.einsum('td,thkd->thk', xb, u_tab[ib]), approximate=False) * gb.astype(xb.dtype)
        return jnp.einsum('thk,thkd->td', act, v_tab[ib])

    out = lax.map(one, (xt.reshape(nb, PEER_BLK, D),
                        eidx.reshape(nb, PEER_BLK, PEER_HEADS, PEER_TOPK),
                        gate.reshape(nb, PEER_BLK, PEER_HEADS, PEER_TOPK)))
    return out.reshape(B, L, D)

def second_inputs(seed: int = 0) -> dict:
    key = jax.random.key(seed)
    ks = jax.random.split(key, 28)
    D = D_MODEL

    def nrm(k, shape, scale):
        return jax.random.normal(k, shape, jnp.float32) * scale

    return {
        'x': nrm(ks[0], (BATCH, SEQ, D), 1.0),
        'c': nrm(ks[1], (BATCH, D), 1.0),
        'ctx': nrm(ks[2], (BATCH, CTX_LEN, D), 1.0),
        'c_ctx': nrm(ks[3], (D,), 1.0),
        'w_ada': nrm(ks[4], (DEPTH, D, N_ADA * D), 0.2 * D ** -0.5),
        'b_ada': nrm(ks[5], (DEPTH, N_ADA * D), 0.02),
        'g_pre_mix': 1.0 + nrm(ks[6], (DEPTH, D), 0.02),
        'g_post_mix': 1.0 + nrm(ks[7], (DEPTH, D), 0.02),
        'g_pre_ffn': 1.0 + nrm(ks[8], (DEPTH, D), 0.02),
        'g_post_ffn': 1.0 + nrm(ks[9], (DEPTH, D), 0.02),
        'w_in': nrm(ks[10], (DEPTH, D, IN_W), D ** -0.5),
        'b_gate': nrm(ks[11], (DEPTH, GATE_W), 0.02),
        'lambda_q1': nrm(ks[12], (DEPTH, DIFF_DH), 0.1),
        'lambda_k1': nrm(ks[13], (DEPTH, DIFF_DH), 0.1),
        'lambda_q2': nrm(ks[14], (DEPTH, DIFF_DH), 0.1),
        'lambda_k2': nrm(ks[15], (DEPTH, DIFF_DH), 0.1),
        'subln_g': 1.0 + nrm(ks[16], (DEPTH, 2 * DIFF_DH), 0.02),
        'sgu_ln_g': 1.0 + nrm(ks[17], (DEPTH, SGU_W), 0.02),
        'sgu_ln_b': nrm(ks[18], (DEPTH, SGU_W), 0.02),
        'sgu_w': nrm(ks[19], (DEPTH, SGU_GROUPS, SGU_CHUNK, SGU_CHUNK), SGU_CHUNK ** -0.5),
        'sgu_b': 1.0 + nrm(ks[20], (DEPTH, SGU_GROUPS, SGU_CHUNK), 0.02),
        'w_branch_attn': nrm(ks[21], (DEPTH, ATTN_OUT, D), ATTN_OUT ** -0.5),
        'w_branch_sgu': nrm(ks[22], (DEPTH, SGU_W, D), SGU_W ** -0.5),
        'w_out': nrm(ks[23], (DEPTH, D, D), D ** -0.5),
        'peer_w_query': nrm(ks[24], (DEPTH, D, PEER_HEADS * PEER_Q_DIM), D ** -0.5),
        'peer_sub_keys': nrm(ks[25], (DEPTH, 2, PEER_N_KEYS, PEER_PK_DIM), PEER_PK_DIM ** -0.5),
        'peer_u': nrm(ks[26], (DEPTH, PEER_N_EXPERTS, D), D ** -0.5),
        'peer_v': nrm(ks[27], (DEPTH, PEER_N_EXPERTS, D), D ** -0.5),
    }

def second_block(x, c, ctx, c_ctx, w_ada, b_ada, g_pre_mix, g_post_mix, g_pre_ffn, g_post_ffn,
              w_in, b_gate, lambda_q1, lambda_k1, lambda_q2, lambda_k2, subln_g,
              sgu_ln_g, sgu_ln_b, sgu_w, sgu_b, w_branch_attn, w_branch_sgu, w_out,
              peer_w_query, peer_sub_keys, peer_u, peer_v):
    B, L, _ = x.shape
    Lc = ctx.shape[1]
    n_rows = L // GRID_W
    rows = jnp.repeat(jnp.arange(n_rows, dtype=jnp.int32), GRID_W)
    cols = jnp.tile(jnp.arange(GRID_W, dtype=jnp.int32), n_rows)

    for l in range(DEPTH):
        last = l == DEPTH - 1
        lam_init = 0.8 - 0.6 * math.exp(-0.3 * l)
        lam = (jnp.exp(jnp.dot(lambda_q1[l].astype(jnp.float32), lambda_k1[l].astype(jnp.float32)))
               - jnp.exp(jnp.dot(lambda_q2[l].astype(jnp.float32), lambda_k2[l].astype(jnp.float32)))
               + lam_init)
        mod = jax.nn.silu(c) @ w_ada[l] + b_ada[l]
        sh1, sc1, gt1, sh2, sc2, gt2 = [m[:, None, :] for m in jnp.split(mod, N_ADA, axis=-1)]
        mod_c = jax.nn.silu(c_ctx) @ w_ada[l] + b_ada[l]
        sh1c, sc1c, gt1c, sh2c, sc2c, gt2c = jnp.split(mod_c, N_ADA, axis=-1)

        h = modulate(rmsnorm(x, g_pre_mix[l]), sh1, sc1)
        hc = modulate(rmsnorm(ctx, g_pre_mix[l]), sh1c, sc1c)
        q, k, v, z, gl = split_proj(h @ w_in[l])
        q = axial_rope(q, rows, cols)
        k = axial_rope(k, rows, cols)
        if last:
            kv_c = hc @ w_in[l][:, Q_W:Q_W + K_W + V_W]
            kc = kv_c[..., :K_W].reshape(B, Lc, 2 * DIFF_HEADS, DIFF_DH)
            vc = kv_c[..., K_W:].reshape(B, Lc, DIFF_HEADS, 2 * DIFF_DH)
        else:
            qc, kc, vc, zc, glc = split_proj(hc @ w_in[l])
        k_all = jnp.concatenate([kc, k], axis=1)
        v_all = jnp.concatenate([vc, v], axis=1)
        y = mix_branches(q, k_all, v_all, z, gl + b_gate[l], lam, lam_init, subln_g[l],
                         sgu_ln_g[l], sgu_ln_b[l], sgu_w[l], sgu_b[l],
                         w_branch_attn[l], w_branch_sgu[l], w_out[l])
        x_new = x + gt1 * rmsnorm(y, g_post_mix[l])

        if not last:
            yc = mix_branches(qc, kc, vc, zc, glc + b_gate[l], lam, lam_init, subln_g[l],
                              sgu_ln_g[l], sgu_ln_b[l], sgu_w[l], sgu_b[l],
                              w_branch_attn[l], w_branch_sgu[l], w_out[l])
            ctx_new = ctx + gt1c * rmsnorm(yc, g_post_mix[l])
            h2c = modulate(rmsnorm(ctx_new, g_pre_ffn[l]), sh2c, sc2c)
            ctx = ctx_new + gt2c * rmsnorm(peer(h2c, peer_w_query[l], peer_sub_keys[l], peer_u[l], peer_v[l]), g_post_ffn[l])

        h2 = modulate(rmsnorm(x_new, g_pre_ffn[l]), sh2, sc2)
        x = x_new + gt2 * rmsnorm(peer(h2, peer_w_query[l], peer_sub_keys[l], peer_u[l], peer_v[l]), g_post_ffn[l])
    return x


def setup_inputs(seed=0):
    out = dict(first_inputs(seed))
    for name, value in second_inputs(seed + 1).items():
        if name != "x":
            out[name + "_2"] = value
    return out


def reference(
    x, c, w_ada, b_ada, g_mix, w_in, b_forget, g_out_a, g_out_b, w_out, g_ffn, w_group, b_group,
    w_router, b_router, w_gate, w_up, w_down, g_final, c_2, ctx_2, c_ctx_2, w_ada_2, b_ada_2,
    g_pre_mix_2, g_post_mix_2, g_pre_ffn_2, g_post_ffn_2, w_in_2, b_gate_2, lambda_q1_2,
    lambda_k1_2, lambda_q2_2, lambda_k2_2, subln_g_2, sgu_ln_g_2, sgu_ln_b_2, sgu_w_2, sgu_b_2,
    w_branch_attn_2, w_branch_sgu_2, w_out_2, peer_w_query_2, peer_sub_keys_2, peer_u_2,
    peer_v_2,
):
    x = first_block(
        x, c, w_ada, b_ada, g_mix, w_in, b_forget, g_out_a, g_out_b, w_out, g_ffn, w_group,
        b_group, w_router, b_router, w_gate, w_up, w_down, g_final,
    )
    return second_block(
        x, c_2, ctx_2, c_ctx_2, w_ada_2, b_ada_2, g_pre_mix_2, g_post_mix_2, g_pre_ffn_2,
        g_post_ffn_2, w_in_2, b_gate_2, lambda_q1_2, lambda_k1_2, lambda_q2_2, lambda_k2_2,
        subln_g_2, sgu_ln_g_2, sgu_ln_b_2, sgu_w_2, sgu_b_2, w_branch_attn_2, w_branch_sgu_2,
        w_out_2, peer_w_query_2, peer_sub_keys_2, peer_u_2, peer_v_2,
    )


_drawn_inputs = setup_inputs


def setup_inputs(seed=0):
    import zlib

    import numpy as np

    out = dict(_drawn_inputs(seed))
    spreads = {}
    factors = {'g_out_a': 6.637,
     'g_out_b': 6.79,
     'g_ffn': 6.056,
     'b_group': 8.0,
     'b_router': 6.998,
     'g_final': 3.298,
     'g_pre_mix_2': 6.171,
     'g_post_mix_2': 8.0,
     'g_pre_ffn_2': 2.774,
     'g_post_ffn_2': 64.0,
     'b_gate_2': 8.0,
     'lambda_q1_2': 4.559,
     'lambda_k1_2': 3.015,
     'lambda_q2_2': 8.0,
     'lambda_k2_2': 8.0,
     'subln_g_2': 50.168,
     'sgu_ln_g_2': 21.702,
     'sgu_ln_b_2': 21.769,
     'sgu_b_2': 21.757}
    for name, (base, spread) in spreads.items():
        noise = np.random.default_rng([zlib.crc32(name.encode()), seed]).standard_normal(out[name].shape)
        drawn = base * np.exp(spread * noise) if base else spread * noise
        out[name] = __import__('jax').numpy.asarray(drawn.astype(out[name].dtype))
    for name, factor in factors.items():
        out[name] = (out[name] * factor).astype(out[name].dtype)
    return out
```

```python
from contextlib import ExitStack

import numpy as np

import concourse.bass as bass
import concourse.mybir as mybir

F32 = mybir.dt.float32
U32 = mybir.dt.uint32
ACT = mybir.ActivationFunctionType
ALU = mybir.AluOpType
AX = mybir.AxisListType

P = 128
SEQ, D = 512, 1024
CTX = 256
KC = D // P
TT = SEQ // P
BANK = 512
SLOTS, TILE = 4, 2048
EPS, LN_EPS = 1e-6, 1e-5

HEADS, DH = 8, 64
TOPK = min(256, SEQ // 4)
GROUPS, PER_GROUP = 4, 8
EXPERTS, FF = GROUPS * PER_GROUP, D // 4
DIFF_HEADS = 8
KEYS = CTX + SEQ
KT = KEYS // P
LAMBDA_INIT = 0.2
SGU_GROUPS = 8
PEER_HEADS, PEER_KEYS, PEER_TOPK = 8, 128, 16
PAIRS = PEER_HEADS * PEER_TOPK
HALF = PEER_KEYS // 2

MASKED, FILL, TAKEN = -1e30, -1e38, -3e38
TAKEN_BELOW = -2e38

AQ, IQ, BQ, BK, AK, IK = 0, 4, 8, 12, 16, 17
FM_CHUNKS = 18
SMALL = 144
G_MIX, G_OUT, G_FFN, G_FINAL, G_PRE_MIX, G_POST_MIX, G_PRE_FFN, G_POST_FFN = range(0, 64, 8)
B_GATE, SUBLN, LAMBDA, N_VECS = 64, 80, 81, 85
N_MOD = 6 * KC
ADA_C, ADA_B1, ADA_B2, N_ADA = 0, 24, 24 + N_MOD, 24 + 2 * N_MOD
SHIFT_1, SCALE_1, GATE_1, SHIFT_2, SCALE_2, GATE_2 = range(0, N_MOD, KC)

STAGES = [("ada1", 24), ("ada2", 24), ("in1", 11), ("out1", 4), ("moe", 3 * EXPERTS), ("qk2", 8), ("v2", 4),
          ("z2", 8), ("gate2", 8), ("branch2", 8), ("out2", 4), ("query", 8), ("peer", PEER_KEYS)]
FIRST = {}
N_TILES = 0
for _name, _n in STAGES:
    FIRST[_name] = N_TILES
    N_TILES += _n
COUNT = dict(STAGES)


class Core:
    pass


class Steps:

    def __init__(self, eng, sem):
        self.eng, self.sem, self.n = eng, sem, 0

    def __call__(self, ins):
        ins.then_inc(self.sem, 1)
        self.n += 1
        self.eng.wait_ge(self.sem, self.n)


def wait_tile(k, pe, n):
    pe.wait_ge(k.tile_loaded[n % SLOTS], 16 * (n // SLOTS + 1))


def slot(k, n):
    return k.ring[:, n % SLOTS, :]


def stream(k, sp, first, count, used, value):
    for n in range(first, min(first + count, N_TILES - SLOTS)):
        sp.wait_ge(used, value(n - first))
        sp.dma_start(slot(k, n + SLOTS), k.weights[n + SLOTS]).then_inc(k.tile_loaded[n % SLOTS], 16)


def load_stage(k):
    nc = k.nc
    with nc.Block(no_gpsimd_drain=True) as block:
        @block.sync
        def _(sp):
            for n in range(SLOTS):
                sp.dma_start(slot(k, n), k.weights[n]).then_inc(k.tile_loaded[n], 16)

        @block.scalar
        def _(act):
            act.dma_start(k.ada_vecs[:], k.d["ada_vecs"]).then_inc(k.loaded, 16)
            act.dma_start(k.vecs[:], k.d["vecs"]).then_inc(k.loaded, 16)
            act.dma_start(k.x[:], k.d["x"]).then_inc(k.loaded, 16)
            act.dma_start(k.ident[:], k.d["ident"]).then_inc(k.loaded, 16)
            act.wait_ge(k.loaded, 64)

        @block.vector
        def _(dve):
            nc.vector.memset(k.ones[:], 1.0).then_inc(k.vstep.sem, 1)
            nc.vector.memset(k.eps[:, 0:1], EPS).then_inc(k.vstep.sem, 1)
            nc.vector.memset(k.eps[:, 1:2], LN_EPS).then_inc(k.vstep.sem, 1)
            k.vstep.n += 3


def ada_stage(k):
    nc = k.nc
    tile_used, cond_ready = k.sem("ada_tile_used"), k.sem("cond_ready")
    n1 = COUNT["ada1"]
    with nc.Block(no_gpsimd_drain=True) as block:
        @block.sync
        def _(sp):
            with sp.Fori(0, 2 * n1 // SLOTS) as g:
                for s in range(SLOTS):
                    n = g * SLOTS + s
                    sp.wait_ge(tile_used, n + 1)
                    sp.dma_start(slot(k, s), k.weights[bass.ds(n + SLOTS, 1)].rearrange("a p n -> p (a n)")).then_inc(
                        k.tile_loaded[s], 16)

        @block.scalar
        def _(act):
            nc.scalar.activation(k.cond[:].rearrange("p c v -> p v c"), k.ada_vecs[:, ADA_C:ADA_C + 24].rearrange(
                "p (v c) -> p v c", v=3), ACT.Silu).then_inc(cond_ready, 1)

        @block.tensor
        def _(pe):
            pe.wait_ge(cond_ready, 1)
            for vectors, out, groups in ((slice(0, 1), k.psum[:, 0, 0:N_MOD].unsqueeze(2), range(0, 1)),
                                         (slice(1, 3), k.psum[:, 1, 0:2 * N_MOD].rearrange("p (m v) -> p m v", v=2),
                                          range(1, 2))):
                base = groups[0] * n1
                with pe.Fori(0, n1 // SLOTS) as g:
                    for s in range(SLOTS):
                        pe.wait_ge(k.tile_loaded[s], 16 * g + 16 * (base // SLOTS + 1))
                        for c in range(2):
                            chunk = g * (2 * SLOTS) + (2 * s + c)
                            for kc in range(KC):
                                mm = nc.tensor.matmul(
                                    out[:, bass.ds(chunk, 1), :].rearrange("p m v -> p (m v)"),
                                    slot(k, s)[:, (c * KC + kc) * P:(c * KC + kc + 1) * P],
                                    k.cond[:, kc, vectors], start=kc == 0, stop=kc == KC - 1)
                        mm.then_inc(tile_used, 1)

        @block.vector
        def _(dve):
            dve.wait_ge(tile_used, 2 * n1)
            step = k.vstep
            step(nc.vector.tensor_tensor(k.mod1[:], k.psum[:, 0, 0:N_MOD], k.ada_vecs[:, ADA_B1:ADA_B1 + N_MOD], ALU.add))
            step(nc.vector.tensor_tensor(
                k.mod2[:], k.psum[:, 1, 0:2 * N_MOD].rearrange("p (m v) -> p v m", v=2),
                k.ada_vecs[:, ADA_B2:ADA_B2 + N_MOD].unsqueeze(1).broadcast_to([P, 2, N_MOD]), ALU.add))

            def fold(part, gain, one):
                step(nc.vector.scalar_tensor_tensor(part, part, one, k.vecs[:, gain:gain + KC], ALU.add, ALU.mult))

            fold(k.mod1[:, SCALE_1:SCALE_1 + KC], G_MIX, 1.0)
            fold(k.mod1[:, SCALE_2:SCALE_2 + KC], G_FFN, 1.0)
            fold(k.mod2[:, 0, SCALE_1:SCALE_1 + KC], G_PRE_MIX, 1.0)
            fold(k.mod2[:, 1, SCALE_1:SCALE_1 + KC], G_PRE_MIX, 1.0)
            fold(k.mod2[:, 0, SCALE_2:SCALE_2 + KC], G_PRE_FFN, 1.0)
            fold(k.mod2[:, 0, GATE_1:GATE_1 + KC], G_POST_MIX, 0.0)
            fold(k.mod2[:, 0, GATE_2:GATE_2 + KC], G_POST_FFN, 0.0)


def norm_stage(k, name, source, target, width, gain, shift=None, add_to=None):
    nc = k.nc
    squared, summed, std_ready, scaled = (k.sem(f"{name}_{s}") for s in ("squared", "summed", "std_ready", "scaled"))
    with ExitStack() as scope:
        square = scope.enter_context(nc.sbuf_tensor(f"{name}_square", [P, 2, width], F32))
        std = scope.enter_context(nc.sbuf_tensor(f"{name}_std", [P, width], F32))
        rstd = scope.enter_context(nc.sbuf_tensor(f"{name}_rstd", [P, width], F32))
        with nc.Block(no_gpsimd_drain=True) as block:
            @block.scalar
            def _(act):
                for c in range(KC):
                    if c >= 2:
                        act.wait_ge(summed, c - 1)
                    nc.scalar.activation(square[:, c % 2], source[:, c], ACT.Square).then_inc(squared, 1)
                act.wait_ge(summed, KC)
                nc.scalar.activation(std[:], k.psum[:, 0, 0:width], ACT.Sqrt, bias=k.eps[:, 0:1], scale=1.0 / D).then_inc(
                    std_ready, 1)
                if shift is not None:
                    for c in range(KC):
                        act.wait_ge(scaled, c + 1)
                        nc.scalar.activation(target[:, c], target[:, c], ACT.Identity, bias=shift[:, c:c + 1])

            @block.tensor
            def _(pe):
                for c in range(KC):
                    pe.wait_ge(squared, c + 1)
                    nc.tensor.matmul(k.psum[:, 0, 0:width], k.ones[:], square[:, c % 2], start=c == 0,
                                     stop=c == KC - 1).then_inc(summed, 1)

            @block.vector
            def _(dve):
                dve.wait_ge(std_ready, 1)
                k.vstep(nc.vector.reciprocal(rstd[:], std[:]))
                for c in range(KC):
                    nc.vector.scalar_tensor_tensor(target[:, c], source[:, c], gain[:, c:c + 1], rstd[:], ALU.mult,
                                                   ALU.mult).then_inc(scaled, 1)
                if add_to is not None:
                    dve.wait_ge(scaled, KC)
                    for c in range(KC):
                        nc.vector.tensor_tensor(add_to[:, c], add_to[:, c], target[:, c], ALU.add)


def chunk_products(k, pe, out, tiles, c, source, done):
    n = tiles + c // 2
    if c % 2 == 0:
        wait_tile(k, pe, n)
    for kc in range(KC):
        at = ((c % 2) * KC + kc) * P
        mm = k.nc.tensor.matmul(out, slot(k, n)[:, at:at + P], source[:, kc], start=kc == 0, stop=kc == KC - 1)
    mm.then_inc(done, 1)


def row_products(k, pe, out, tiles, token_tile, done):
    for kc in range(KC):
        mm = k.nc.tensor.matmul(out, token_tile(kc), slot(k, tiles + kc // 4)[:, (kc % 4) * BANK:(kc % 4 + 1) * BANK],
                                start=kc == 0, stop=kc == KC - 1)
    mm.then_inc(done, 1)


def in_projection_stage(k):
    nc = k.nc
    done, copied, rows_done, rows_copied, loaded = (
        k.sem(s) for s in ("in1_done", "in1_copied", "in1_rows_done", "in1_rows_copied", "in1_loaded"))
    first = FIRST["in1"]
    n_fm = FM_CHUNKS // 2
    with ExitStack() as scope:
        w_small = scope.enter_context(nc.sbuf_tensor("w_small", [P, KC, SMALL], F32))
        with nc.Block(no_gpsimd_drain=True) as block:
            @block.sync
            def _(sp):
                sp.dma_start(w_small[:], k.d["w_small"]).then_inc(loaded, 16)
                stream(k, sp, first, n_fm, done, lambda n: 2 * (n + 1))
                stream(k, sp, first + n_fm, 2, rows_done, lambda n: TT)

            @block.tensor
            def _(pe):
                for c in range(FM_CHUNKS):
                    if c >= 4:
                        pe.wait_ge(copied, c - 3)
                    chunk_products(k, pe, k.psum[:, c % 4], first, c, k.h, done)
                wait_tile(k, pe, first + n_fm)
                wait_tile(k, pe, first + n_fm + 1)
                for t in range(TT):
                    if t >= 2:
                        pe.wait_ge(rows_copied, t - 1)
                    row_products(k, pe, k.psum[:, 4 + t % 2], first + n_fm, lambda kc: k.h[:, kc, t * P:(t + 1) * P], rows_done)
                pe.wait_ge(loaded, 16)
                for t in range(TT):
                    for kc in range(KC):
                        mm = nc.tensor.matmul(k.psum[:, 6 + t // 2, (t % 2) * SMALL:(t % 2 + 1) * SMALL],
                                              k.h[:, kc, t * P:(t + 1) * P], w_small[:, kc], start=kc == 0, stop=kc == KC - 1)
                mm.then_inc(rows_done, 1)

            @block.scalar
            def _(act):
                for c in range(FM_CHUNKS):
                    act.wait_ge(done, c + 1)
                    query = c < IQ or BQ <= c < BK
                    nc.scalar.activation(k.proj[:, c], k.psum[:, c % 4], ACT.Copy, scale=DH ** -0.5 if query else 1.0).then_inc(
                        copied, 1)

            @block.vector
            def _(dve):
                for t in range(TT):
                    dve.wait_ge(rows_done, t + 1)
                    nc.vector.tensor_copy(k.v_b[:, t], k.psum[:, 4 + t % 2]).then_inc(rows_copied, 1)
                dve.wait_ge(rows_done, TT + 1)
                for i in range(2):
                    nc.vector.tensor_copy(k.small[:, 2 * i:2 * i + 2], k.psum[:, 6 + i, 0:2 * SMALL].rearrange(
                        "p (t n) -> p t n", t=2)).then_inc(rows_copied, 1)


def forget_stage(k):
    nc = k.nc
    loaded, at_vector, at_scalar, summed = (k.sem(f"forget_{s}") for s in ("loaded", "vector", "scalar", "summed"))
    with ExitStack() as scope:
        tri = scope.enter_context(nc.sbuf_tensor("tri", [P, TT, SEQ], F32))
        b_row = scope.enter_context(nc.sbuf_tensor("b_forget_row", [P, HEADS], F32))
        z, mag, e, log_f = (scope.enter_context(nc.sbuf_tensor(f"forget_{n}", [P, TT, HEADS], F32)) for n in
                            ("z", "mag", "e", "log_f"))
        with nc.Block(no_gpsimd_drain=True) as block:
            @block.sync
            def _(sp):
                sp.dma_start(b_row[:], k.d["b_forget"][0].partition_broadcast(P)).then_inc(loaded, 16)
                sp.dma_start(tri[:], k.d["tri"]).then_inc(loaded, 16)
                sp.dma_start(k.causal[:], k.d["causal"]).then_inc(loaded, 16)
                sp.dma_start(k.head_rows[:], k.d["head_rows"]).then_inc(loaded, 16)
                sp.dma_start(k.slope_pos[:], k.d["slope_pos"]).then_inc(loaded, 16)
                sp.wait_ge(loaded, 80)

            @block.vector
            def _(dve):
                step = k.vstep
                dve.wait_ge(loaded, 80)
                step(nc.vector.tensor_tensor(z[:], k.small[:, :, 136:144], b_row[:].unsqueeze(1).broadcast_to([P, TT, HEADS]),
                                             ALU.add))
                nc.vector.scalar_tensor_tensor(mag[:], z[:], -1.0, z[:], ALU.mult, ALU.max).then_inc(at_vector, 1)
                dve.wait_ge(at_scalar, 2)
                nc.vector.scalar_tensor_tensor(log_f[:], z[:], 0.0, e[:], ALU.min, ALU.subtract).then_inc(at_vector, 1)

            @block.scalar
            def _(act):
                act.wait_ge(at_vector, 1)
                nc.scalar.activation(e[:], mag[:], ACT.Exp, scale=-1.0).then_inc(at_scalar, 1)
                act.wait_ge(at_scalar, 1)
                nc.scalar.activation(e[:], e[:], ACT.Ln, bias=1.0).then_inc(at_scalar, 1)
                act.wait_ge(summed, 1)
                nc.scalar.activation(k.neg_cum[:], k.psum[0:HEADS, 0], ACT.Copy, scale=-1.0)

            @block.tensor
            def _(pe):
                pe.wait_ge(loaded, 80)
                pe.wait_ge(at_vector, 2)
                for t in range(TT):
                    mm = nc.tensor.matmul(k.psum[0:HEADS, 0], log_f[:, t], tri[:, t], start=t == 0, stop=t == TT - 1)
                mm.then_inc(summed, 1)


def head_half(chunk_view, half):
    return chunk_view[half * DH:(half + 1) * DH]


def index_stage(k):
    nc = k.nc
    done, relued, added = (k.sem(f"index_{s}") for s in ("done", "relued", "added"))
    units = [(i, h) for i in range(1, TT) for h in range(HEADS)]
    with ExitStack() as scope:
        score = scope.enter_context(nc.sbuf_tensor("index_score", [P, TT, SEQ], F32))
        relu = scope.enter_context(nc.sbuf_tensor("index_relu", [P, 2, SEQ], F32))
        top = scope.enter_context(nc.sbuf_tensor("index_top", [P, TT, 8], F32))
        with nc.Block(no_gpsimd_drain=True) as block:
            @block.tensor
            def _(pe):
                for u, (i, h) in enumerate(units):
                    if u >= 2:
                        pe.wait_ge(relued, u - 1)
                    nc.tensor.matmul(k.psum[:, u % 2, 0:P * (i + 1)],
                                     head_half(k.proj[:, IQ + h // 2, i * P:(i + 1) * P], h % 2),
                                     head_half(k.proj[:, IK, 0:P * (i + 1)], h % 2), start=True, stop=True).then_inc(done, 1)

            @block.scalar
            def _(act):
                for u, (i, h) in enumerate(units):
                    act.wait_ge(done, u + 1)
                    if u >= 2:
                        act.wait_ge(added, u - 1)
                    nc.scalar.activation(relu[:, u % 2, 0:P * (i + 1)], k.psum[:, u % 2, 0:P * (i + 1)], ACT.Relu).then_inc(
                        relued, 1)

            @block.vector
            def _(dve):
                step = k.vstep
                for u, (i, h) in enumerate(units):
                    w = P * (i + 1)
                    weight = k.small[:, i, 128 + h:129 + h]
                    dve.wait_ge(relued, u + 1)
                    if h == 0:
                        nc.vector.tensor_scalar(score[:, i, 0:w], relu[:, u % 2, 0:w], weight, None, ALU.mult).then_inc(added, 1)
                    else:
                        dve.wait_ge(added, u)
                        nc.vector.scalar_tensor_tensor(score[:, i, 0:w], relu[:, u % 2, 0:w], weight, score[:, i, 0:w],
                                                       ALU.mult, ALU.add).then_inc(added, 1)
                dve.wait_ge(added, len(units))
                for i in range(1, TT):
                    part = score[:, i, P * i:P * (i + 1)]
                    step(nc.vector.scalar_tensor_tensor(part, k.causal[:, SEQ - P:SEQ], FILL / MASKED, part, ALU.mult, ALU.add))
                for _round in range(TOPK // 8):
                    for i in range(1, TT):
                        step(nc.vector.max(top[:, i], score[:, i, 0:P * (i + 1)]))
                    for i in range(1, TT):
                        step(nc.vector.match_replace(score[:, i, 0:P * (i + 1)], top[:, i], score[:, i, 0:P * (i + 1)], TAKEN))
                nc.vector.tensor_copy(k.chosen[:, 0, 0:P], k.causal[:, SEQ - P:SEQ])
                for i in range(1, TT):
                    w = P * (i + 1)
                    nc.vector.tensor_scalar(k.chosen[:, i, 0:w], score[:, i, 0:w], TAKEN_BELOW, MASKED, ALU.is_gt, ALU.mult)


def attention_stage(k):
    nc = k.nc
    scored, masked, exped, turned, turned_copied, weighed, out_copied = (
        k.sem(f"attn_{s}") for s in ("scored", "masked", "exped", "turned", "turned_copied", "weighed", "out_copied"))
    units = [(a, i, h) for i in range(TT) for a in range(2) for h in range(HEADS)]
    n = len(units)
    with ExitStack() as scope:
        def sb(name, shape):
            return scope.enter_context(nc.sbuf_tensor(name, shape, F32))

        logits, probs, probs_t = sb("attn_logits", [P, 2, SEQ]), sb("attn_probs", [P, 2, SEQ]), sb("attn_probs_t", [P, 2, SEQ])
        neg_max, total, inv = sb("attn_neg_max", [P, n]), sb("attn_total", [P, n]), sb("attn_inv", [P, n])
        with nc.Block(no_gpsimd_drain=True) as block:
            @block.tensor
            def _(pe):
                def score(u):
                    a, i, h = units[u]
                    w = P * (i + 1)
                    if u >= 2:
                        pe.wait_ge(masked, u - 1)
                    if a == 0:
                        q, key, half, rows = AQ + h % 4, AK, h // 4, k.slope_pos[:, SEQ - w:SEQ]
                    else:
                        q, key, half, rows = BQ + h // 2, BK + h // 2, h % 2, k.neg_cum[:, 0:w]
                    out = k.psum[:, u % 2, 0:w]
                    nc.tensor.matmul(out, head_half(k.proj[:, q, i * P:(i + 1) * P], half), head_half(k.proj[:, key, 0:w], half),
                                     start=True, stop=False)
                    nc.tensor.matmul(out, k.head_rows[:, h], rows, start=False, stop=True).then_inc(scored, 1)

                def turn(u):
                    i = units[u][1]
                    pe.wait_ge(exped, u + 1)
                    if u >= 2:
                        pe.wait_ge(turned_copied, u - 1)
                    for s in range(i + 1):
                        mm = nc.tensor.transpose(k.psum[:, 2 + u % 2, s * P:(s + 1) * P], probs[:, u % 2, s * P:(s + 1) * P],
                                                 k.ident[:])
                    mm.then_inc(turned, 1)

                def weigh(u):
                    a, i, h = units[u]
                    pe.wait_ge(turned_copied, u + 1)
                    if u >= 2:
                        pe.wait_ge(out_copied, u - 1)
                    for s in range(i + 1):
                        v = k.small[:, s, (h // 4) * DH:(h // 4 + 1) * DH] if a == 0 else k.v_b[:, s, h * DH:(h + 1) * DH]
                        mm = nc.tensor.matmul(k.psum[:, 4 + u % 2, 0:DH], probs_t[:, u % 2, s * P:(s + 1) * P], v,
                                              start=s == 0, stop=s == i)
                    mm.then_inc(weighed, 1)

                for t in range(n + 2):
                    if t < n:
                        score(t)
                    if 1 <= t <= n:
                        turn(t - 1)
                    if t >= 2:
                        weigh(t - 2)

            @block.vector
            def _(dve):
                def mask(u):
                    a, i, _h = units[u]
                    w = P * (i + 1)
                    dve.wait_ge(scored, u + 1)
                    if u >= 2:
                        dve.wait_ge(exped, u - 1)
                    mask_rows = k.chosen[:, i, 0:w] if a == 0 else k.causal[:, SEQ - w:SEQ]
                    k.vstep(nc.vector.tensor_tensor(logits[:, u % 2, 0:w], k.psum[:, u % 2, 0:w], mask_rows, ALU.add))
                    nc.vector.tensor_reduce(neg_max[:, u:u + 1], logits[:, u % 2, 0:w], AX.X, ALU.max, negate=True).then_inc(
                        masked, 1)

                def normalise(u):
                    a, i, h = units[u]
                    dve.wait_ge(exped, u + 1)
                    k.vstep(nc.vector.reciprocal(inv[:, u:u + 1], total[:, u:u + 1]))
                    dve.wait_ge(weighed, u + 1)
                    at = a * HEADS * DH + h * DH
                    nc.vector.tensor_scalar(k.o[:, i, at:at + DH], k.psum[:, 4 + u % 2, 0:DH], inv[:, u:u + 1], None,
                                            ALU.mult).then_inc(out_copied, 1)

                for t in range(n + 2):
                    if t < n:
                        mask(t)
                    if t >= 2:
                        normalise(t - 2)

            @block.scalar
            def _(act):
                def exp(u):
                    w = P * (units[u][1] + 1)
                    act.wait_ge(masked, u + 1)
                    if u >= 2:
                        act.wait_ge(turned, u - 1)
                    nc.scalar.activation(probs[:, u % 2, 0:w], logits[:, u % 2, 0:w], ACT.Exp, bias=neg_max[:, u:u + 1],
                                         accum_out=total[:, u:u + 1]).then_inc(exped, 1)

                def copy_turned(u):
                    w = P * (units[u][1] + 1)
                    act.wait_ge(turned, u + 1)
                    if u >= 2:
                        act.wait_ge(weighed, u - 1)
                    nc.scalar.activation(probs_t[:, u % 2, 0:w], k.psum[:, 2 + u % 2, 0:w], ACT.Copy).then_inc(turned_copied, 1)

                for t in range(n + 1):
                    if t < n:
                        exp(t)
                    if t >= 1:
                        copy_turned(t - 1)


def head_norm_stage(k, name, groups, gain, gain_scale=1.0):
    nc = k.nc
    std_ready, scaled, turned, copied, rooted = (k.sem(f"{name}_{s}") for s in ("std", "scaled", "turned", "copied", "rooted"))
    width = D // groups
    with ExitStack() as scope:
        square = scope.enter_context(nc.sbuf_tensor(f"{name}_square", [P, D], F32))
        total = scope.enter_context(nc.sbuf_tensor(f"{name}_total", [P, TT, groups], F32))
        rstd = scope.enter_context(nc.sbuf_tensor(f"{name}_rstd", [P, TT, groups], F32))
        gains = scope.enter_context(nc.sbuf_tensor(f"{name}_gains", [P, KC], F32))
        with nc.Block(no_gpsimd_drain=True) as block:
            @block.vector
            def _(dve):
                step = k.vstep
                step(nc.vector.tensor_scalar(gains[:], gain, gain_scale, None, ALU.mult))
                for t in range(TT):
                    step(nc.vector.tensor_tensor(square[:], k.o[:, t], k.o[:, t], ALU.mult))
                    step(nc.vector.tensor_reduce(total[:, t], square[:].rearrange("p (g n) -> p g n", g=groups), AX.X, ALU.add))
                nc.vector.tensor_scalar(total[:], total[:], 1.0 / width, EPS, ALU.mult, ALU.add).then_inc(std_ready, 1)
                dve.wait_ge(rooted, 1)
                step(nc.vector.reciprocal(rstd[:], total[:]))
                for t in range(TT):
                    rows = k.o[:, t].rearrange("p (g n) -> p g n", g=groups)
                    nc.vector.tensor_tensor(rows, rows, rstd[:, t].unsqueeze(2).broadcast_to([P, groups, width]),
                                            ALU.mult).then_inc(scaled, 1)

            @block.tensor
            def _(pe):
                pe.wait_ge(scaled, TT)
                for c in range(KC):
                    if c >= 4:
                        pe.wait_ge(copied, c - 3)
                    for t in range(TT):
                        mm = nc.tensor.transpose(k.psum[:, c % 4, t * P:(t + 1) * P], k.o[:, t, c * P:(c + 1) * P], k.ident[:])
                    mm.then_inc(turned, 1)

            @block.scalar
            def _(act):
                act.wait_ge(std_ready, 1)
                nc.scalar.activation(total[:], total[:], ACT.Sqrt).then_inc(rooted, 1)
                for c in range(KC):
                    act.wait_ge(turned, c + 1)
                    nc.scalar.activation(k.h[:, c], k.psum[:, c % 4], ACT.Copy, scale=gains[:, c:c + 1]).then_inc(copied, 1)


def out_projection_stage(k):
    nc = k.nc
    done, added = k.sem("out1_done"), k.sem("out1_added")
    first = FIRST["out1"]
    with nc.Block(no_gpsimd_drain=True) as block:
        @block.sync
        def _(sp):
            stream(k, sp, first, COUNT["out1"], done, lambda n: 2 * (n + 1))

        @block.tensor
        def _(pe):
            for c in range(KC):
                if c >= 4:
                    pe.wait_ge(added, c - 3)
                chunk_products(k, pe, k.psum[:, c % 4], first, c, k.h, done)

        @block.vector
        def _(dve):
            for c in range(KC):
                dve.wait_ge(done, c + 1)
                nc.vector.scalar_tensor_tensor(k.x[:, c], k.psum[:, c % 4], k.mod1[:, GATE_1 + c:GATE_1 + c + 1], k.x[:, c],
                                               ALU.mult, ALU.add).then_inc(added, 1)


def first_of_largest(k, sb, name, values, n, prio):
    nc, step = k.nc, k.vstep
    shape = [P, TT, n]
    top, less, mark, best, hot = (sb(f"{name}_{s}", [P, TT] if s in ("top", "best") else shape) for s in
                                  ("top", "less", "mark", "best", "hot"))
    step(nc.vector.tensor_reduce(top[:], values, AX.X, ALU.max))
    step(nc.vector.tensor_tensor(less[:], values, top[:].unsqueeze(2).broadcast_to(shape), ALU.subtract))
    step(nc.vector.tensor_scalar(mark[:], less[:], 0.0, None, ALU.is_equal))
    step(nc.vector.tensor_tensor(mark[:], mark[:], prio[:, 0:n].unsqueeze(1).broadcast_to(shape), ALU.mult))
    step(nc.vector.tensor_reduce(best[:], mark[:], AX.X, ALU.max))
    step(nc.vector.tensor_tensor(hot[:], mark[:], best[:].unsqueeze(2).broadcast_to(shape), ALU.is_equal))
    return top, less, hot


def router_stage(k):
    nc = k.nc
    loaded, routed, at_vector, at_scalar, turned, stored = (
        k.sem(f"route_{s}") for s in ("loaded", "routed", "vector", "scalar", "turned", "stored"))
    n = GROUPS + EXPERTS
    with ExitStack() as scope:
        def sb(name, shape):
            return scope.enter_context(nc.sbuf_tensor(name, shape, F32))

        w_route, b_route, prio = sb("w_route", [P, KC, n]), sb("b_route", [P, n]), sb("prio", [P, PER_GROUP])
        logits, picked = sb("route_logits", [P, TT, n]), sb("route_picked", [P, TT, GROUPS, PER_GROUP])
        expert, second = sb("route_expert", [P, TT, PER_GROUP]), sb("route_second", [P, TT, PER_GROUP])
        exp_group, group_sum, p_group = sb("exp_group", [P, TT, GROUPS]), sb("group_sum", [P, TT]), sb("p_group", [P, TT])
        delta, w_first, w_second = sb("route_delta", [P, TT]), sb("w_first", [P, TT]), sb("w_second", [P, TT])
        comb8, comb = sb("comb8", [P, TT, PER_GROUP]), sb("comb", [P, TT, GROUPS, PER_GROUP])
        comb_t = sb("comb_t", [EXPERTS, SEQ])
        with nc.Block(no_gpsimd_drain=True) as block:
            @block.sync
            def _(sp):
                sp.dma_start(w_route[:], k.d["w_route"]).then_inc(loaded, 16)
                sp.dma_start(b_route[:], k.d["b_route"][0].partition_broadcast(P)).then_inc(loaded, 16)
                sp.dma_start(prio[:], k.d["prio"]).then_inc(loaded, 16)
                sp.wait_ge(at_scalar, 3)
                sp.dma_start(k.comb_dram, comb_t[:]).then_inc(stored, 16)
                sp.wait_ge(stored, 16)

            @block.tensor
            def _(pe):
                pe.wait_ge(loaded, 48)
                for t in range(TT):
                    for kc in range(KC):
                        mm = nc.tensor.matmul(k.psum[:, 0, t * n:(t + 1) * n], k.h[:, kc, t * P:(t + 1) * P], w_route[:, kc],
                                              start=kc == 0, stop=kc == KC - 1)
                mm.then_inc(routed, 1)
                pe.wait_ge(at_vector, 3)
                for t in range(TT):
                    mm = nc.tensor.transpose(k.psum[0:EXPERTS, 1, t * P:(t + 1) * P],
                                             comb[:, t].rearrange("p g e -> p (g e)"), k.ident[:])
                mm.then_inc(turned, 1)

            @block.scalar
            def _(act):
                act.wait_ge(at_vector, 1)
                nc.scalar.activation(exp_group[:], k.route_less[:], ACT.Exp).then_inc(at_scalar, 1)
                act.wait_ge(at_vector, 2)
                nc.scalar.activation(w_second[:], delta[:], ACT.Exp).then_inc(at_scalar, 1)
                act.wait_ge(turned, 1)
                nc.scalar.activation(comb_t[:], k.psum[0:EXPERTS, 1], ACT.Copy).then_inc(at_scalar, 1)

            @block.vector
            def _(dve):
                step = k.vstep
                dve.wait_ge(loaded, 48)
                dve.wait_ge(routed, 1)
                step(nc.vector.tensor_tensor(logits[:], k.psum[:, 0, 0:TT * n].rearrange("p (t n) -> p t n", n=n),
                                             b_route[:].unsqueeze(1).broadcast_to([P, TT, n]), ALU.add))
                _top, less, group = first_of_largest(k, sb, "group", logits[:, :, 0:GROUPS], GROUPS, prio)
                nc.vector.tensor_copy(k.route_less[:], less[:]).then_inc(at_vector, 1)
                for g in range(GROUPS):
                    step(nc.vector.tensor_tensor(picked[:, :, g], logits[:, :, GROUPS + g * PER_GROUP:GROUPS + (g + 1) * PER_GROUP],
                                                 group[:, :, g:g + 1].broadcast_to([P, TT, PER_GROUP]), ALU.mult))
                step(nc.vector.tensor_reduce(expert[:], picked[:].rearrange("p t g e -> p t e g"), AX.X, ALU.add))
                top1, _less1, hot1 = first_of_largest(k, sb, "best1", expert[:], PER_GROUP, prio)
                step(nc.vector.scalar_tensor_tensor(second[:], hot1[:], MASKED, expert[:], ALU.mult, ALU.add))
                top2, _less2, hot2 = first_of_largest(k, sb, "best2", second[:], PER_GROUP, prio)
                nc.vector.tensor_tensor(delta[:], top2[:], top1[:], ALU.subtract).then_inc(at_vector, 1)
                dve.wait_ge(at_scalar, 2)
                step(nc.vector.tensor_reduce(group_sum[:], exp_group[:], AX.X, ALU.add))
                step(nc.vector.reciprocal(p_group[:], group_sum[:]))
                step(nc.vector.tensor_scalar(w_first[:], w_second[:], 1.0, None, ALU.add))
                step(nc.vector.reciprocal(w_first[:], w_first[:]))
                step(nc.vector.tensor_tensor(w_first[:], w_first[:], p_group[:], ALU.mult))
                step(nc.vector.tensor_tensor(w_second[:], w_second[:], w_first[:], ALU.mult))
                for hot, w in ((hot1, w_first), (hot2, w_second)):
                    step(nc.vector.tensor_tensor(hot[:], hot[:], w[:].unsqueeze(2).broadcast_to([P, TT, PER_GROUP]), ALU.mult))
                step(nc.vector.tensor_tensor(comb8[:], hot1[:], hot2[:], ALU.add))
                for g in range(GROUPS):
                    ins = nc.vector.tensor_tensor(comb[:, :, g], comb8[:], group[:, :, g:g + 1].broadcast_to([P, TT, PER_GROUP]),
                                                  ALU.mult)
                ins.then_inc(at_vector, 1)


def moe_stage(k):
    nc = k.nc
    in_done, silu_done, up_done, act_ready, down_done, added = (
        k.sem(f"moe_{s}") for s in ("in_done", "silu_done", "up_done", "act_ready", "down_done", "added"))
    weight_loaded = [k.sem(f"moe_weight_loaded{i}") for i in range(2)]
    first = FIRST["moe"]
    LOOP = 4
    turns = (EXPERTS - 1) // LOOP
    loops = (EXPERTS - 2) // LOOP
    with ExitStack() as scope:
        def sb(name, shape):
            return scope.enter_context(nc.sbuf_tensor(name, shape, F32))

        weight, silu = sb("moe_weight", [P, 2, SEQ]), sb("moe_silu", [P, 2, SEQ])
        hidden, acts = sb("moe_hidden", [P, 2, SEQ]), sb("moe_acts", [P, 2, 2, SEQ])
        with nc.Block(no_gpsimd_drain=True) as block:
            @block.sync
            def _(sp):
                def refill(n, used, value, r):
                    s = (first + r) % SLOTS
                    sp.wait_ge(used, value)
                    sp.dma_start(k.ring[:, s, :], k.weights[bass.ds(n + (first + SLOTS), 1)].rearrange("a p n -> p (a n)")).then_inc(
                        k.tile_loaded[s], 16)

                def expert_tiles(e, r):
                    refill(3 * e + 2, in_done, 4 * e + 6, 3 * r + 2)
                    refill(3 * e + 3, in_done, 4 * e + 8, 3 * r + 3)
                    refill(3 * e + 4, down_done, 8 * e + 8, 3 * r + 4)

                refill(0, in_done, 2, 0)
                refill(1, in_done, 4, 1)
                with sp.Fori(0, turns) as g:
                    for j in range(LOOP):
                        expert_tiles(g * LOOP + j, j)
                for e in range(turns * LOOP, EXPERTS - 1):
                    expert_tiles(e, e)
                refill(3 * EXPERTS - 1, down_done, 8 * EXPERTS, 3 * EXPERTS - 1)

            @block.gpsimd
            def _(pool):
                def load(e, j):
                    pool.dma_start(weight[:, j % 2], k.comb_dram[bass.ds(e, 1)].partition_broadcast(P)).then_inc(
                        weight_loaded[j % 2], 16)

                load(0, 0)
                load(1, 1)
                with pool.Fori(0, EXPERTS // 2 - 1) as g:
                    for j in range(2):
                        pool.wait_ge(act_ready, 4 * g + 2 * j + 2)
                        load(2 * g + (j + 2), j)

            @block.tensor
            def _(pe):
                def gate_up(c, s, bank):
                    for kc in range(KC):
                        at = (c * KC + kc) * P
                        mm = nc.tensor.matmul(k.psum[:, bank], k.ring[:, s, at:at + P], k.h[:, kc], start=kc == 0, stop=kc == KC - 1)
                    mm.then_inc(in_done, 1)

                def down(e, s, parity, wait):
                    for m in range(KC):
                        if wait or m >= 4:
                            pe.wait_ge(added, 8 * e + (m - 3))
                        for kc in range(2):
                            at = kc * D + m * P
                            mm = nc.tensor.matmul(k.psum[:, 4 + m % 4], k.ring[:, s, at:at + P], acts[:, parity, kc],
                                                  start=kc == 0, stop=kc == 1)
                        mm.then_inc(down_done, 1)

                def turn(n):
                    return 16 * ((first + n) // SLOTS + 1)

                def body(e, r, shift):
                    pe.wait_ge(act_ready, 2 * e + 2)
                    for i in range(2):
                        n = 3 * r + 2 + i
                        pe.wait_ge(k.tile_loaded[(first + n) % SLOTS], shift + turn(n))
                        for c in range(2):
                            gate_up(c, (first + n) % SLOTS, 2 * i + c)
                    n = 3 * r + 4
                    pe.wait_ge(k.tile_loaded[(first + n) % SLOTS], shift + turn(n))
                    down(e, (first + n) % SLOTS, r % 2, r > 0)

                for i in range(2):
                    wait_tile(k, pe, first + i)
                    for c in range(2):
                        gate_up(c, (first + i) % SLOTS, 2 * i + c)
                body(0, 0, 0)
                with pe.Fori(0, loops) as g:
                    for j in range(1, LOOP + 1):
                        body(g * LOOP + j, j, g * (16 * 3 * LOOP // SLOTS))
                for e in range(loops * LOOP + 1, EXPERTS - 1):
                    body(e, e, 0)
                n = 3 * EXPERTS - 1
                wait_tile(k, pe, first + n)
                pe.wait_ge(act_ready, 2 * EXPERTS)
                down(EXPERTS - 1, (first + n) % SLOTS, (EXPERTS - 1) % 2, True)

            @block.scalar
            def _(act):
                def body(e, wait):
                    for c in range(2):
                        act.wait_ge(in_done, 4 * e + (c + 1))
                        if wait:
                            act.wait_ge(up_done, 2 * e + (c - 1))
                        nc.scalar.activation(silu[:, c], k.psum[:, c], ACT.Silu).then_inc(silu_done, 1)

                body(0, False)
                with act.Fori(1, EXPERTS) as e:
                    body(e, True)

            @block.vector
            def _(dve):
                def gate(e, parity, turn):
                    dve.wait_ge(weight_loaded[parity], turn)
                    for c in range(2):
                        dve.wait_ge(silu_done, 2 * e + (c + 1))
                        dve.wait_ge(in_done, 4 * e + (c + 3))
                        nc.vector.tensor_tensor(hidden[:, c], silu[:, c], k.psum[:, 2 + c], ALU.mult).then_inc(up_done, 1)
                    for c in range(2):
                        dve.wait_ge(up_done, 2 * e + (c + 1))
                        nc.vector.tensor_tensor(acts[:, parity, c], hidden[:, c], weight[:, parity], ALU.mult).then_inc(act_ready, 1)

                def add(e):
                    for m in range(KC):
                        dve.wait_ge(down_done, 8 * e + (m + 1))
                        nc.vector.tensor_tensor(k.y[:, m], k.y[:, m], k.psum[:, 4 + m % 4], ALU.add).then_inc(added, 1)

                k.vstep(nc.vector.memset(k.y[:], 0.0))
                gate(0, 0, 16)
                gate(1, 1, 16)
                add(0)
                with dve.Fori(1, EXPERTS // 2) as g:
                    for j in range(2):
                        gate(2 * g + j, j, 16 * g + 16)
                        add(2 * g + (j - 1))
                add(EXPERTS - 1)


def add_gated_stage(k, y, gate):
    nc = k.nc
    with nc.Block(no_gpsimd_drain=True) as block:
        @block.vector
        def _(dve):
            for c in range(KC):
                nc.vector.scalar_tensor_tensor(k.x[:, c], y[:, c], gate[:, c:c + 1], k.x[:, c], ALU.mult, ALU.add)


def load_context_stage(k):
    nc = k.nc
    loaded = k.sem("context_loaded")
    with nc.Block(no_gpsimd_drain=True) as block:
        @block.sync
        def _(sp):
            sp.dma_start(k.h_ctx[:], k.d["ctx"]).then_inc(loaded, 16)
            sp.dma_start(k.rope[:], k.d["rope"]).then_inc(loaded, 16)
            sp.dma_start(k.swap[:], k.d["swap"]).then_inc(loaded, 16)
            sp.wait_ge(loaded, 48)


def qk_stage(k):
    nc = k.nc
    done, copied, swapped, rotated, ctx_done, ctx_copied = (
        k.sem(f"qk_{s}") for s in ("done", "copied", "swapped", "rotated", "ctx_done", "ctx_copied"))
    first = FIRST["qk2"]
    n = 2 * KC
    with ExitStack() as scope:
        raw = scope.enter_context(nc.sbuf_tensor("qk_raw", [P, 2, SEQ], F32))
        with_cos = scope.enter_context(nc.sbuf_tensor("qk_with_cos", [P, 2, SEQ], F32))
        with_sin = scope.enter_context(nc.sbuf_tensor("qk_with_sin", [P, 2, SEQ], F32))

        with nc.Block(no_gpsimd_drain=True) as block:
            @block.sync
            def _(sp):
                stream(k, sp, first, KC // 2, done, lambda i: 2 * (i + 1))
                stream(k, sp, first + KC // 2, KC // 2, ctx_done, lambda i: 2 * (i + 1))

            @block.tensor
            def _(pe):
                def swap(c):
                    pe.wait_ge(copied, c + 1)
                    if c >= 2:
                        pe.wait_ge(rotated, c - 1)
                    nc.tensor.matmul(k.psum[:, 2 + c % 2], k.swap[:], raw[:, c % 2], start=True, stop=True).then_inc(swapped, 1)

                for c in range(n):
                    if c >= 2:
                        pe.wait_ge(copied, c - 1)
                    chunk_products(k, pe, k.psum[:, c % 2], first, c, k.h, done)
                    if c >= KC:
                        i = c - KC
                        if i >= 2:
                            pe.wait_ge(ctx_copied, i - 1)
                        chunk_products_again(k, pe, k.psum[:, 4 + i % 2, 0:CTX], first, c, k.h_ctx, ctx_done)
                    if c >= 1:
                        swap(c - 1)
                swap(n - 1)

            @block.scalar
            def _(act):
                for c in range(n):
                    act.wait_ge(done, c + 1)
                    if c >= 2:
                        act.wait_ge(swapped, c - 1)
                        act.wait_ge(rotated, c - 1)
                    nc.scalar.activation(raw[:, c % 2], k.psum[:, c % 2], ACT.Copy, scale=DH ** -0.5 if c < KC else 1.0).then_inc(
                        copied, 1)
                    if c >= KC:
                        i = c - KC
                        act.wait_ge(ctx_done, i + 1)
                        nc.scalar.activation(k.k2[:, i, 0:CTX], k.psum[:, 4 + i % 2, 0:CTX], ACT.Copy).then_inc(ctx_copied, 1)

            @block.vector
            def _(dve):
                for c in range(n):
                    target = k.q2[:, c] if c < KC else k.k2[:, c - KC, CTX:KEYS]
                    dve.wait_ge(copied, c + 1)
                    nc.vector.tensor_tensor(with_cos[:, c % 2], raw[:, c % 2], k.rope[:, 0], ALU.mult)
                    dve.wait_ge(swapped, c + 1)
                    k.vstep(nc.vector.tensor_tensor(with_sin[:, c % 2], k.psum[:, 2 + c % 2], k.rope[:, 1], ALU.mult))
                    nc.vector.tensor_tensor(target, with_cos[:, c % 2], with_sin[:, c % 2], ALU.add).then_inc(rotated, 1)


def chunk_products_again(k, pe, out, tiles, c, source, done):
    n = tiles + c // 2
    for kc in range(KC):
        at = ((c % 2) * KC + kc) * P
        mm = k.nc.tensor.matmul(out, slot(k, n)[:, at:at + P], source[:, kc], start=kc == 0, stop=kc == KC - 1)
    mm.then_inc(done, 1)


def values_stage(k):
    nc = k.nc
    done, copied = k.sem("v2_done"), k.sem("v2_copied")
    first = FIRST["v2"]
    with nc.Block(no_gpsimd_drain=True) as block:
        @block.sync
        def _(sp):
            stream(k, sp, first, 4, done, lambda n: KT * (n // 2 + 1))

        @block.tensor
        def _(pe):
            for half in range(2):
                for i in range(2):
                    wait_tile(k, pe, first + 2 * half + i)
                for t in range(KT):
                    u = half * KT + t
                    if u >= 4:
                        pe.wait_ge(copied, u - 3)
                    c = CTX // P
                    row_products(k, pe, k.psum[:, u % 4], first + 2 * half,
                                 lambda kc: k.h_ctx[:, kc, t * P:(t + 1) * P] if t < c else k.h[:, kc, (t - c) * P:(t - c + 1) * P],
                                 done)

        @block.scalar
        def _(act):
            for u in range(2 * KT):
                act.wait_ge(done, u + 1)
                nc.scalar.activation(k.v2[:, u % KT, (u // KT) * BANK:(u // KT + 1) * BANK], k.psum[:, u % 4], ACT.Copy).then_inc(
                    copied, 1)


def sgu_projection_stage(k):
    nc = k.nc
    done, copied, rows_done = k.sem("z_done"), k.sem("z_copied"), k.sem("z_rows_done")
    first = FIRST["z2"]
    with nc.Block(no_gpsimd_drain=True) as block:
        @block.sync
        def _(sp):
            stream(k, sp, first, 4, done, lambda n: 2 * (n + 1))
            stream(k, sp, first + 4, 4, rows_done, lambda n: TT * (n // 2 + 1))

        @block.tensor
        def _(pe):
            for c in range(KC):
                if c >= 4:
                    pe.wait_ge(copied, c - 3)
                chunk_products(k, pe, k.psum[:, c % 4], first, c, k.h, done)
            for half in range(2):
                for i in range(2):
                    wait_tile(k, pe, first + 4 + 2 * half + i)
                for t in range(TT):
                    u = KC + half * TT + t
                    pe.wait_ge(copied, u - 3)
                    row_products(k, pe, k.psum[:, u % 4], first + 4 + 2 * half, lambda kc: k.h[:, kc, t * P:(t + 1) * P], rows_done)

        @block.scalar
        def _(act):
            for c in range(KC):
                act.wait_ge(done, c + 1)
                nc.scalar.activation(k.u[:, c], k.psum[:, c % 4], ACT.Gelu).then_inc(copied, 1)
            for u in range(2 * TT):
                act.wait_ge(rows_done, u + 1)
                nc.scalar.activation(k.vz[:, u % TT, (u // TT) * BANK:(u // TT + 1) * BANK], k.psum[:, (KC + u) % 4],
                                     ACT.Gelu).then_inc(copied, 1)


def sgu_stage(k):
    nc = k.nc
    loaded, normed, mixed, used, at_scalar = (k.sem(f"sgu_{s}") for s in ("loaded", "normed", "mixed", "used", "scalar"))
    with ExitStack() as scope:
        def sb(name, shape):
            return scope.enter_context(nc.sbuf_tensor(name, shape, F32))

        w_s, b_s = sb("sgu_w", [P, SGU_GROUPS, P]), sb("sgu_b", [P, SGU_GROUPS, P])
        ln = sb("sgu_ln", [P, 2, D])
        stats, moments = sb("sgu_stats", [P, TT, 2, 6]), sb("sgu_moments", [P, TT, 2])
        std, with_bias = sb("sgu_std", [P, TT]), sb("sgu_with_bias", [P, 2, SEQ])
        with nc.Block(no_gpsimd_drain=True) as block:
            @block.sync
            def _(sp):
                sp.dma_start(ln[:, 0], k.d["ln_g"][0].partition_broadcast(P)).then_inc(loaded, 16)
                sp.dma_start(ln[:, 1], k.d["ln_b"][0].partition_broadcast(P)).then_inc(loaded, 16)
                sp.dma_start(b_s[:].rearrange("p g n -> p (g n)"), k.d["sgu_b"][0].partition_broadcast(P)).then_inc(loaded, 16)
                sp.dma_start(w_s[:], k.d["sgu_w"]).then_inc(loaded, 16)

            @block.vector
            def _(dve):
                step = k.vstep
                for t in range(TT):
                    for i in range(2):
                        step(nc.vector.bn_stats(stats[:, t, i], k.vz[:, t, i * BANK:(i + 1) * BANK]))
                    step(nc.vector.bn_aggr(moments[:, t], stats[:, t].rearrange("p i n -> p (i n)")))
                nc.vector.tensor_copy(std[:], moments[:, :, 1]).then_inc(normed, 1)
                dve.wait_ge(at_scalar, 1)
                step(nc.vector.reciprocal(std[:], std[:]))
                dve.wait_ge(loaded, 64)
                for t in range(TT):
                    step(nc.vector.tensor_scalar(k.vz[:, t], k.vz[:, t], moments[:, t, 0:1], std[:, t:t + 1], ALU.subtract, ALU.mult))
                for t in range(TT):
                    step(nc.vector.tensor_tensor(k.vz[:, t], k.vz[:, t], ln[:, 0], ALU.mult))
                for t in range(TT):
                    nc.vector.tensor_tensor(k.vz[:, t], k.vz[:, t], ln[:, 1], ALU.add).then_inc(normed, 1)
                for g in range(SGU_GROUPS):
                    dve.wait_ge(mixed, g + 1)
                    part = with_bias[:, g % 2].rearrange("p (t n) -> p t n", t=TT)
                    k.vstep(nc.vector.tensor_tensor(part, k.psum[:, g % 4].rearrange("p (t n) -> p t n", t=TT),
                                                    b_s[:, g].unsqueeze(1).broadcast_to([P, TT, P]), ALU.add))
                    nc.vector.tensor_tensor(k.u[:, g], k.u[:, g], with_bias[:, g % 2], ALU.mult).then_inc(used, 1)

            @block.scalar
            def _(act):
                act.wait_ge(normed, 1)
                nc.scalar.activation(std[:], std[:], ACT.Sqrt, bias=k.eps[:, 1:2]).then_inc(at_scalar, 1)

            @block.tensor
            def _(pe):
                pe.wait_ge(loaded, 64)
                pe.wait_ge(normed, 1 + TT)
                for g in range(SGU_GROUPS):
                    if g >= 4:
                        pe.wait_ge(used, g - 3)
                    for t in range(TT):
                        mm = nc.tensor.matmul(k.psum[:, g % 4, t * P:(t + 1) * P], k.vz[:, t, g * P:(g + 1) * P], w_s[:, g],
                                              start=True, stop=True)
                    mm.then_inc(mixed, 1)


def diff_attention_stage(k):
    nc = k.nc
    scored, maxed, exped, mixed, turned, turned_copied, weighed, out_copied, lam_vector, lam_scalar, lam_dot = (
        k.sem(f"diff_{s}") for s in ("scored", "maxed", "exped", "mixed", "turned", "turned_copied", "weighed", "out_copied",
                                     "lam_vector", "lam_scalar", "lam_dot"))
    units = [(i, h) for i in range(TT) for h in range(DIFF_HEADS)]
    n = len(units)
    HALF_KEYS = KEYS // 2
    with ExitStack() as scope:
        def sb(name, shape):
            return scope.enter_context(nc.sbuf_tensor(name, shape, F32))

        probs, minus, probs_t = sb("diff_probs", [P, 2, 2, KEYS]), sb("diff_minus", [P, KEYS]), sb("diff_probs_t", [P, 2, KEYS])
        neg_max, total, inv = sb("diff_neg_max", [P, 2 * n]), sb("diff_total", [P, 2 * n]), sb("diff_inv", [P, 2 * n])
        lam_prod, lam_exp, neg_lam = sb("lam_prod", [P, 2]), sb("lam_exp", [P, 2]), sb("neg_lam", [P, 1])
        with nc.Block(no_gpsimd_drain=True) as block:
            @block.tensor
            def _(pe):
                def score(u, j):
                    i, h = units[u]
                    v = 2 * u + j
                    if v >= 2:
                        pe.wait_ge(exped, v - 1)
                    q = head_half(k.q2[:, h, i * P:(i + 1) * P], j)
                    nc.tensor.matmul(k.psum[:, 2 * j, :], q, head_half(k.k2[:, h, 0:BANK], j), start=True, stop=True)
                    nc.tensor.matmul(k.psum[:, 2 * j + 1, 0:KEYS - BANK], q, head_half(k.k2[:, h, BANK:KEYS], j), start=True,
                                     stop=True).then_inc(scored, 1)

                def turn(u):
                    pe.wait_ge(mixed, u + 1)
                    for half in range(2):
                        if u >= 1:
                            pe.wait_ge(turned_copied, 2 * u + half - 1)
                        for s in range(3):
                            at = half * HALF_KEYS + s * P
                            mm = nc.tensor.transpose(k.psum[:, 4 + half, s * P:(s + 1) * P], probs[:, u % 2, 0, at:at + P], k.ident[:])
                        mm.then_inc(turned, 1)

                def weigh(u):
                    h = units[u][1]
                    pe.wait_ge(turned_copied, 2 * u + 2)
                    if u >= 2:
                        pe.wait_ge(out_copied, u - 1)
                    for s in range(KT):
                        mm = nc.tensor.matmul(k.psum[:, 6 + u % 2, 0:P], probs_t[:, u % 2, s * P:(s + 1) * P],
                                              k.v2[:, s, h * P:(h + 1) * P], start=s == 0, stop=s == KT - 1)
                    mm.then_inc(weighed, 1)

                pe.wait_ge(lam_vector, 1)
                nc.tensor.matmul(k.psum[:, 7, 0:2], k.ones[:], lam_prod[:], start=True, stop=True).then_inc(lam_dot, 1)
                pe.wait_ge(lam_scalar, 1)
                for t in range(n + 2):
                    if t < n:
                        score(t, 0)
                        score(t, 1)
                    if 1 <= t <= n:
                        turn(t - 1)
                    if t >= 2:
                        weigh(t - 2)

            @block.vector
            def _(dve):
                step = k.vstep

                def maxima(u):
                    for j in range(2):
                        v = 2 * u + j
                        dve.wait_ge(scored, v + 1)
                        row = k.psum[:, 2 * j:2 * j + 2].rearrange("p b n -> p (b n)")[:, 0:KEYS]
                        nc.vector.tensor_reduce(neg_max[:, v:v + 1], row, AX.X, ALU.max, negate=True).then_inc(maxed, 1)

                def mix(u):
                    dve.wait_ge(exped, 2 * u + 2)
                    step(nc.vector.reciprocal(inv[:, 2 * u:2 * u + 2], total[:, 2 * u:2 * u + 2]))
                    step(nc.vector.tensor_tensor(inv[:, 2 * u + 1:2 * u + 2], inv[:, 2 * u + 1:2 * u + 2], neg_lam[:], ALU.mult))
                    step(nc.vector.tensor_scalar(minus[:], probs[:, u % 2, 1], inv[:, 2 * u + 1:2 * u + 2], None, ALU.mult))
                    nc.vector.scalar_tensor_tensor(probs[:, u % 2, 0], probs[:, u % 2, 0], inv[:, 2 * u:2 * u + 1], minus[:],
                                                   ALU.mult, ALU.add).then_inc(mixed, 1)

                def copy_out(u):
                    i, h = units[u]
                    dve.wait_ge(weighed, u + 1)
                    nc.vector.tensor_copy(k.o[:, i, h * P:(h + 1) * P], k.psum[:, 6 + u % 2, 0:P]).then_inc(out_copied, 1)

                step(nc.vector.memset(lam_prod[:], 0.0))
                nc.vector.tensor_tensor(lam_prod[0:DH], k.vecs[0:DH, LAMBDA:LAMBDA + 4:2], k.vecs[0:DH, LAMBDA + 1:LAMBDA + 4:2],
                                        ALU.mult).then_inc(lam_vector, 1)
                dve.wait_ge(lam_scalar, 1)
                step(nc.vector.tensor_tensor(neg_lam[:], lam_exp[:, 1:2], lam_exp[:, 0:1], ALU.subtract))
                step(nc.vector.tensor_scalar(neg_lam[:], neg_lam[:], LAMBDA_INIT, None, ALU.subtract))
                for t in range(n + 3):
                    if t < n:
                        maxima(t)
                    if 1 <= t <= n:
                        mix(t - 1)
                    if t >= 3:
                        copy_out(t - 3)

            @block.scalar
            def _(act):
                def exp(u):
                    for j in range(2):
                        v = 2 * u + j
                        act.wait_ge(maxed, v + 1)
                        if u >= 2:
                            act.wait_ge(turned, 2 * (u - 1))
                        row = k.psum[:, 2 * j:2 * j + 2].rearrange("p b n -> p (b n)")[:, 0:KEYS]
                        nc.scalar.activation(probs[:, u % 2, j], row, ACT.Exp, bias=neg_max[:, v:v + 1],
                                             accum_out=total[:, v:v + 1]).then_inc(exped, 1)

                def copy_turned(u):
                    for half in range(2):
                        act.wait_ge(turned, 2 * u + half + 1)
                        if u >= 2:
                            act.wait_ge(weighed, u - 1)
                        nc.scalar.activation(probs_t[:, u % 2, half * HALF_KEYS:(half + 1) * HALF_KEYS],
                                             k.psum[:, 4 + half, 0:HALF_KEYS], ACT.Copy).then_inc(turned_copied, 1)

                act.wait_ge(lam_dot, 1)
                nc.scalar.activation(lam_exp[:], k.psum[:, 7, 0:2], ACT.Exp).then_inc(lam_scalar, 1)
                for t in range(n + 1):
                    if t < n:
                        exp(t)
                    if t >= 1:
                        copy_turned(t - 1)


def gates_stage(k):
    nc = k.nc
    done, copied = k.sem("gate2_done"), k.sem("gate2_copied")
    first = FIRST["gate2"]
    with nc.Block(no_gpsimd_drain=True) as block:
        @block.sync
        def _(sp):
            stream(k, sp, first, 8, done, lambda n: 2 * (n + 1))

        @block.tensor
        def _(pe):
            for c in range(2 * KC):
                if c >= 4:
                    pe.wait_ge(copied, c - 3)
                chunk_products(k, pe, k.psum[:, c % 4], first, c, k.h, done)

        @block.scalar
        def _(act):
            for c in range(2 * KC):
                act.wait_ge(done, c + 1)
                nc.scalar.activation(k.gates[:, c], k.psum[:, c % 4], ACT.Sigmoid, bias=k.vecs[:, B_GATE + c:B_GATE + c + 1]).then_inc(
                    copied, 1)


def branches_stage(k):
    nc = k.nc
    done, gated, summed, out_done, out_copied = (k.sem(f"branch_{s}") for s in ("done", "gated", "summed", "out_done", "out_copied"))
    first, first_out = FIRST["branch2"], FIRST["out2"]
    with nc.Block(no_gpsimd_drain=True) as block:
        @block.sync
        def _(sp):
            stream(k, sp, first, 8, done, lambda n: 2 * (n + 1))
            stream(k, sp, first_out, 4, out_done, lambda n: 2 * (n + 1))

        @block.tensor
        def _(pe):
            for c in range(2 * KC):
                if c >= 4:
                    pe.wait_ge(gated, c - 3)
                chunk_products(k, pe, k.psum[:, c % 4], first, c, k.h if c < KC else k.u, done)
            pe.wait_ge(summed, KC)
            for c in range(KC):
                if c >= 4:
                    pe.wait_ge(out_copied, c - 3)
                chunk_products(k, pe, k.psum[:, 4 + c % 4], first_out, c, k.gates, out_done)

        @block.vector
        def _(dve):
            for c in range(2 * KC):
                dve.wait_ge(done, c + 1)
                nc.vector.tensor_tensor(k.gates[:, c], k.gates[:, c], k.psum[:, c % 4], ALU.mult).then_inc(gated, 1)
                if c >= KC:
                    dve.wait_ge(gated, c + 1)
                    nc.vector.tensor_tensor(k.gates[:, c - KC], k.gates[:, c - KC], k.gates[:, c], ALU.add).then_inc(summed, 1)

        @block.scalar
        def _(act):
            for c in range(KC):
                act.wait_ge(out_done, c + 1)
                nc.scalar.activation(k.y2[:, c], k.psum[:, 4 + c % 4], ACT.Copy).then_inc(out_copied, 1)


def query_stage(k):
    nc = k.nc
    done, copied, squared, stat_done, rooted, scored, scaled, loaded, at_vector = (
        k.sem(f"query_{s}") for s in ("done", "copied", "squared", "stat_done", "rooted", "scored", "scaled", "loaded", "vector"))
    first = FIRST["query"]
    n = 2 * PEER_HEADS
    with ExitStack() as scope:
        def sb(name, shape):
            return scope.enter_context(nc.sbuf_tensor(name, shape, F32))

        keys, raw, square = sb("peer_keys", [P, 2, PEER_KEYS]), sb("query_raw", [P, n, SEQ]), sb("query_square", [P, 2, SEQ])
        rstd = sb("query_rstd", [P, TT, n])
        with nc.Block(no_gpsimd_drain=True) as block:
            @block.sync
            def _(sp):
                sp.dma_start(keys[:], k.d["peer_keys"]).then_inc(loaded, 16)
                stream(k, sp, first, 8, done, lambda i: 2 * (i + 1))

            @block.tensor
            def _(pe):
                def stat(c):
                    pe.wait_ge(squared, c + 1)
                    for t in range(TT):
                        mm = nc.tensor.matmul(k.psum[:, 4, t * n + c:t * n + c + 1], square[:, c % 2, t * P:(t + 1) * P],
                                              k.ones[:, 0:1], start=True, stop=True)
                    mm.then_inc(stat_done, 1)

                for c in range(n):
                    if c >= 4:
                        pe.wait_ge(squared, c - 3)
                        pe.wait_ge(copied, c - 3)
                    chunk_products(k, pe, k.psum[:, c % 4], first, c, k.h, done)
                    if c >= 1:
                        stat(c - 1)
                stat(n - 1)
                pe.wait_ge(loaded, 16)
                pe.wait_ge(copied, n)
                for c in range(n):
                    if c >= 3:
                        pe.wait_ge(scaled, c - 2)
                    for t in range(TT):
                        mm = nc.tensor.matmul(k.psum[:, 5 + c % 3, t * P:(t + 1) * P], raw[:, c, t * P:(t + 1) * P], keys[:, c % 2],
                                              start=True, stop=True)
                    mm.then_inc(scored, 1)

            @block.scalar
            def _(act):
                for c in range(n):
                    act.wait_ge(done, c + 1)
                    if c >= 2:
                        act.wait_ge(stat_done, c - 1)
                    nc.scalar.activation(raw[:, c], k.psum[:, c % 4], ACT.Copy).then_inc(copied, 1)
                    nc.scalar.activation(square[:, c % 2], k.psum[:, c % 4], ACT.Square).then_inc(squared, 1)
                act.wait_ge(stat_done, n)
                nc.scalar.activation(rstd[:].rearrange("p t n -> p (t n)"), k.psum[:, 4, 0:TT * n], ACT.Sqrt, bias=k.eps[:, 0:1],
                                     scale=1.0 / P).then_inc(rooted, 1)

            @block.vector
            def _(dve):
                dve.wait_ge(rooted, 1)
                k.vstep(nc.vector.reciprocal(rstd[:], rstd[:]))
                for c in range(n):
                    dve.wait_ge(scored, c + 1)
                    nc.vector.tensor_tensor(k.scores[:, :, c], k.psum[:, 5 + c % 3].rearrange("p (t n) -> p t n", t=TT),
                                            rstd[:, :, c:c + 1].broadcast_to([P, TT, PEER_KEYS]), ALU.mult).then_inc(scaled, 1)


def peer_choice_stage(k):
    nc = k.nc
    loaded, ready, exped, turned, copied = (k.sem(f"choice_{s}") for s in ("loaded", "ready", "exped", "turned", "copied"))
    H, K = PEER_HEADS, PEER_TOPK
    with ExitStack() as scope:
        def sb(name, shape, dt=F32):
            return scope.enter_context(nc.sbuf_tensor(name, shape, dt))

        ramp = sb("choice_ramp", [P, K])
        top, index_u, index = sb("sub_top", [P, 2 * H, K]), sb("sub_index_u", [P, 2 * H, K], U32), sb("sub_index", [P, 2 * H, K])
        cand, best = sb("choice_cand", [P, H, K * K]), sb("choice_best", [P, H, K])
        place, place_a, place_b = (sb(f"choice_place{s}", [P, PAIRS], U32) for s in ("", "_a", "_b"))
        place_f = sb("choice_place_f", [P, PAIRS])
        hot = sb("choice_hot", [P, PAIRS, K])
        picked = sb("choice_picked", [P, 3, 2, PAIRS])
        expo, total = sb("choice_exp", [P, H, K]), sb("choice_total", [P, H])
        with nc.Block(no_gpsimd_drain=True) as block:
            @block.sync
            def _(sp):
                sp.dma_start(ramp[:], k.d["iota"][:, 0:K]).then_inc(loaded, 16)

            @block.vector
            def _(dve):
                step = k.vstep

                def best_of(rows, values, places):
                    for r in range(0, K, 8):
                        for j, row in enumerate(rows):
                            nc.vector.max(values(j)[:, r:r + 8], row).then_inc(step.sem, 1)
                            step.n += 1
                        dve.wait_ge(step.sem, step.n)
                        for j, row in enumerate(rows):
                            nc.vector.max_index(places(j)[:, r:r + 8], values(j)[:, r:r + 8], row).then_inc(step.sem, 1)
                            step.n += 1
                        dve.wait_ge(step.sem, step.n)
                        if r + 8 < K:
                            for j, row in enumerate(rows):
                                nc.vector.match_replace(row, values(j)[:, r:r + 8], row, TAKEN).then_inc(step.sem, 1)
                                step.n += 1
                            dve.wait_ge(step.sem, step.n)

                dve.wait_ge(loaded, 16)
                for t in range(TT):
                    best_of([k.scores[:, t, c] for c in range(2 * H)], lambda j: top[:, j], lambda j: index_u[:, j])
                    step(nc.vector.tensor_copy(index[:], index_u[:]))
                    halves = top[:].rearrange("p (h s) n -> p h s n", s=2)
                    for h in range(H):
                        step(nc.vector.tensor_tensor(cand[:, h].rearrange("p (a b) -> p a b", b=K),
                                                     halves[:, h, 0].unsqueeze(2).broadcast_to([P, K, K]),
                                                     halves[:, h, 1].unsqueeze(1).broadcast_to([P, K, K]), ALU.add))
                    places = place[:].rearrange("p (h n) -> p h n", h=H)
                    best_of([cand[:, h] for h in range(H)], lambda j: best[:, j], lambda j: places[:, j])
                    step(nc.vector.tensor_scalar(place_a[:], place[:], 4, None, ALU.logical_shift_right))
                    step(nc.vector.tensor_scalar(place_b[:], place[:], K - 1, None, ALU.bitwise_and))
                    if t >= 2:
                        dve.wait_ge(copied, t - 1)
                    for s, at in ((0, place_a), (1, place_b)):
                        step(nc.vector.tensor_copy(place_f[:], at[:]))
                        step(nc.vector.tensor_tensor(hot[:], place_f[:].unsqueeze(2).broadcast_to([P, PAIRS, K]),
                                                     ramp[:].unsqueeze(1).broadcast_to([P, PAIRS, K]), ALU.is_equal))
                        hot_h = hot[:].rearrange("p (h n) a -> p h n a", h=H)
                        lists = index[:].rearrange("p (h s) n -> p h s n", s=2)
                        for h in range(H):
                            step(nc.vector.tensor_tensor(hot_h[:, h], hot_h[:, h],
                                                         lists[:, h, s].unsqueeze(1).broadcast_to([P, K, K]), ALU.mult))
                        step(nc.vector.tensor_reduce(picked[:, s, t % 2], hot[:], AX.X, ALU.add))
                    if t >= 1:
                        dve.wait_ge(exped, t)
                    nc.vector.tensor_tensor(expo[:], best[:], best[:, :, 0:1].broadcast_to([P, H, K]), ALU.subtract).then_inc(ready, 1)
                    dve.wait_ge(exped, t + 1)
                    step(nc.vector.tensor_reduce(total[:], expo[:], AX.X, ALU.add))
                    step(nc.vector.reciprocal(total[:], total[:]))
                    nc.vector.tensor_tensor(picked[:, 2, t % 2].rearrange("p (h n) -> p h n", h=H), expo[:],
                                            total[:].unsqueeze(2).broadcast_to([P, H, K]), ALU.mult).then_inc(ready, 1)

            @block.scalar
            def _(act):
                for t in range(TT):
                    act.wait_ge(ready, 2 * t + 1)
                    nc.scalar.activation(expo[:], expo[:], ACT.Exp).then_inc(exped, 1)
                    act.wait_ge(turned, t + 1)
                    nc.scalar.activation(k.pairs[:, :, t * P:(t + 1) * P], k.psum[:, t % 2, 0:3 * P].rearrange("p (s n) -> p s n", s=3),
                                         ACT.Copy).then_inc(copied, 1)

            @block.tensor
            def _(pe):
                for t in range(TT):
                    pe.wait_ge(ready, 2 * t + 2)
                    if t >= 2:
                        pe.wait_ge(copied, t - 1)
                    for s in range(3):
                        mm = nc.tensor.transpose(k.psum[:, t % 2, s * P:(s + 1) * P], picked[:, s, t % 2], k.ident[:])
                    mm.then_inc(turned, 1)


def save_stage(k):
    nc = k.nc
    saved = k.sem("x_saved")
    with nc.Block(no_gpsimd_drain=True) as block:
        @block.sync
        def _(sp):
            sp.dma_start(k.x_dram, k.x[:]).then_inc(saved, 16)
            sp.wait_ge(saved, 16)


def peer_gates_stage(k, half):
    nc = k.nc
    hot, used, copied, loaded = (k.sem(f"gates{half}_{s}") for s in ("hot", "used", "copied", "loaded"))
    GROUP = 4
    hot1 = k.acts[:, 0].rearrange("p a n -> p (a n)").rearrange("p (b t n) -> p b t n", b=2, t=GROUP)
    hot2 = k.acts[:, 1].rearrange("p a n -> p (a n)")[:, 0:2 * GROUP * HALF].rearrange("p (b t n) -> p b t n", b=2, t=GROUP)
    index1, index2, gate = (k.pairs[:, s] for s in range(3))
    turns = SEQ // (2 * GROUP)
    with nc.Block(no_gpsimd_drain=True) as block:
        @block.sync
        def _(sp):
            if half == 0:
                sp.dma_start(k.iota[:], k.d["iota"]).then_inc(loaded, 16)

        @block.vector
        def _(dve):
            if half == 0:
                dve.wait_ge(loaded, 16)
                nc.vector.memset(k.y3[:], 0.0)
            dve.sem_inc(used, 2)
            with dve.Fori(0, turns) as g:
                for b in range(2):
                    dve.wait_ge(used, 2 * g + (b + 1))
                    for i in range(GROUP):
                        t = g * (2 * GROUP) + (b * GROUP + i)
                        nc.vector.tensor_scalar(hot1[:, b, i], k.iota[:], index1[:, bass.ds(t, 1)], None, ALU.is_equal)
                        ins = nc.vector.tensor_scalar(hot2[:, b, i], k.iota[:, half * HALF:(half + 1) * HALF],
                                                      index2[:, bass.ds(t, 1)], gate[:, bass.ds(t, 1)], ALU.is_equal, ALU.mult)
                    ins.then_inc(hot, 1)

        @block.tensor
        def _(pe):
            with pe.Fori(0, turns) as g:
                for b in range(2):
                    pe.wait_ge(copied, 2 * g + (b + 1))
                    pe.wait_ge(hot, 2 * g + (b + 1))
                    for i in range(GROUP):
                        mm = nc.tensor.matmul(k.psum[:, b, i * HALF:(i + 1) * HALF], hot1[:, b, i], hot2[:, b, i], start=True, stop=True)
                    mm.then_inc(used, 1)

        @block.scalar
        def _(act):
            act.sem_inc(copied, 2)
            with act.Fori(0, turns) as g:
                for b in range(2):
                    act.wait_ge(used, 2 * g + (b + 3))
                    nc.scalar.activation(
                        k.gate_map[:, :, bass.ds(g * (2 * GROUP) + b * GROUP, GROUP)].rearrange("p j t -> p t j"),
                        k.psum[:, b, 0:GROUP * HALF].rearrange("p (t j) -> p t j", t=GROUP), ACT.Copy).then_inc(copied, 1)


def peer_stage(k, half):
    nc = k.nc
    hid_done, gelu_done, gated, v_done, added = (k.sem(f"peer{half}_{s}") for s in ("hid_done", "gelu_done", "gated", "v_done", "added"))
    batches = HALF // 2
    first = FIRST["peer"] + half * 2 * batches
    loops = (batches - 2) // 2
    with nc.Block(no_gpsimd_drain=True) as block:
        @block.sync
        def _(sp):
            def refill(n, used, value, r):
                s = (first + r) % SLOTS
                sp.wait_ge(used, value)
                sp.dma_start(k.ring[:, s, :], k.weights[bass.ds(n + (first + SLOTS), 1)].rearrange("a p n -> p (a n)")).then_inc(
                    k.tile_loaded[s], 16)

            def batch_tiles(b, r):
                refill(2 * b + 1, hid_done, 2 * b + 4, 2 * r + 1)
                refill(2 * b + 2, v_done, 8 * b + 8, 2 * r + 2)

            refill(0, hid_done, 2, 0)
            end = (batches - 1) if half == 0 else (batches - 3)
            with sp.Fori(0, end // 2) as g:
                for j in range(2):
                    batch_tiles(2 * g + j, j)
            if end % 2:
                batch_tiles(end - 1, end - 1)
            if half == 0:
                refill(2 * batches - 1, v_done, 8 * batches, 2 * batches - 1)
            else:
                refill(2 * end + 1, hid_done, 2 * end + 4, 2 * end + 1)

        @block.tensor
        def _(pe):
            def hidden(parity, s):
                for jj in range(2):
                    for kc in range(KC):
                        at = (jj * KC + kc) * P
                        mm = nc.tensor.matmul(k.psum[:, 2 * parity + jj], k.ring[:, s, at:at + P], k.h[:, kc], start=kc == 0, stop=kc == KC - 1)
                    mm.then_inc(hid_done, 1)

            def out(b, parity, s, wait):
                for m in range(KC):
                    if wait or m >= 4:
                        pe.wait_ge(added, 8 * b + (m - 3))
                    for jj in range(2):
                        at = jj * D + m * P
                        mm = nc.tensor.matmul(k.psum[:, 4 + m % 4], k.ring[:, s, at:at + P], k.acts[:, parity, jj], start=jj == 0, stop=jj == 1)
                    mm.then_inc(v_done, 1)

            def turn(n):
                return 16 * ((first + n) // SLOTS + 1)

            def body(b, r, shift):
                if r > 0:
                    pe.wait_ge(gelu_done, 2 * b)
                n = 2 * r + 1
                pe.wait_ge(k.tile_loaded[(first + n) % SLOTS], shift + turn(n))
                hidden((r + 1) % 2, (first + n) % SLOTS)
                pe.wait_ge(gated, 2 * b + 2)
                pe.wait_ge(k.tile_loaded[(first + n + 1) % SLOTS], shift + turn(n + 1))
                out(b, r % 2, (first + n + 1) % SLOTS, r > 0)

            wait_tile(k, pe, first)
            hidden(0, first % SLOTS)
            body(0, 0, 0)
            with pe.Fori(0, loops) as g:
                for j in range(1, 3):
                    body(2 * g + j, j, 16 * g)
            for b in range(2 * loops + 1, batches - 1):
                body(b, b, 0)
            n = 2 * batches - 1
            wait_tile(k, pe, first + n)
            pe.wait_ge(gated, 2 * batches)
            out(batches - 1, (batches - 1) % 2, (first + n) % SLOTS, True)

        @block.scalar
        def _(act):
            with act.Fori(0, batches // 2) as g:
                for j in range(2):
                    for jj in range(2):
                        act.wait_ge(hid_done, 4 * g + (2 * j + jj + 1))
                        nc.scalar.activation(k.acts[:, j, jj], k.psum[:, 2 * j + jj], ACT.Gelu).then_inc(gelu_done, 1)

        @block.vector
        def _(dve):
            def gate(b, parity):
                for jj in range(2):
                    dve.wait_ge(gelu_done, 2 * b + (jj + 1))
                    nc.vector.tensor_tensor(k.acts[:, parity, jj], k.acts[:, parity, jj],
                                            k.gate_map[:, bass.ds(2 * b + jj, 1)].rearrange("p a n -> p (a n)"), ALU.mult).then_inc(gated, 1)

            def add(b):
                for m in range(KC):
                    dve.wait_ge(v_done, 8 * b + (m + 1))
                    nc.vector.tensor_tensor(k.y3[:, m], k.y3[:, m], k.psum[:, 4 + m % 4], ALU.add).then_inc(added, 1)

            gate(0, 0)
            gate(1, 1)
            add(0)
            with dve.Fori(1, batches // 2) as g:
                for j in range(2):
                    gate(2 * g + j, j)
                    add(2 * g + (j - 1))
            add(batches - 1)


def reload_stage(k):
    nc = k.nc
    loaded = k.sem("x_reloaded")
    with nc.Block(no_gpsimd_drain=True) as block:
        @block.sync
        def _(sp):
            sp.dma_start(k.x2[:], k.x_dram).then_inc(loaded, 16)
            sp.wait_ge(loaded, 16)

        @block.vector
        def _(dve):
            nc.vector.memset(k.ones2[:], 1.0)


def store_stage(k):
    nc = k.nc
    stored = k.sem("out_stored")
    with nc.Block(no_gpsimd_drain=True) as block:
        @block.sync
        def _(sp):
            sp.dma_start(k.d["out"], k.x2[:]).then_inc(stored, 16)
            sp.wait_ge(stored, 16)


def build(nc, d):
    with ExitStack() as whole:
        k = Core()
        k.nc, k.d, k.weights = nc, d, d["weights"]
        k.sem = lambda name: whole.enter_context(nc.semaphore(name))

        def place(scope, **shapes):
            return [scope.enter_context(nc.sbuf_tensor(name, shape, F32)) for name, shape in shapes.items()]

        k.tile_loaded = [k.sem(f"tile_loaded{i}") for i in range(SLOTS)]
        k.loaded = k.sem("vectors_loaded")
        k.vstep = Steps(nc.vector, k.sem("vector_step"))
        k.psum = whole.enter_context(nc.psum_tensor("psum", [P, 8, BANK], F32))
        k.comb_dram = nc.dram_tensor("comb_dram", (EXPERTS, SEQ), F32, kind="Internal").ap()
        k.x_dram = nc.dram_tensor("x_dram", (P, KC, SEQ), F32, kind="Internal").ap()
        k.ring, k.mod1, k.mod2, k.vecs, k.eps, k.h, k.pairs = place(
            whole, ring=[P, SLOTS, TILE], mod1=[P, N_MOD], mod2=[P, 2, N_MOD], vecs=[P, N_VECS], eps=[P, 2], h=[P, KC, SEQ],
            pairs=[P, 3, SEQ])
        with ExitStack() as main:
            k.x, k.ident, k.ones = place(main, x=[P, KC, SEQ], ident=[P, P], ones=[P, P])
            with ExitStack() as scope:
                k.ada_vecs, k.cond = place(scope, ada_vecs=[P, N_ADA], cond=[P, KC, 3])
                load_stage(k)
                ada_stage(k)
            norm_stage(k, "norm_mix", k.x, k.h, SEQ, k.mod1[:, SCALE_1:SCALE_1 + KC], k.mod1[:, SHIFT_1:SHIFT_1 + KC])
            with ExitStack() as scope:
                (k.proj, k.v_b, k.small, k.causal, k.chosen, k.o, k.neg_cum, k.slope_pos, k.head_rows) = place(
                    scope, proj=[P, FM_CHUNKS, SEQ], v_b=[P, TT, HEADS * DH], small=[P, TT, SMALL], causal=[P, SEQ],
                    chosen=[P, TT, SEQ], o=[P, TT, D], neg_cum=[HEADS, SEQ], slope_pos=[HEADS, SEQ], head_rows=[HEADS, HEADS, P])
                in_projection_stage(k)
                forget_stage(k)
                index_stage(k)
                attention_stage(k)
                head_norm_stage(k, "out1_norm", 2, k.vecs[:, G_OUT:G_OUT + KC])
            out_projection_stage(k)
            norm_stage(k, "norm_ffn", k.x, k.h, SEQ, k.mod1[:, SCALE_2:SCALE_2 + KC], k.mod1[:, SHIFT_2:SHIFT_2 + KC])
            with ExitStack() as scope:
                k.y, k.route_less = place(scope, y=[P, KC, SEQ], route_less=[P, TT, GROUPS])
                router_stage(k)
                moe_stage(k)
                add_gated_stage(k, k.y, k.mod1[:, GATE_2:GATE_2 + KC])
            norm_stage(k, "norm_final", k.x, k.x, SEQ, k.vecs[:, G_FINAL:G_FINAL + KC])
            with ExitStack() as scope:
                k.u, k.o = place(scope, u=[P, KC, SEQ], o2=[P, TT, D])
                with ExitStack() as attention:
                    k.q2, k.k2, k.v2 = place(attention, q2=[P, KC, SEQ], k2=[P, KC, KEYS], v2=[P, KT, D])
                    with ExitStack() as inner:
                        k.h_ctx, k.rope, k.swap = place(inner, h_ctx=[P, KC, CTX], rope=[P, 2, SEQ], swap=[P, P])
                        load_context_stage(k)
                        norm_stage(k, "norm_ctx", k.h_ctx, k.h_ctx, CTX, k.mod2[:, 1, SCALE_1:SCALE_1 + KC],
                                   k.mod2[:, 1, SHIFT_1:SHIFT_1 + KC])
                        norm_stage(k, "norm_mix2", k.x, k.h, SEQ, k.mod2[:, 0, SCALE_1:SCALE_1 + KC],
                                   k.mod2[:, 0, SHIFT_1:SHIFT_1 + KC])
                        qk_stage(k)
                        values_stage(k)
                    with ExitStack() as inner:
                        (k.vz,) = place(inner, vz=[P, TT, D])
                        sgu_projection_stage(k)
                        sgu_stage(k)
                    diff_attention_stage(k)
                (k.gates,) = place(scope, gates=[P, 2 * KC, SEQ])
                gates_stage(k)
                head_norm_stage(k, "out2_norm", DIFF_HEADS, k.vecs[:, SUBLN:SUBLN + 1].broadcast_to([P, KC]), 1.0 - LAMBDA_INIT)
                k.y2 = k.o[:].rearrange("p t d -> p (t d)").rearrange("p (c n) -> p c n", c=KC)
                branches_stage(k)
                norm_stage(k, "norm_post_mix", k.y2, k.y2, SEQ, k.mod2[:, 0, GATE_1:GATE_1 + KC], add_to=k.x)
            norm_stage(k, "norm_ffn2", k.x, k.h, SEQ, k.mod2[:, 0, SCALE_2:SCALE_2 + KC], k.mod2[:, 0, SHIFT_2:SHIFT_2 + KC])
            with ExitStack() as scope:
                (k.scores,) = place(scope, scores=[P, TT, 2 * PEER_HEADS, PEER_KEYS])
                query_stage(k)
                peer_choice_stage(k)
            save_stage(k)
        with ExitStack() as tail:
            (k.y3,) = place(tail, y3=[P, KC, SEQ])
            with ExitStack() as scope:
                k.gate_map, k.acts, k.iota = place(scope, gate_map=[P, HALF, SEQ], acts=[P, 2, 2, SEQ], iota=[P, P])
                for half in range(2):
                    peer_gates_stage(k, half)
                    peer_stage(k, half)
            k.x2, k.ones2 = place(tail, x2=[P, KC, SEQ], ones2=[P, P])
            k.ones = k.ones2
            reload_stage(k)
            norm_stage(k, "norm_post_ffn", k.y3, k.y3, SEQ, k.mod2[:, 0, GATE_2:GATE_2 + KC], add_to=k.x2)
            store_stage(k)
        return k



def feature_major(w):
    m = w.shape[1]
    return w.reshape(KC, P, m // (2 * P), 2, P).transpose(2, 1, 3, 0, 4).reshape(m // (2 * P), P, TILE)


def token_major(w):
    m = w.shape[1]
    return w.reshape(2, KC // 2, P, m // BANK, BANK).transpose(3, 0, 2, 1, 4).reshape(2 * (m // BANK), P, TILE)


def columns(v):
    return np.ascontiguousarray(v).reshape(-1, P).T


def pack_weights(i):
    w = np.empty((N_TILES, P, TILE), np.float32)

    def put(stage, at, tiles):
        w[FIRST[stage] + at:FIRST[stage] + at + len(tiles)] = tiles

    put("ada1", 0, feature_major(i["w_ada"][0]))
    put("ada2", 0, feature_major(i["w_ada_2"][0]))
    aq, ak, av, iq, ik, iw, bq, bk, bv, bf = np.split(
        i["w_in"][0], np.cumsum([512, 128, 128, 512, 64, 8, 512, 512, 512]).tolist(), axis=1)
    aq = aq.reshape(D, 2, 4, DH).transpose(0, 2, 1, 3).reshape(D, 512)
    put("in1", 0, feature_major(np.concatenate([aq, iq, bq, bk, ak, ik, ik], axis=1)))
    put("in1", FM_CHUNKS // 2, token_major(bv))
    put("out1", 0, feature_major(i["w_out"][0]))
    for e in range(EXPERTS):
        at = 3 * e - 1 if e else 0
        put("moe", at, feature_major(i["w_gate"][0, e]))
        put("moe", at + 1, feature_major(i["w_up"][0, e]))
        put("moe", 3 * e + 4 if e < EXPERTS - 1 else 3 * e + 2, i["w_down"][0, e].reshape(2, P, D).transpose(1, 0, 2).reshape(1, P, TILE))
    w2 = i["w_in_2"][0]
    put("qk2", 0, feature_major(w2[:, 0:2 * D]))
    put("v2", 0, token_major(w2[:, 2 * D:3 * D]))
    put("z2", 0, feature_major(w2[:, 3 * D:4 * D]))
    put("z2", 4, token_major(w2[:, 4 * D:5 * D]))
    put("gate2", 0, feature_major(w2[:, 5 * D:7 * D]))
    put("branch2", 0, feature_major(i["w_branch_attn_2"][0]))
    put("branch2", 4, feature_major(i["w_branch_sgu_2"][0]))
    put("out2", 0, feature_major(i["w_out_2"][0]))
    put("query", 0, feature_major(i["peer_w_query_2"][0]))
    u = i["peer_u_2"][0].reshape(PEER_KEYS, PEER_KEYS // 2, 2, KC, P).transpose(1, 4, 2, 3, 0).reshape(PEER_KEYS // 2, P, TILE)
    v = i["peer_v_2"][0].reshape(PEER_KEYS, PEER_KEYS // 2, TILE).transpose(1, 0, 2)
    batches = HALF // 2
    for half in range(2):
        for b in range(batches):
            put("peer", half * 2 * batches + (2 * b - 1 if b else 0), u[half * batches + b:half * batches + b + 1])
            put("peer", half * 2 * batches + (2 * b + 2 if b < batches - 1 else 2 * b + 1), v[half * batches + b:half * batches + b + 1])
    return w


def constants():
    t = np.arange(SEQ)
    q = np.arange(P)
    causal = np.zeros((P, SEQ), np.float32)
    causal[:, SEQ - P:] = np.where(q[None, :] > q[:, None], MASKED, 0.0)
    slopes = 2.0 ** -np.arange(1, HEADS + 1)
    head_rows = np.zeros((HEADS, HEADS, P), np.float32)
    head_rows[np.arange(HEADS), np.arange(HEADS)] = 1.0
    n_freq = DH // 4
    inv = (np.float32(10000.0) ** (-np.arange(n_freq, dtype=np.float32) / np.float32(n_freq))).astype(np.float32)
    f = np.arange(P) % DH
    pos = np.where((f < DH // 2)[:, None], (t // 64)[None, :], (t % 64)[None, :]).astype(np.float32)
    angle = (pos * inv[f % n_freq][:, None]).astype(np.float32)
    sign = np.where(f % (DH // 2) < n_freq, -1.0, 1.0)
    rope = np.stack([np.cos(angle), np.sin(angle) * sign[:, None]], axis=1).astype(np.float32)
    swap = np.zeros((P, P), np.float32)
    swap[np.arange(P) ^ n_freq, np.arange(P)] = 1.0
    return {
        "ident": np.eye(P, dtype=np.float32),
        "iota": np.tile(np.arange(P, dtype=np.float32), (P, 1)),
        "tri": (q[:, None, None] + P * np.arange(TT)[None, :, None] <= t[None, None, :]).astype(np.float32),
        "causal": causal,
        "head_rows": head_rows,
        "slope_pos": (slopes[:, None] * (t - (SEQ - P))[None, :]).astype(np.float32),
        "prio": np.tile(np.arange(PER_GROUP, 0, -1).astype(np.float32), (P, 1)),
        "rope": rope,
        "swap": swap,
    }


def lay_out(i):
    lam = np.zeros((P, 4), np.float32)
    for n, name in enumerate(("lambda_q1_2", "lambda_k1_2", "lambda_q2_2", "lambda_k2_2")):
        lam[:DH, n] = i[name][0]
    small = np.split(i["w_in"][0], np.cumsum([512, 128, 128, 512, 64, 8, 1536]).tolist(), axis=1)
    rows = lambda w: w.reshape(KC, P, -1).transpose(1, 0, 2)
    return constants() | {
        "weights": pack_weights(i),
        "x": rows(i["x"][0].T),
        "ctx": rows(i["ctx_2"][0].T),
        "ada_vecs": np.concatenate([columns(i["c"]), columns(i["c_2"]), columns(i["c_ctx_2"]), columns(i["b_ada"]),
                                    columns(i["b_ada_2"])], axis=1),
        "vecs": np.concatenate([columns(i[n]) for n in ("g_mix", "g_out_a", "g_out_b", "g_ffn", "g_final", "g_pre_mix_2", "g_post_mix_2",
                                                        "g_pre_ffn_2", "g_post_ffn_2", "b_gate_2", "subln_g_2")] + [lam], axis=1),
        "w_small": rows(np.concatenate([small[2], small[5], small[7]], axis=1)),
        "b_forget": i["b_forget"],
        "w_route": rows(np.concatenate([i["w_group"][0], i["w_router"][0].transpose(1, 0, 2).reshape(D, EXPERTS)], axis=1)),
        "b_route": np.concatenate([i["b_group"], i["b_router"].reshape(1, EXPERTS)], axis=1),
        "ln_g": i["sgu_ln_g_2"],
        "ln_b": i["sgu_ln_b_2"],
        "sgu_w": i["sgu_w_2"][0].transpose(2, 0, 1),
        "sgu_b": i["sgu_b_2"].reshape(1, D),
        "peer_keys": i["peer_sub_keys_2"][0].transpose(2, 0, 1),
    }


def program(arrays, nc):
    d = {n: nc.dram_tensor("in_" + n, a.shape, F32, kind="ExternalInput").ap() for n, a in arrays.items()}
    d["out"] = nc.dram_tensor("out", (P, KC, SEQ), F32, kind="ExternalOutput").ap()
    return build(nc, d)


def kernel(**inputs):
    import concourse.bacc as bacc
    from concourse.bass_utils import run_bass_kernel_spmd

    arrays = {n: np.ascontiguousarray(a) for n, a in lay_out({n: np.asarray(a) for n, a in inputs.items()}).items()}
    nc = bacc.Bacc("TRN2", target_bir_lowering=False, num_devices=1)
    program(arrays, nc)
    result = run_bass_kernel_spmd(nc, [{"in_" + n: a for n, a in arrays.items()}], core_ids=[0]).results[0]["out"]
    return np.ascontiguousarray(result.transpose(1, 0, 2).reshape(D, SEQ).T).reshape(1, SEQ, D)
```

```python
from contextlib import ExitStack

import numpy as np

import concourse.bass as bass
import concourse.mybir as mybir

F32 = mybir.dt.float32
F32R = mybir.dt.float32r
U32 = mybir.dt.uint32
ACT = mybir.ActivationFunctionType
ALU = mybir.AluOpType
AX = mybir.AxisListType

P = 128
SEQ, D = 512, 1024
CTX = 256
KC = D // P
TT = SEQ // P
BANK = 512
SLOTS, TILE = 4, 2048
EPS, LN_EPS = 1e-6, 1e-5

HEADS, DH = 8, 64
TOPK = min(256, SEQ // 4)
GROUPS, PER_GROUP = 4, 8
EXPERTS, FF = GROUPS * PER_GROUP, D // 4
EXPERT_TILES = (2 * SEQ + EXPERTS * (P - 1)) // P
DIFF_HEADS = 8
KEYS = CTX + SEQ
KT = KEYS // P
LAMBDA_INIT = 0.2
SGU_GROUPS = 8
PEER_HEADS, PEER_KEYS, PEER_TOPK = 8, 128, 16
PAIRS = PEER_HEADS * PEER_TOPK
SPAN = 64

MASKED, FILL, TAKEN = -1e30, -1e38, -3e38
TAKEN_BELOW = -2e38

AQ, IQ, BQ, BK, AK, IK = 0, 4, 8, 12, 16, 17
FM_CHUNKS = 18
SMALL = 144
G_MIX, G_OUT, G_FFN, G_FINAL, G_PRE_MIX, G_POST_MIX, G_PRE_FFN, G_POST_FFN = range(0, 64, 8)
B_GATE, SUBLN, LAMBDA, N_VECS = 64, 80, 81, 85
N_MOD = 6 * KC
ADA_C, ADA_B1, ADA_B2, N_ADA = 0, 24, 24 + N_MOD, 24 + 2 * N_MOD
SHIFT_1, SCALE_1, GATE_1, SHIFT_2, SCALE_2, GATE_2 = range(0, N_MOD, KC)

STAGES = [("ada1", 24), ("ada2", 24), ("in1", 11), ("out1", 4), ("qk2", 8), ("v2", 4),
          ("z2", 8), ("gate2", 8), ("branch2", 8), ("out2", 4), ("query", 8), ("peer", PEER_KEYS)]
FIRST = {}
N_TILES = 0
for _name, _n in STAGES:
    FIRST[_name] = N_TILES
    N_TILES += _n
COUNT = dict(STAGES)


class Core:
    pass


class Steps:

    def __init__(self, eng, sem):
        self.eng, self.sem, self.n = eng, sem, 0

    def __call__(self, ins):
        ins.then_inc(self.sem, 1)
        self.n += 1
        self.eng.wait_ge(self.sem, self.n)


def wait_tile(k, pe, n):
    pe.wait_ge(k.tile_loaded[n % SLOTS], 16 * (n // SLOTS + 1))


def slot(k, n):
    return k.ring[:, n % SLOTS, :]


def stream(k, sp, first, count, used, value):
    for n in range(first, min(first + count, N_TILES - SLOTS)):
        sp.wait_ge(used, value(n - first))
        sp.dma_start(slot(k, n + SLOTS), k.weights[n + SLOTS]).then_inc(k.tile_loaded[n % SLOTS], 16)


def load_stage(k):
    nc = k.nc
    with nc.Block(no_gpsimd_drain=True) as block:
        @block.sync
        def _(sp):
            for n in range(SLOTS):
                sp.dma_start(slot(k, n), k.weights[n]).then_inc(k.tile_loaded[n], 16)

        @block.scalar
        def _(act):
            act.dma_start(k.ada_vecs[:], k.d["ada_vecs"]).then_inc(k.loaded, 16)
            act.dma_start(k.vecs[:], k.d["vecs"]).then_inc(k.loaded, 16)
            act.dma_start(k.x[:], k.d["x"]).then_inc(k.loaded, 16)
            act.dma_start(k.ident[:], k.d["ident"]).then_inc(k.loaded, 16)
            act.wait_ge(k.loaded, 64)

        @block.vector
        def _(dve):
            nc.vector.memset(k.ones[:], 1.0).then_inc(k.vstep.sem, 1)
            nc.vector.memset(k.eps[:, 0:1], EPS).then_inc(k.vstep.sem, 1)
            nc.vector.memset(k.eps[:, 1:2], LN_EPS).then_inc(k.vstep.sem, 1)
            k.vstep.n += 3


def ada_stage(k):
    nc = k.nc
    tile_used, cond_ready, rows_copied, turned, added = (
        k.sem(f"ada_{s}") for s in ("tile_used", "cond_ready", "rows_copied", "turned", "added"))
    n1 = COUNT["ada1"]
    rows = k.ada_rows
    with nc.Block(no_gpsimd_drain=True) as block:
        @block.sync
        def _(sp):
            with sp.Fori(0, 2 * n1 // SLOTS) as g:
                for s in range(SLOTS):
                    n = g * SLOTS + s
                    sp.wait_ge(tile_used, n + 1)
                    sp.dma_start(slot(k, s), k.weights[bass.ds(n + SLOTS, 1)].rearrange("a p n -> p (a n)")).then_inc(
                        k.tile_loaded[s], 16)

        @block.scalar
        def _(act):
            nc.scalar.activation(k.cond[:].rearrange("p c v -> p v c"), k.ada_vecs[:, ADA_C:ADA_C + 24].rearrange(
                "p (v c) -> p v c", v=3), ACT.Silu).then_inc(cond_ready, 1)

        spans = D * 6 // BANK
        turns, per_span = spans // 2, BANK // P
        blocks = ((0, slice(0, 1)), (spans, slice(1, 3)))

        @block.tensor
        def _(pe):
            pe.wait_ge(cond_ready, 1)
            for base, vectors in blocks:
                width = vectors.stop - vectors.start
                with pe.Fori(0, turns) as g:
                    for b in range(2):
                        pe.wait_ge(rows_copied, 2 * g + (base + b + 1))
                        for s in (2 * b, 2 * b + 1):
                            pe.wait_ge(k.tile_loaded[s], 16 * g + 16 * (base // 2 + 1))
                            for kc in range(KC // 2):
                                n = (s % 2) * (KC // 2) + kc
                                mm = nc.tensor.matmul(k.psum[0:width, b], k.cond[:, n, vectors], slot(k, s)[:, kc * BANK:(kc + 1) * BANK],
                                                      start=n == 0, stop=n == KC - 1)
                            mm.then_inc(tile_used, 1)
                    for b in range(2):
                        pe.wait_ge(rows_copied, 2 * g + (base + b + 2 + 1))
                        pe.wait_ge(added, 2 * g + (base + b + 1))
                        for c in range(per_span):
                            mm = nc.tensor.matmul(k.psum[:, 2 + b, c * width:(c + 1) * width], rows[0:width, b, c * P:(c + 1) * P],
                                                  k.ident[0:width, 0:width], start=True, stop=True)
                        mm.then_inc(turned, 1)

        @block.vector
        def _(dve):
            step = k.vstep
            dve.sem_inc(rows_copied, 2)
            dve.wait_ge(rows_copied, 2)
            dve.sem_inc(added, 2)
            for base, vectors in blocks:
                width = vectors.stop - vectors.start
                bias = ADA_B1 if base == 0 else ADA_B2
                with dve.Fori(0, turns) as g:
                    for b in range(2):
                        dve.wait_ge(tile_used, 4 * g + (2 * base + 2 * b + 2))
                        nc.vector.tensor_copy(rows[0:width, b], k.psum[0:width, b]).then_inc(rows_copied, 1)
                    for b in range(2):
                        dve.wait_ge(turned, 2 * g + (base + b + 1))
                        at = g * (2 * per_span) + b * per_span
                        sums = k.psum[:, 2 + b, 0:per_span * width].rearrange("p (m v) -> p v m", v=width)
                        add = k.ada_vecs[:, bass.ds(at + bias, per_span)].unsqueeze(1).broadcast_to([P, width, per_span])
                        out = k.mod1[:, bass.ds(at, per_span)].unsqueeze(1) if base == 0 else k.mod2[:, :, bass.ds(at, per_span)]
                        nc.vector.tensor_tensor(out, sums, add, ALU.add).then_inc(added, 1)
            dve.wait_ge(added, 2 + 2 * spans)

            def fold(part, gain, one):
                step(nc.vector.scalar_tensor_tensor(part, part, one, k.vecs[:, gain:gain + KC], ALU.add, ALU.mult))

            fold(k.mod1[:, SCALE_1:SCALE_1 + KC], G_MIX, 1.0)
            fold(k.mod1[:, SCALE_2:SCALE_2 + KC], G_FFN, 1.0)
            fold(k.mod2[:, 0, SCALE_1:SCALE_1 + KC], G_PRE_MIX, 1.0)
            fold(k.mod2[:, 1, SCALE_1:SCALE_1 + KC], G_PRE_MIX, 1.0)
            fold(k.mod2[:, 0, SCALE_2:SCALE_2 + KC], G_PRE_FFN, 1.0)
            fold(k.mod2[:, 0, GATE_1:GATE_1 + KC], G_POST_MIX, 0.0)
            fold(k.mod2[:, 0, GATE_2:GATE_2 + KC], G_POST_FFN, 0.0)


def norm_stage(k, name, source, target, width, gain, shift=None, add_to=None):
    nc = k.nc
    squared, summed, std_ready, scaled = k.norm_sems
    turn, k.norms = k.norms, k.norms + 1
    before = KC * turn
    with ExitStack() as scope:
        square = scope.enter_context(nc.sbuf_tensor(f"{name}_square", [P, 2, width], F32))
        std = scope.enter_context(nc.sbuf_tensor(f"{name}_std", [P, width], F32))
        rstd = scope.enter_context(nc.sbuf_tensor(f"{name}_rstd", [P, width], F32))
        with nc.Block(no_gpsimd_drain=True) as block:
            @block.scalar
            def _(act):
                for c in range(KC):
                    if c >= 2:
                        act.wait_ge(summed, before + c - 1)
                    nc.scalar.activation(square[:, c % 2], source[:, c], ACT.Square).then_inc(squared, 1)
                act.wait_ge(summed, before + KC)
                nc.scalar.activation(std[:], k.psum[:, 0, 0:width], ACT.Sqrt, bias=k.eps[:, 0:1], scale=1.0 / D).then_inc(
                    std_ready, 1)
                if shift is not None:
                    for c in range(KC):
                        act.wait_ge(scaled, before + c + 1)
                        nc.scalar.activation(target[:, c], target[:, c], ACT.Identity, bias=shift[:, c:c + 1])

            @block.tensor
            def _(pe):
                for c in range(KC):
                    pe.wait_ge(squared, before + c + 1)
                    nc.tensor.matmul(k.psum[:, 0, 0:width], k.ones[:], square[:, c % 2], start=c == 0,
                                     stop=c == KC - 1).then_inc(summed, 1)

            @block.vector
            def _(dve):
                dve.wait_ge(std_ready, turn + 1)
                k.vstep(nc.vector.reciprocal(rstd[:], std[:]))
                for c in range(KC):
                    nc.vector.scalar_tensor_tensor(target[:, c], source[:, c], gain[:, c:c + 1], rstd[:], ALU.mult,
                                                   ALU.mult).then_inc(scaled, 1)
                if add_to is not None:
                    dve.wait_ge(scaled, before + KC)
                    for c in range(KC):
                        nc.vector.tensor_tensor(add_to[:, c], add_to[:, c], target[:, c], ALU.add)


def chunk_products(k, pe, out, tiles, c, source, done):
    n = tiles + c // 2
    if c % 2 == 0:
        wait_tile(k, pe, n)
    for kc in range(KC):
        at = ((c % 2) * KC + kc) * P
        mm = k.nc.tensor.matmul(out, slot(k, n)[:, at:at + P], source[:, kc], start=kc == 0, stop=kc == KC - 1)
    mm.then_inc(done, 1)


def row_products(k, pe, out, tiles, token_tile, done):
    for kc in range(KC):
        mm = k.nc.tensor.matmul(out, token_tile(kc), slot(k, tiles + kc // 4)[:, (kc % 4) * BANK:(kc % 4 + 1) * BANK],
                                start=kc == 0, stop=kc == KC - 1)
    mm.then_inc(done, 1)


def in_projection_stage(k):
    nc = k.nc
    done, copied, rows_done, rows_copied, loaded = (
        k.sem(s) for s in ("in1_done", "in1_copied", "in1_rows_done", "in1_rows_copied", "in1_loaded"))
    first = FIRST["in1"]
    n_fm = FM_CHUNKS // 2
    with ExitStack() as scope:
        w_small = scope.enter_context(nc.sbuf_tensor("w_small", [P, KC, SMALL], F32))
        with nc.Block(no_gpsimd_drain=True) as block:
            @block.sync
            def _(sp):
                sp.dma_start(w_small[:], k.d["w_small"]).then_inc(loaded, 16)
                stream(k, sp, first, n_fm, done, lambda n: 2 * (n + 1))
                stream(k, sp, first + n_fm, 2, rows_done, lambda n: TT)

            @block.tensor
            def _(pe):
                for c in range(FM_CHUNKS):
                    if c >= 4:
                        pe.wait_ge(copied, c - 3)
                    chunk_products(k, pe, k.psum[:, c % 4], first, c, k.h, done)
                wait_tile(k, pe, first + n_fm)
                wait_tile(k, pe, first + n_fm + 1)
                for t in range(TT):
                    if t >= 2:
                        pe.wait_ge(rows_copied, t - 1)
                    row_products(k, pe, k.psum[:, 4 + t % 2], first + n_fm, lambda kc: k.h[:, kc, t * P:(t + 1) * P], rows_done)
                pe.wait_ge(loaded, 16)
                for t in range(TT):
                    for kc in range(KC):
                        mm = nc.tensor.matmul(k.psum[:, 6 + t // 2, (t % 2) * SMALL:(t % 2 + 1) * SMALL],
                                              k.h[:, kc, t * P:(t + 1) * P], w_small[:, kc], start=kc == 0, stop=kc == KC - 1)
                mm.then_inc(rows_done, 1)

            @block.scalar
            def _(act):
                for c in range(FM_CHUNKS):
                    act.wait_ge(done, c + 1)
                    query = c < IQ or BQ <= c < BK
                    nc.scalar.activation(k.proj[:, c], k.psum[:, c % 4], ACT.Copy, scale=DH ** -0.5 if query else 1.0).then_inc(
                        copied, 1)

            @block.vector
            def _(dve):
                for t in range(TT):
                    dve.wait_ge(rows_done, t + 1)
                    nc.vector.tensor_copy(k.v_b[:, t], k.psum[:, 4 + t % 2]).then_inc(rows_copied, 1)
                dve.wait_ge(rows_done, TT + 1)
                for i in range(2):
                    nc.vector.tensor_copy(k.small[:, 2 * i:2 * i + 2], k.psum[:, 6 + i, 0:2 * SMALL].rearrange(
                        "p (t n) -> p t n", t=2)).then_inc(rows_copied, 1)


def forget_stage(k):
    nc = k.nc
    loaded, at_vector, at_scalar, summed = (k.sem(f"forget_{s}") for s in ("loaded", "vector", "scalar", "summed"))
    with ExitStack() as scope:
        tri = scope.enter_context(nc.sbuf_tensor("tri", [P, TT, SEQ], F32))
        b_row = scope.enter_context(nc.sbuf_tensor("b_forget_row", [P, HEADS], F32))
        z, mag, e, log_f = (scope.enter_context(nc.sbuf_tensor(f"forget_{n}", [P, TT, HEADS], F32)) for n in
                            ("z", "mag", "e", "log_f"))
        with nc.Block(no_gpsimd_drain=True) as block:
            @block.sync
            def _(sp):
                sp.dma_start(b_row[:], k.d["b_forget"][0].partition_broadcast(P)).then_inc(loaded, 16)
                sp.dma_start(tri[:], k.d["tri"]).then_inc(loaded, 16)
                sp.dma_start(k.causal[:], k.d["causal"]).then_inc(loaded, 16)
                sp.dma_start(k.head_rows[:], k.d["head_rows"]).then_inc(loaded, 16)
                sp.dma_start(k.slope_pos[:], k.d["slope_pos"]).then_inc(loaded, 16)
                sp.wait_ge(loaded, 80)

            @block.vector
            def _(dve):
                step = k.vstep
                dve.wait_ge(loaded, 80)
                step(nc.vector.tensor_tensor(z[:], k.small[:, :, 136:144], b_row[:].unsqueeze(1).broadcast_to([P, TT, HEADS]),
                                             ALU.add))
                nc.vector.scalar_tensor_tensor(mag[:], z[:], -1.0, z[:], ALU.mult, ALU.max).then_inc(at_vector, 1)
                dve.wait_ge(at_scalar, 2)
                nc.vector.scalar_tensor_tensor(log_f[:], z[:], 0.0, e[:], ALU.min, ALU.subtract).then_inc(at_vector, 1)

            @block.scalar
            def _(act):
                act.wait_ge(at_vector, 1)
                nc.scalar.activation(e[:], mag[:], ACT.Exp, scale=-1.0).then_inc(at_scalar, 1)
                act.wait_ge(at_scalar, 1)
                nc.scalar.activation(e[:], e[:], ACT.Ln, bias=1.0).then_inc(at_scalar, 1)
                act.wait_ge(summed, 1)
                nc.scalar.activation(k.neg_cum[:], k.psum[0:HEADS, 0], ACT.Copy, scale=-1.0)

            @block.tensor
            def _(pe):
                pe.wait_ge(loaded, 80)
                pe.wait_ge(at_vector, 2)
                for t in range(TT):
                    mm = nc.tensor.matmul(k.psum[0:HEADS, 0], log_f[:, t], tri[:, t], start=t == 0, stop=t == TT - 1)
                mm.then_inc(summed, 1)


def head_half(chunk_view, half):
    return chunk_view[half * DH:(half + 1) * DH]


def index_stage(k):
    nc = k.nc
    done, relued, added = (k.sem(f"index_{s}") for s in ("done", "relued", "added"))
    units = [(i, h) for i in range(1, TT) for h in range(HEADS)]
    with ExitStack() as scope:
        score = scope.enter_context(nc.sbuf_tensor("index_score", [P, TT, SEQ], F32))
        relu = scope.enter_context(nc.sbuf_tensor("index_relu", [P, 2, SEQ], F32))
        top = scope.enter_context(nc.sbuf_tensor("index_top", [P, TT, 8], F32))
        with nc.Block(no_gpsimd_drain=True) as block:
            @block.tensor
            def _(pe):
                for u, (i, h) in enumerate(units):
                    if u >= 2:
                        pe.wait_ge(relued, u - 1)
                    nc.tensor.matmul(k.psum[:, u % 2, 0:P * (i + 1)],
                                     head_half(k.proj[:, IQ + h // 2, i * P:(i + 1) * P], h % 2),
                                     head_half(k.proj[:, IK, 0:P * (i + 1)], h % 2), start=True, stop=True).then_inc(done, 1)

            @block.scalar
            def _(act):
                for u, (i, h) in enumerate(units):
                    act.wait_ge(done, u + 1)
                    if u >= 2:
                        act.wait_ge(added, u - 1)
                    nc.scalar.activation(relu[:, u % 2, 0:P * (i + 1)], k.psum[:, u % 2, 0:P * (i + 1)], ACT.Relu).then_inc(
                        relued, 1)

            @block.vector
            def _(dve):
                step = k.vstep
                for u, (i, h) in enumerate(units):
                    w = P * (i + 1)
                    weight = k.small[:, i, 128 + h:129 + h]
                    dve.wait_ge(relued, u + 1)
                    if h == 0:
                        nc.vector.tensor_scalar(score[:, i, 0:w], relu[:, u % 2, 0:w], weight, None, ALU.mult).then_inc(added, 1)
                    else:
                        dve.wait_ge(added, u)
                        nc.vector.scalar_tensor_tensor(score[:, i, 0:w], relu[:, u % 2, 0:w], weight, score[:, i, 0:w],
                                                       ALU.mult, ALU.add).then_inc(added, 1)
                dve.wait_ge(added, len(units))
                for i in range(1, TT):
                    part = score[:, i, P * i:P * (i + 1)]
                    step(nc.vector.scalar_tensor_tensor(part, k.causal[:, SEQ - P:SEQ], FILL / MASKED, part, ALU.mult, ALU.add))
                for _round in range(TOPK // 8):
                    for i in range(1, TT):
                        step(nc.vector.max(top[:, i], score[:, i, 0:P * (i + 1)]))
                    for i in range(1, TT):
                        step(nc.vector.match_replace(score[:, i, 0:P * (i + 1)], top[:, i], score[:, i, 0:P * (i + 1)], TAKEN))
                nc.vector.tensor_copy(k.chosen[:, 0, 0:P], k.causal[:, SEQ - P:SEQ])
                for i in range(1, TT):
                    w = P * (i + 1)
                    nc.vector.tensor_scalar(k.chosen[:, i, 0:w], score[:, i, 0:w], TAKEN_BELOW, MASKED, ALU.is_gt, ALU.mult)


def attention_stage(k):
    nc = k.nc
    scored, masked, exped, turned, turned_copied, weighed, out_copied = (
        k.sem(f"attn_{s}") for s in ("scored", "masked", "exped", "turned", "turned_copied", "weighed", "out_copied"))
    units = [(a, i, h) for i in range(TT) for a in range(2) for h in range(HEADS)]
    n = len(units)
    with ExitStack() as scope:
        def sb(name, shape):
            return scope.enter_context(nc.sbuf_tensor(name, shape, F32))

        logits, probs, probs_t = sb("attn_logits", [P, 2, SEQ]), sb("attn_probs", [P, 2, SEQ]), sb("attn_probs_t", [P, 2, SEQ])
        neg_max, total, inv = sb("attn_neg_max", [P, n]), sb("attn_total", [P, n]), sb("attn_inv", [P, n])
        with nc.Block(no_gpsimd_drain=True) as block:
            @block.tensor
            def _(pe):
                def score(u):
                    a, i, h = units[u]
                    w = P * (i + 1)
                    if u >= 2:
                        pe.wait_ge(masked, u - 1)
                    if a == 0:
                        q, key, half, rows = AQ + h % 4, AK, h // 4, k.slope_pos[:, SEQ - w:SEQ]
                    else:
                        q, key, half, rows = BQ + h // 2, BK + h // 2, h % 2, k.neg_cum[:, 0:w]
                    out = k.psum[:, u % 2, 0:w]
                    nc.tensor.matmul(out, head_half(k.proj[:, q, i * P:(i + 1) * P], half), head_half(k.proj[:, key, 0:w], half),
                                     start=True, stop=False)
                    nc.tensor.matmul(out, k.head_rows[:, h], rows, start=False, stop=True).then_inc(scored, 1)

                def turn(u):
                    i = units[u][1]
                    pe.wait_ge(exped, u + 1)
                    if u >= 2:
                        pe.wait_ge(turned_copied, u - 1)
                    for s in range(i + 1):
                        mm = nc.tensor.transpose(k.psum[:, 2 + u % 2, s * P:(s + 1) * P], probs[:, u % 2, s * P:(s + 1) * P],
                                                 k.ident[:])
                    mm.then_inc(turned, 1)

                def weigh(u):
                    a, i, h = units[u]
                    pe.wait_ge(turned_copied, u + 1)
                    if u >= 2:
                        pe.wait_ge(out_copied, u - 1)
                    for s in range(i + 1):
                        v = k.small[:, s, (h // 4) * DH:(h // 4 + 1) * DH] if a == 0 else k.v_b[:, s, h * DH:(h + 1) * DH]
                        mm = nc.tensor.matmul(k.psum[:, 4 + u % 2, 0:DH], probs_t[:, u % 2, s * P:(s + 1) * P], v,
                                              start=s == 0, stop=s == i)
                    mm.then_inc(weighed, 1)

                for t in range(n + 2):
                    if t < n:
                        score(t)
                    if 1 <= t <= n:
                        turn(t - 1)
                    if t >= 2:
                        weigh(t - 2)

            @block.vector
            def _(dve):
                def mask(u):
                    a, i, _h = units[u]
                    w = P * (i + 1)
                    dve.wait_ge(scored, u + 1)
                    if u >= 2:
                        dve.wait_ge(exped, u - 1)
                    mask_rows = k.chosen[:, i, 0:w] if a == 0 else k.causal[:, SEQ - w:SEQ]
                    k.vstep(nc.vector.tensor_tensor(logits[:, u % 2, 0:w], k.psum[:, u % 2, 0:w], mask_rows, ALU.add))
                    nc.vector.tensor_reduce(neg_max[:, u:u + 1], logits[:, u % 2, 0:w], AX.X, ALU.max, negate=True).then_inc(
                        masked, 1)

                def normalise(u):
                    a, i, h = units[u]
                    dve.wait_ge(exped, u + 1)
                    k.vstep(nc.vector.reciprocal(inv[:, u:u + 1], total[:, u:u + 1]))
                    dve.wait_ge(weighed, u + 1)
                    at = a * HEADS * DH + h * DH
                    nc.vector.tensor_scalar(k.o[:, i, at:at + DH], k.psum[:, 4 + u % 2, 0:DH], inv[:, u:u + 1], None,
                                            ALU.mult).then_inc(out_copied, 1)

                for t in range(n + 2):
                    if t < n:
                        mask(t)
                    if t >= 2:
                        normalise(t - 2)

            @block.scalar
            def _(act):
                def exp(u):
                    w = P * (units[u][1] + 1)
                    act.wait_ge(masked, u + 1)
                    if u >= 2:
                        act.wait_ge(turned, u - 1)
                    nc.scalar.activation(probs[:, u % 2, 0:w], logits[:, u % 2, 0:w], ACT.Exp, bias=neg_max[:, u:u + 1],
                                         accum_out=total[:, u:u + 1]).then_inc(exped, 1)

                def copy_turned(u):
                    w = P * (units[u][1] + 1)
                    act.wait_ge(turned, u + 1)
                    if u >= 2:
                        act.wait_ge(weighed, u - 1)
                    nc.scalar.activation(probs_t[:, u % 2, 0:w], k.psum[:, 2 + u % 2, 0:w], ACT.Copy).then_inc(turned_copied, 1)

                for t in range(n + 1):
                    if t < n:
                        exp(t)
                    if t >= 1:
                        copy_turned(t - 1)


def head_norm_stage(k, name, groups, gain, gain_scale=1.0):
    nc = k.nc
    std_ready, scaled, turned, copied, rooted = (k.sem(f"{name}_{s}") for s in ("std", "scaled", "turned", "copied", "rooted"))
    width = D // groups
    with ExitStack() as scope:
        square = scope.enter_context(nc.sbuf_tensor(f"{name}_square", [P, D], F32))
        total = scope.enter_context(nc.sbuf_tensor(f"{name}_total", [P, TT, groups], F32))
        rstd = scope.enter_context(nc.sbuf_tensor(f"{name}_rstd", [P, TT, groups], F32))
        gains = scope.enter_context(nc.sbuf_tensor(f"{name}_gains", [P, KC], F32))
        with nc.Block(no_gpsimd_drain=True) as block:
            @block.vector
            def _(dve):
                step = k.vstep
                step(nc.vector.tensor_scalar(gains[:], gain, gain_scale, None, ALU.mult))
                for t in range(TT):
                    step(nc.vector.tensor_tensor(square[:], k.o[:, t], k.o[:, t], ALU.mult))
                    step(nc.vector.tensor_reduce(total[:, t], square[:].rearrange("p (g n) -> p g n", g=groups), AX.X, ALU.add))
                nc.vector.tensor_scalar(total[:], total[:], 1.0 / width, EPS, ALU.mult, ALU.add).then_inc(std_ready, 1)
                dve.wait_ge(rooted, 1)
                step(nc.vector.reciprocal(rstd[:], total[:]))
                for t in range(TT):
                    rows = k.o[:, t].rearrange("p (g n) -> p g n", g=groups)
                    nc.vector.tensor_tensor(rows, rows, rstd[:, t].unsqueeze(2).broadcast_to([P, groups, width]),
                                            ALU.mult).then_inc(scaled, 1)

            @block.tensor
            def _(pe):
                pe.wait_ge(scaled, TT)
                for c in range(KC):
                    if c >= 4:
                        pe.wait_ge(copied, c - 3)
                    for t in range(TT):
                        mm = nc.tensor.transpose(k.psum[:, c % 4, t * P:(t + 1) * P], k.o[:, t, c * P:(c + 1) * P], k.ident[:])
                    mm.then_inc(turned, 1)

            @block.scalar
            def _(act):
                act.wait_ge(std_ready, 1)
                nc.scalar.activation(total[:], total[:], ACT.Sqrt).then_inc(rooted, 1)
                for c in range(KC):
                    act.wait_ge(turned, c + 1)
                    nc.scalar.activation(k.h[:, c], k.psum[:, c % 4], ACT.Copy, scale=gains[:, c:c + 1]).then_inc(copied, 1)


def out_projection_stage(k):
    nc = k.nc
    done, added = k.sem("out1_done"), k.sem("out1_added")
    first = FIRST["out1"]
    with nc.Block(no_gpsimd_drain=True) as block:
        @block.sync
        def _(sp):
            stream(k, sp, first, COUNT["out1"], done, lambda n: 2 * (n + 1))

        @block.tensor
        def _(pe):
            for c in range(KC):
                if c >= 4:
                    pe.wait_ge(added, c - 3)
                chunk_products(k, pe, k.psum[:, c % 4], first, c, k.h, done)

        @block.vector
        def _(dve):
            for c in range(KC):
                dve.wait_ge(done, c + 1)
                nc.vector.scalar_tensor_tensor(k.x[:, c], k.psum[:, c % 4], k.mod1[:, GATE_1 + c:GATE_1 + c + 1], k.x[:, c],
                                               ALU.mult, ALU.add).then_inc(added, 1)


def first_of_largest(k, sb, name, values, n, prio):
    nc, step = k.nc, k.vstep
    shape = [P, TT, n]
    top, less, mark, best, hot = (sb(f"{name}_{s}", [P, TT] if s in ("top", "best") else shape) for s in
                                  ("top", "less", "mark", "best", "hot"))
    step(nc.vector.tensor_reduce(top[:], values, AX.X, ALU.max))
    step(nc.vector.tensor_tensor(less[:], values, top[:].unsqueeze(2).broadcast_to(shape), ALU.subtract))
    step(nc.vector.tensor_scalar(mark[:], less[:], 0.0, None, ALU.is_equal))
    step(nc.vector.tensor_tensor(mark[:], mark[:], prio[:, 0:n].unsqueeze(1).broadcast_to(shape), ALU.mult))
    step(nc.vector.tensor_reduce(best[:], mark[:], AX.X, ALU.max))
    step(nc.vector.tensor_tensor(hot[:], mark[:], best[:].unsqueeze(2).broadcast_to(shape), ALU.is_equal))
    return top, less, hot


def router_stage(k):
    nc = k.nc
    loaded, routed, at_vector, at_scalar, turned, copied, stored = (
        k.sem(f"route_{s}") for s in ("loaded", "routed", "vector", "scalar", "turned", "copied", "stored"))
    n = GROUPS + EXPERTS
    with ExitStack() as scope:
        def sb(name, shape):
            return scope.enter_context(nc.sbuf_tensor(name, shape, F32))

        w_route, b_route, prio = sb("w_route", [P, KC, n]), sb("b_route", [P, n]), sb("prio", [P, PER_GROUP])
        logits, picked = sb("route_logits", [P, TT, n]), sb("route_picked", [P, TT, GROUPS, PER_GROUP])
        expert, second = sb("route_expert", [P, TT, PER_GROUP]), sb("route_second", [P, TT, PER_GROUP])
        exp_group, group_sum, p_group = sb("exp_group", [P, TT, GROUPS]), sb("group_sum", [P, TT]), sb("p_group", [P, TT])
        delta, w_first, w_second = sb("route_delta", [P, TT]), sb("w_first", [P, TT]), sb("w_second", [P, TT])
        h_rows = sb("h_rows", [P, TT, D])
        with nc.Block(no_gpsimd_drain=True) as block:
            @block.sync
            def _(sp):
                sp.dma_start(w_route[:], k.d["w_route"]).then_inc(loaded, 16)
                sp.dma_start(b_route[:], k.d["b_route"][0].partition_broadcast(P)).then_inc(loaded, 16)
                sp.dma_start(prio[:], k.d["prio"]).then_inc(loaded, 16)
                sp.wait_ge(copied, 2 * TT)
                sp.dma_start(k.h_dram.rearrange("(t p) d -> p t d", p=P), h_rows[:]).then_inc(stored, 16)
                sp.wait_ge(stored, 16)

            @block.tensor
            def _(pe):
                pe.wait_ge(loaded, 48)
                for t in range(TT):
                    for kc in range(KC):
                        mm = nc.tensor.matmul(k.psum[:, 0, t * n:(t + 1) * n], k.h[:, kc, t * P:(t + 1) * P], w_route[:, kc],
                                              start=kc == 0, stop=kc == KC - 1)
                mm.then_inc(routed, 1)
                for half in range(2 * TT):
                    if half >= 4:
                        pe.wait_ge(copied, half - 3)
                    for c in range(KC // 2):
                        mm = nc.tensor.transpose(k.psum[:, 1 + half % 4, c * P:(c + 1) * P],
                                                 k.h[:, (half % 2) * (KC // 2) + c, (half // 2) * P:(half // 2 + 1) * P], k.ident[:])
                    mm.then_inc(turned, 1)

            @block.scalar
            def _(act):
                act.wait_ge(at_vector, 1)
                nc.scalar.activation(exp_group[:], k.route_less[:], ACT.Exp).then_inc(at_scalar, 1)
                act.wait_ge(at_vector, 2)
                nc.scalar.activation(w_second[:], delta[:], ACT.Exp).then_inc(at_scalar, 1)
                for half in range(2 * TT):
                    act.wait_ge(turned, half + 1)
                    nc.scalar.activation(h_rows[:, half // 2, (half % 2) * BANK:(half % 2 + 1) * BANK], k.psum[:, 1 + half % 4], ACT.Copy).then_inc(
                        copied, 1)

            @block.vector
            def _(dve):
                step = k.vstep
                dve.wait_ge(loaded, 48)
                dve.wait_ge(routed, 1)
                step(nc.vector.tensor_tensor(logits[:], k.psum[:, 0, 0:TT * n].rearrange("p (t n) -> p t n", n=n),
                                             b_route[:].unsqueeze(1).broadcast_to([P, TT, n]), ALU.add))
                _top, less, group = first_of_largest(k, sb, "group", logits[:, :, 0:GROUPS], GROUPS, prio)
                nc.vector.tensor_copy(k.route_less[:], less[:]).then_inc(at_vector, 1)
                for g in range(GROUPS):
                    step(nc.vector.tensor_tensor(picked[:, :, g], logits[:, :, GROUPS + g * PER_GROUP:GROUPS + (g + 1) * PER_GROUP],
                                                 group[:, :, g:g + 1].broadcast_to([P, TT, PER_GROUP]), ALU.mult))
                step(nc.vector.tensor_reduce(expert[:], picked[:].rearrange("p t g e -> p t e g"), AX.X, ALU.add))
                top1, _less1, hot1 = first_of_largest(k, sb, "best1", expert[:], PER_GROUP, prio)
                step(nc.vector.scalar_tensor_tensor(second[:], hot1[:], MASKED, expert[:], ALU.mult, ALU.add))
                top2, _less2, hot2 = first_of_largest(k, sb, "best2", second[:], PER_GROUP, prio)
                nc.vector.tensor_tensor(delta[:], top2[:], top1[:], ALU.subtract).then_inc(at_vector, 1)
                dve.wait_ge(at_scalar, 2)
                step(nc.vector.tensor_reduce(group_sum[:], exp_group[:], AX.X, ALU.add))
                step(nc.vector.reciprocal(p_group[:], group_sum[:]))
                step(nc.vector.tensor_scalar(w_first[:], w_second[:], 1.0, None, ALU.add))
                step(nc.vector.reciprocal(w_first[:], w_first[:]))
                step(nc.vector.tensor_tensor(k.pick_weight[:, 0], w_first[:], p_group[:], ALU.mult))
                step(nc.vector.tensor_tensor(k.pick_weight[:, 1], w_second[:], k.pick_weight[:, 0], ALU.mult))
                for choice, hot in enumerate((hot1, hot2)):
                    for g in range(GROUPS):
                        step(nc.vector.tensor_tensor(k.pick[:, choice, :, g * PER_GROUP:(g + 1) * PER_GROUP], hot[:],
                                                     group[:, :, g:g + 1].broadcast_to([P, TT, PER_GROUP]), ALU.mult))


def plan_stage(k):
    nc = k.nc
    loaded, picks_ready, counted, slots_ready, zeroed, cleared, scattered = (
        k.sem(f"plan_{s}") for s in ("loaded", "picks_ready", "counted", "slots_ready", "zeroed", "cleared", "scattered"))
    T, E = EXPERT_TILES, EXPERTS
    PAD = E // 2
    with ExitStack() as scope:
        def sb(name, shape, kind=F32):
            return scope.enter_context(nc.sbuf_tensor(name, shape, kind))

        before, iota, token = sb("before", [P, P]), sb("tile_iota", [P, P]), sb("token", [P, TT])
        both, ranked, based = sb("both_picks", [P, TT, E]), sb("ranked", [P, 2, TT, E]), sb("based", [P, 2, TT, E])
        count, tiles, base = sb("expert_count", [P, E]), sb("expert_tiles", [P, E]), sb("expert_base", [P, E])
        sums = [sb(f"tile_sums{i}", [P, PAD + E]) for i in range(2)]
        passed, owner = sb("passed", [P, T, E]), sb("tile_owner", [P, T])
        rank, first, carry, slot_f = (sb(n, [P, 2, TT]) for n in ("pick_rank", "pick_base", "pick_carry", "pick_slot_f"))
        token_u, place_u, zero = sb("token_u", [P, TT], U32), sb("pick_place", [P, 2, TT], U32), sb("no_token", [P, T], U32)
        with nc.Block(no_gpsimd_drain=True) as block:
            @block.sync
            def _(sp):
                for part, name in ((before, "before"), (iota, "iota"), (token, "token")):
                    sp.dma_start(part[:], k.d[name]).then_inc(loaded, 16)
                sp.wait_ge(zeroed, 1)
                sp.dma_start(k.token_dram.rearrange("(p t) o -> p (t o)", p=P), zero[:]).then_inc(cleared, 16)
                sp.wait_ge(scattered, 16 * 2 * TT)
                sp.dma_start(k.slot_token[:], k.token_dram.rearrange("(p t) o -> p (t o)", p=P)).then_inc(loaded, 16)
                sp.wait_ge(loaded, 64)

            @block.gpsimd
            def _(pool):
                pool.wait_ge(cleared, 16)
                pool.wait_ge(slots_ready, 1)
                for choice in range(2):
                    for t in range(TT):
                        pool.indirect_dma_start(k.token_dram, bass.IndirectOffsetOnAxis(ap=place_u[:, choice, t:t + 1], axis=0),
                                                token_u[:, t:t + 1], None).then_inc(scattered, 16)
                pool.wait_ge(scattered, 16 * 2 * TT)

            @block.tensor
            def _(pe):
                pe.wait_ge(loaded, 48)
                pe.wait_ge(picks_ready, 1)
                for t in range(TT):
                    for i in range(t + 1):
                        nc.tensor.matmul(k.psum[:, 0, t * E:(t + 1) * E], k.ones[:] if i < t else before[:], both[:, i],
                                         start=i == 0, stop=i == t)
                for i in range(TT):
                    mm = nc.tensor.matmul(k.psum[:, 1, 0:E], k.ones[:], both[:, i], start=i == 0, stop=i == TT - 1)
                mm.then_inc(counted, 1)

            @block.vector
            def _(dve):
                step = k.vstep
                nc.vector.memset(zero[:], 0).then_inc(zeroed, 1)
                nc.vector.tensor_tensor(both[:], k.pick[:, 0], k.pick[:, 1], ALU.add).then_inc(picks_ready, 1)
                for part in sums:
                    step(nc.vector.memset(part[:, 0:PAD], 0.0))
                dve.wait_ge(loaded, 48)
                step(nc.vector.tensor_copy(token_u[:], token[:]))
                dve.wait_ge(counted, 1)
                step(nc.vector.tensor_copy(count[:], k.psum[:, 1, 0:E]))
                step(nc.vector.tensor_scalar(tiles[:], count[:], 0.0, None, ALU.is_gt))
                for m in range(1, TT):
                    step(nc.vector.scalar_tensor_tensor(tiles[:], count[:], float(m * P), tiles[:], ALU.is_gt, ALU.add))
                step(nc.vector.tensor_copy(sums[0][:, PAD:], tiles[:]))
                shift, at = 1, 0
                while shift < E:
                    step(nc.vector.tensor_tensor(sums[1 - at][:, PAD:], sums[at][:, PAD:], sums[at][:, PAD - shift:PAD - shift + E], ALU.add))
                    shift, at = 2 * shift, 1 - at
                total = sums[at][:, PAD:]
                step(nc.vector.tensor_tensor(base[:], total, tiles[:], ALU.subtract))
                step(nc.vector.tensor_tensor(passed[:], total.unsqueeze(1).broadcast_to([P, T, E]),
                                             iota[:, 0:T].unsqueeze(2).broadcast_to([P, T, E]), ALU.is_le))
                step(nc.vector.tensor_reduce(owner[:], passed[:], AX.X, ALU.add))
                step(nc.vector.tensor_scalar(owner[:], owner[:], float(E - 1), float(P), ALU.min, ALU.mult))
                step(nc.vector.tensor_scalar(owner[:], owner[:], token[:, 0:1], None, ALU.add))
                step(nc.vector.tensor_copy(k.expert_row[:], owner[:]))
                ranks = k.psum[:, 0, 0:TT * E].rearrange("p (t e) -> p t e", e=E)
                for choice in range(2):
                    step(nc.vector.tensor_tensor(ranked[:, choice], k.pick[:, choice], ranks, ALU.mult))
                    step(nc.vector.tensor_tensor(based[:, choice], k.pick[:, choice], base[:].unsqueeze(1).broadcast_to([P, TT, E]),
                                                 ALU.mult))
                step(nc.vector.tensor_reduce(rank[:], ranked[:], AX.X, ALU.add))
                step(nc.vector.tensor_reduce(first[:], based[:], AX.X, ALU.add))
                step(nc.vector.scalar_tensor_tensor(slot_f[:], first[:], float(P), rank[:], ALU.mult, ALU.add))
                step(nc.vector.tensor_copy(k.pick_slot[:], slot_f[:]))
                step(nc.vector.tensor_scalar(carry[:], rank[:], float(P), None, ALU.is_ge))
                for m in range(2, TT):
                    step(nc.vector.scalar_tensor_tensor(carry[:], rank[:], float(m * P), carry[:], ALU.is_ge, ALU.add))
                step(nc.vector.scalar_tensor_tensor(rank[:], carry[:], float(-P), rank[:], ALU.mult, ALU.add))
                step(nc.vector.tensor_tensor(first[:], first[:], carry[:], ALU.add))
                step(nc.vector.scalar_tensor_tensor(slot_f[:], rank[:], float(T), first[:], ALU.mult, ALU.add))
                nc.vector.tensor_copy(place_u[:], slot_f[:]).then_inc(slots_ready, 1)


def moe_stage(k):
    nc = k.nc
    x_turned, x_ready, in_done, silu_done, a_ready, a_turned, at_ready, down_done, y_ready = (
        k.sem(f"moe_{s}") for s in ("x_turned", "x_ready", "in_done", "silu_done", "a_ready", "a_turned", "at_ready", "down_done", "y_ready"))
    x_loaded, in_loaded, down_loaded, y_stored = (
        [k.sem(f"moe_{s}{i}") for i in range(2)] for s in ("x_loaded", "in_loaded", "down_loaded", "y_stored"))
    T = EXPERT_TILES
    loops = (T - 3) // 2
    with ExitStack() as scope:
        def sb(name, shape):
            return scope.enter_context(nc.sbuf_tensor(name, shape, F32))

        w_in, w_down = sb("w_expert_in", [P, 2, KC, 2 * FF]), sb("w_expert_down", [P, 2, 2, D])
        x_rows, x_turn = sb("x_rows", [P, 2, D]), sb("x_turn", [P, 2, KC, P])
        silu, a, a_turn, y_rows = sb("moe_silu", [P, 2, FF]), sb("moe_a", [P, 2, FF]), sb("a_turn", [P, 2, P]), sb("y_rows", [P, 2, D])
        x_banks, in_banks, a_bank, y_banks = (0, 1), (2, 3), 4, (5, 6)
        with nc.Block(no_gpsimd_drain=True) as block:
            @block.gpsimd
            def _(pool):
                def gather(out, table, rows, m, done):
                    pool.indirect_dma_start(out, None, table, bass.IndirectOffsetOnAxis(ap=rows[:, m:m + 1], axis=0)).then_inc(done, 16)

                def tokens(m):
                    if m >= 2:
                        pool.wait_ge(x_turned, m - 1)
                    gather(x_rows[:, m % 2], k.h_dram, k.slot_token, m, x_loaded[m % 2])

                def gate_up(m):
                    if m >= 2:
                        pool.wait_ge(in_done, m - 1)
                    gather(w_in[:, m % 2].rearrange("p c n -> p (c n)"), k.d["experts_in"], k.expert_row, m, in_loaded[m % 2])

                def down(m):
                    if m >= 2:
                        pool.wait_ge(down_done, m - 1)
                    gather(w_down[:, m % 2].rearrange("p c n -> p (c n)"), k.d["experts_down"], k.expert_row, m, down_loaded[m % 2])

                tokens(0)
                gate_up(0)
                for m in range(1, T):
                    tokens(m)
                    gate_up(m)
                    down(m - 1)
                down(T - 1)

            @block.tensor
            def _(pe):
                def turn_x(m, r):
                    pe.wait_ge(x_loaded[r % 2], turns(m, r))
                    if r > 0:
                        pe.wait_ge(x_ready, m)
                    for c in range(KC):
                        at = (c % 4) * P
                        mm = nc.tensor.transpose(k.psum[:, x_banks[c // 4], at:at + P], x_rows[:, r % 2, c * P:(c + 1) * P], k.ident[:])
                    mm.then_inc(x_turned, 1)

                def gate_up(m, r):
                    pe.wait_ge(x_ready, m + 1)
                    pe.wait_ge(in_loaded[r % 2], turns(m, r))
                    if r >= 2:
                        pe.wait_ge(a_ready, m - 1)
                    for c in range(KC):
                        mm = nc.tensor.matmul(k.psum[:, in_banks[r % 2]], x_turn[:, r % 2, c], w_in[:, r % 2, c], start=c == 0, stop=c == KC - 1)
                    mm.then_inc(in_done, 1)

                def turn_a(n, r):
                    pe.wait_ge(a_ready, n + 1)
                    if r > 0:
                        pe.wait_ge(at_ready, n)
                    for c in range(2):
                        mm = nc.tensor.transpose(k.psum[:, a_bank, c * P:(c + 1) * P], a[:, r % 2, c * P:(c + 1) * P], k.ident[:])
                    mm.then_inc(a_turned, 1)

                def down(n, r):
                    pe.wait_ge(at_ready, n + 1)
                    pe.wait_ge(down_loaded[r % 2], turns(n, r))
                    if r > 0:
                        pe.wait_ge(y_ready, n)
                    for half, bank in enumerate(y_banks):
                        for c in range(2):
                            mm = nc.tensor.matmul(k.psum[:, bank], a_turn[:, c], w_down[:, r % 2, c, half * BANK:(half + 1) * BANK],
                                                  start=c == 0, stop=c == 1)
                    mm.then_inc(down_done, 1)

                def step(n, r):
                    if r + 1 < T:
                        gate_up(n + 1, r + 1)
                    turn_a(n, r)
                    if r + 2 < T:
                        turn_x(n + 2, r + 2)
                    down(n, r)

                turn_x(0, 0)
                turn_x(1, 1)
                gate_up(0, 0)
                step(0, 0)
                with pe.Fori(0, loops) as g:
                    for r in (1, 2):
                        step(2 * g + r, r)
                for n in range(2 * loops + 1, T):
                    step(n, n)

            @block.scalar
            def _(act):
                def copy_x(m, r):
                    act.wait_ge(x_turned, m + 1)
                    if r >= 2:
                        act.wait_ge(in_done, m - 1)
                    for i in range(2):
                        ins = nc.scalar.activation(x_turn[:, r % 2, 4 * i:4 * i + 4].rearrange("p c n -> p (c n)"), k.psum[:, x_banks[i]], ACT.Copy)
                    ins.then_inc(x_ready, 1)

                def gate(m, r):
                    act.wait_ge(in_done, m + 1)
                    if r >= 2:
                        act.wait_ge(a_ready, m - 1)
                    nc.scalar.activation(silu[:, r % 2], k.psum[:, in_banks[r % 2], 0:FF], ACT.Silu).then_inc(silu_done, 1)

                def step(n, r):
                    if r + 1 < T:
                        gate(n + 1, r + 1)
                    act.wait_ge(a_turned, n + 1)
                    if r > 0:
                        act.wait_ge(down_done, n)
                    nc.scalar.activation(a_turn[:].rearrange("p c n -> p (c n)"), k.psum[:, a_bank, 0:FF], ACT.Copy).then_inc(at_ready, 1)
                    if r + 2 < T:
                        copy_x(n + 2, r + 2)

                copy_x(0, 0)
                copy_x(1, 1)
                gate(0, 0)
                step(0, 0)
                with act.Fori(0, loops) as g:
                    for r in (1, 2):
                        step(2 * g + r, r)
                for n in range(2 * loops + 1, T):
                    step(n, n)

            @block.vector
            def _(dve):
                def up(m, r):
                    dve.wait_ge(silu_done, m + 1)
                    if r >= 2:
                        dve.wait_ge(a_turned, m - 1)
                    nc.vector.tensor_tensor(a[:, r % 2], silu[:, r % 2], k.psum[:, in_banks[r % 2], FF:2 * FF], ALU.mult).then_inc(a_ready, 1)

                def step(n, r):
                    if r + 1 < T:
                        up(n + 1, r + 1)
                    dve.wait_ge(down_done, n + 1)
                    if r >= 2:
                        dve.wait_ge(y_stored[r % 2], turns(n, r) - 16)
                    for half, bank in enumerate(y_banks):
                        ins = nc.vector.tensor_copy(y_rows[:, r % 2, half * BANK:(half + 1) * BANK], k.psum[:, bank])
                    ins.then_inc(y_ready, 1)

                up(0, 0)
                step(0, 0)
                step(1, 1)
                step(2, 2)
                with dve.Fori(1, loops) as g:
                    for r in (1, 2):
                        step(2 * g + r, r + 2)
                for n in range(2 * loops + 1, T):
                    step(n, n)

            @block.sync
            def _(sp):
                def store(n, r):
                    sp.wait_ge(y_ready, n + 1)
                    sp.dma_start(k.y_dram.rearrange("(n p) d -> n p d", p=P)[bass.ds(n, 1)].rearrange("n p d -> p (n d)"),
                                 y_rows[:, r % 2]).then_inc(y_stored[r % 2], 16)

                with sp.Fori(0, T // 2) as g:
                    for r in range(2):
                        store(2 * g + r, r)
                if T % 2:
                    store(T - 1, T - 1)
                for i in range(2):
                    sp.wait_ge(y_stored[i], 16 * ((T + 1 - i) // 2))


def turns(n, r):
    return (n - r % 2) * 8 + 16


def moe_out_stage(k):
    nc = k.nc
    summed, turned, added = (k.sem(f"moe_out_{s}") for s in ("summed", "turned", "added"))
    got = [k.sem(f"moe_out_got{i}") for i in range(2)]
    gate = k.mod1[:, GATE_2:GATE_2 + KC]
    with ExitStack() as scope:
        picked, y_sum = (scope.enter_context(nc.sbuf_tensor(n, shape, F32)) for n, shape in (
            ("picked_rows", [P, 2, 2, D]), ("y_sum", [P, 2, D])))
        with nc.Block(no_gpsimd_drain=True) as block:
            @block.gpsimd
            def _(pool):
                for t in range(TT):
                    if t >= 2:
                        pool.wait_ge(summed, t - 1)
                    for choice in range(2):
                        pool.indirect_dma_start(picked[:, t % 2, choice], None, k.y_dram, bass.IndirectOffsetOnAxis(
                            ap=k.pick_slot[:, choice, t:t + 1], axis=0)).then_inc(got[t % 2], 16)

            @block.vector
            def _(dve):
                def add(t):
                    for c in range(KC):
                        dve.wait_ge(turned, 2 * t + c // 4 + 1)
                        part = k.x[:, c, t * P:(t + 1) * P]
                        nc.vector.scalar_tensor_tensor(part, k.psum[:, 2 * (t % 2) + c // 4, (c % 4) * P:(c % 4 + 1) * P], gate[:, c:c + 1],
                                                       part, ALU.mult, ALU.add).then_inc(added, 1)

                for t in range(TT):
                    dve.wait_ge(got[t % 2], 32 * (t // 2 + 1))
                    if t >= 2:
                        dve.wait_ge(turned, 2 * (t - 1))
                    k.vstep(nc.vector.tensor_scalar(y_sum[:, t % 2], picked[:, t % 2, 0], k.pick_weight[:, 0, t:t + 1], None, ALU.mult))
                    nc.vector.scalar_tensor_tensor(y_sum[:, t % 2], picked[:, t % 2, 1], k.pick_weight[:, 1, t:t + 1], y_sum[:, t % 2],
                                                   ALU.mult, ALU.add).then_inc(summed, 1)
                    if t > 0:
                        add(t - 1)
                add(TT - 1)

            @block.tensor
            def _(pe):
                for t in range(TT):
                    pe.wait_ge(summed, t + 1)
                    if t >= 2:
                        pe.wait_ge(added, KC * (t - 1))
                    for c in range(KC):
                        mm = nc.tensor.transpose(k.psum[:, 2 * (t % 2) + c // 4, (c % 4) * P:(c % 4 + 1) * P],
                                                 y_sum[:, t % 2, c * P:(c + 1) * P], k.ident[:])
                        if c % 4 == 3:
                            mm.then_inc(turned, 1)


def load_context_stage(k):
    nc = k.nc
    loaded = k.sem("context_loaded")
    with nc.Block(no_gpsimd_drain=True) as block:
        @block.sync
        def _(sp):
            sp.dma_start(k.h_ctx[:], k.d["ctx"]).then_inc(loaded, 16)
            sp.dma_start(k.rope[:], k.d["rope"]).then_inc(loaded, 16)
            sp.dma_start(k.swap[:], k.d["swap"]).then_inc(loaded, 16)
            sp.wait_ge(loaded, 48)


def qk_stage(k):
    nc = k.nc
    done, copied, swapped, rotated, ctx_done, ctx_copied = (
        k.sem(f"qk_{s}") for s in ("done", "copied", "swapped", "rotated", "ctx_done", "ctx_copied"))
    first = FIRST["qk2"]
    n = 2 * KC
    with ExitStack() as scope:
        raw = scope.enter_context(nc.sbuf_tensor("qk_raw", [P, 2, SEQ], F32))
        with_cos = scope.enter_context(nc.sbuf_tensor("qk_with_cos", [P, 2, SEQ], F32))
        with_sin = scope.enter_context(nc.sbuf_tensor("qk_with_sin", [P, 2, SEQ], F32))

        with nc.Block(no_gpsimd_drain=True) as block:
            @block.sync
            def _(sp):
                stream(k, sp, first, KC // 2, done, lambda i: 2 * (i + 1))
                stream(k, sp, first + KC // 2, KC // 2, ctx_done, lambda i: 2 * (i + 1))

            @block.tensor
            def _(pe):
                def swap(c):
                    pe.wait_ge(copied, c + 1)
                    if c >= 2:
                        pe.wait_ge(rotated, c - 1)
                    nc.tensor.matmul(k.psum[:, 2 + c % 2], k.swap[:], raw[:, c % 2], start=True, stop=True).then_inc(swapped, 1)

                for c in range(n):
                    if c >= 2:
                        pe.wait_ge(copied, c - 1)
                    chunk_products(k, pe, k.psum[:, c % 2], first, c, k.h, done)
                    if c >= KC:
                        i = c - KC
                        if i >= 2:
                            pe.wait_ge(ctx_copied, i - 1)
                        chunk_products_again(k, pe, k.psum[:, 4 + i % 2, 0:CTX], first, c, k.h_ctx, ctx_done)
                    if c >= 1:
                        swap(c - 1)
                swap(n - 1)

            @block.scalar
            def _(act):
                for c in range(n):
                    act.wait_ge(done, c + 1)
                    if c >= 2:
                        act.wait_ge(swapped, c - 1)
                        act.wait_ge(rotated, c - 1)
                    nc.scalar.activation(raw[:, c % 2], k.psum[:, c % 2], ACT.Copy, scale=DH ** -0.5 if c < KC else 1.0).then_inc(
                        copied, 1)
                    if c >= KC:
                        i = c - KC
                        act.wait_ge(ctx_done, i + 1)
                        nc.scalar.activation(k.k2[:, i, 0:CTX], k.psum[:, 4 + i % 2, 0:CTX], ACT.Copy).then_inc(ctx_copied, 1)

            @block.vector
            def _(dve):
                for c in range(n):
                    target = k.q2[:, c] if c < KC else k.k2[:, c - KC, CTX:KEYS]
                    dve.wait_ge(copied, c + 1)
                    nc.vector.tensor_tensor(with_cos[:, c % 2], raw[:, c % 2], k.rope[:, 0], ALU.mult)
                    dve.wait_ge(swapped, c + 1)
                    k.vstep(nc.vector.tensor_tensor(with_sin[:, c % 2], k.psum[:, 2 + c % 2], k.rope[:, 1], ALU.mult))
                    nc.vector.tensor_tensor(target, with_cos[:, c % 2], with_sin[:, c % 2], ALU.add).then_inc(rotated, 1)


def chunk_products_again(k, pe, out, tiles, c, source, done):
    n = tiles + c // 2
    for kc in range(KC):
        at = ((c % 2) * KC + kc) * P
        mm = k.nc.tensor.matmul(out, slot(k, n)[:, at:at + P], source[:, kc], start=kc == 0, stop=kc == KC - 1)
    mm.then_inc(done, 1)


def values_stage(k):
    nc = k.nc
    done, copied = k.sem("v2_done"), k.sem("v2_copied")
    first = FIRST["v2"]
    with nc.Block(no_gpsimd_drain=True) as block:
        @block.sync
        def _(sp):
            stream(k, sp, first, 4, done, lambda n: KT * (n // 2 + 1))

        @block.tensor
        def _(pe):
            for half in range(2):
                for i in range(2):
                    wait_tile(k, pe, first + 2 * half + i)
                for t in range(KT):
                    u = half * KT + t
                    if u >= 4:
                        pe.wait_ge(copied, u - 3)
                    c = CTX // P
                    row_products(k, pe, k.psum[:, u % 4], first + 2 * half,
                                 lambda kc: k.h_ctx[:, kc, t * P:(t + 1) * P] if t < c else k.h[:, kc, (t - c) * P:(t - c + 1) * P],
                                 done)

        @block.scalar
        def _(act):
            for u in range(2 * KT):
                act.wait_ge(done, u + 1)
                nc.scalar.activation(k.v2[:, u % KT, (u // KT) * BANK:(u // KT + 1) * BANK], k.psum[:, u % 4], ACT.Copy).then_inc(
                    copied, 1)


def sgu_projection_stage(k):
    nc = k.nc
    done, copied, rows_done = k.sem("z_done"), k.sem("z_copied"), k.sem("z_rows_done")
    first = FIRST["z2"]
    with nc.Block(no_gpsimd_drain=True) as block:
        @block.sync
        def _(sp):
            stream(k, sp, first, 4, done, lambda n: 2 * (n + 1))
            stream(k, sp, first + 4, 4, rows_done, lambda n: TT * (n // 2 + 1))

        @block.tensor
        def _(pe):
            for c in range(KC):
                if c >= 4:
                    pe.wait_ge(copied, c - 3)
                chunk_products(k, pe, k.psum[:, c % 4], first, c, k.h, done)
            for half in range(2):
                for i in range(2):
                    wait_tile(k, pe, first + 4 + 2 * half + i)
                for t in range(TT):
                    u = KC + half * TT + t
                    pe.wait_ge(copied, u - 3)
                    row_products(k, pe, k.psum[:, u % 4], first + 4 + 2 * half, lambda kc: k.h[:, kc, t * P:(t + 1) * P], rows_done)

        @block.scalar
        def _(act):
            for c in range(KC):
                act.wait_ge(done, c + 1)
                nc.scalar.activation(k.u[:, c], k.psum[:, c % 4], ACT.Gelu).then_inc(copied, 1)
            for u in range(2 * TT):
                act.wait_ge(rows_done, u + 1)
                nc.scalar.activation(k.vz[:, u % TT, (u // TT) * BANK:(u // TT + 1) * BANK], k.psum[:, (KC + u) % 4],
                                     ACT.Gelu).then_inc(copied, 1)


def sgu_stage(k):
    nc = k.nc
    loaded, normed, mixed, used, at_scalar = (k.sem(f"sgu_{s}") for s in ("loaded", "normed", "mixed", "used", "scalar"))
    with ExitStack() as scope:
        def sb(name, shape):
            return scope.enter_context(nc.sbuf_tensor(name, shape, F32))

        w_s, b_s = sb("sgu_w", [P, SGU_GROUPS, P]), sb("sgu_b", [P, SGU_GROUPS, P])
        ln = sb("sgu_ln", [P, 2, D])
        stats, moments = sb("sgu_stats", [P, TT, 2, 6]), sb("sgu_moments", [P, TT, 2])
        std, with_bias = sb("sgu_std", [P, TT]), sb("sgu_with_bias", [P, 2, SEQ])
        with nc.Block(no_gpsimd_drain=True) as block:
            @block.sync
            def _(sp):
                sp.dma_start(ln[:, 0], k.d["ln_g"][0].partition_broadcast(P)).then_inc(loaded, 16)
                sp.dma_start(ln[:, 1], k.d["ln_b"][0].partition_broadcast(P)).then_inc(loaded, 16)
                sp.dma_start(b_s[:].rearrange("p g n -> p (g n)"), k.d["sgu_b"][0].partition_broadcast(P)).then_inc(loaded, 16)
                sp.dma_start(w_s[:], k.d["sgu_w"]).then_inc(loaded, 16)

            @block.vector
            def _(dve):
                step = k.vstep
                for t in range(TT):
                    for i in range(2):
                        step(nc.vector.bn_stats(stats[:, t, i], k.vz[:, t, i * BANK:(i + 1) * BANK]))
                    step(nc.vector.bn_aggr(moments[:, t], stats[:, t].rearrange("p i n -> p (i n)")))
                nc.vector.tensor_copy(std[:], moments[:, :, 1]).then_inc(normed, 1)
                dve.wait_ge(at_scalar, 1)
                step(nc.vector.reciprocal(std[:], std[:]))
                dve.wait_ge(loaded, 64)
                for t in range(TT):
                    step(nc.vector.tensor_scalar(k.vz[:, t], k.vz[:, t], moments[:, t, 0:1], std[:, t:t + 1], ALU.subtract, ALU.mult))
                for t in range(TT):
                    step(nc.vector.tensor_tensor(k.vz[:, t], k.vz[:, t], ln[:, 0], ALU.mult))
                for t in range(TT):
                    nc.vector.tensor_tensor(k.vz[:, t], k.vz[:, t], ln[:, 1], ALU.add).then_inc(normed, 1)
                for g in range(SGU_GROUPS):
                    dve.wait_ge(mixed, g + 1)
                    part = with_bias[:, g % 2].rearrange("p (t n) -> p t n", t=TT)
                    k.vstep(nc.vector.tensor_tensor(part, k.psum[:, g % 4].rearrange("p (t n) -> p t n", t=TT),
                                                    b_s[:, g].unsqueeze(1).broadcast_to([P, TT, P]), ALU.add))
                    nc.vector.tensor_tensor(k.u[:, g], k.u[:, g], with_bias[:, g % 2], ALU.mult).then_inc(used, 1)

            @block.scalar
            def _(act):
                act.wait_ge(normed, 1)
                nc.scalar.activation(std[:], std[:], ACT.Sqrt, bias=k.eps[:, 1:2]).then_inc(at_scalar, 1)

            @block.tensor
            def _(pe):
                pe.wait_ge(loaded, 64)
                pe.wait_ge(normed, 1 + TT)
                for g in range(SGU_GROUPS):
                    if g >= 4:
                        pe.wait_ge(used, g - 3)
                    for t in range(TT):
                        mm = nc.tensor.matmul(k.psum[:, g % 4, t * P:(t + 1) * P], k.vz[:, t, g * P:(g + 1) * P], w_s[:, g],
                                              start=True, stop=True)
                    mm.then_inc(mixed, 1)


def diff_attention_stage(k):
    nc = k.nc
    scored, maxed, exped, mixed, turned, turned_copied, weighed, out_copied, lam_vector, lam_scalar, lam_dot = (
        k.sem(f"diff_{s}") for s in ("scored", "maxed", "exped", "mixed", "turned", "turned_copied", "weighed", "out_copied",
                                     "lam_vector", "lam_scalar", "lam_dot"))
    units = [(i, h) for i in range(TT) for h in range(DIFF_HEADS)]
    n = len(units)
    HALF_KEYS = KEYS // 2
    with ExitStack() as scope:
        def sb(name, shape):
            return scope.enter_context(nc.sbuf_tensor(name, shape, F32))

        probs, minus, probs_t = sb("diff_probs", [P, 2, 2, KEYS]), sb("diff_minus", [P, KEYS]), sb("diff_probs_t", [P, 2, KEYS])
        neg_max, total, inv = sb("diff_neg_max", [P, 2 * n]), sb("diff_total", [P, 2 * n]), sb("diff_inv", [P, 2 * n])
        lam_prod, lam_exp, neg_lam = sb("lam_prod", [P, 2]), sb("lam_exp", [P, 2]), sb("neg_lam", [P, 1])
        with nc.Block(no_gpsimd_drain=True) as block:
            @block.tensor
            def _(pe):
                def score(u, j):
                    i, h = units[u]
                    v = 2 * u + j
                    if v >= 2:
                        pe.wait_ge(exped, v - 1)
                    q = head_half(k.q2[:, h, i * P:(i + 1) * P], j)
                    nc.tensor.matmul(k.psum[:, 2 * j, :], q, head_half(k.k2[:, h, 0:BANK], j), start=True, stop=True)
                    nc.tensor.matmul(k.psum[:, 2 * j + 1, 0:KEYS - BANK], q, head_half(k.k2[:, h, BANK:KEYS], j), start=True,
                                     stop=True).then_inc(scored, 1)

                def turn(u):
                    pe.wait_ge(mixed, u + 1)
                    for half in range(2):
                        if u >= 1:
                            pe.wait_ge(turned_copied, 2 * u + half - 1)
                        for s in range(3):
                            at = half * HALF_KEYS + s * P
                            mm = nc.tensor.transpose(k.psum[:, 4 + half, s * P:(s + 1) * P], probs[:, u % 2, 0, at:at + P], k.ident[:])
                        mm.then_inc(turned, 1)

                def weigh(u):
                    h = units[u][1]
                    pe.wait_ge(turned_copied, 2 * u + 2)
                    if u >= 2:
                        pe.wait_ge(out_copied, u - 1)
                    for s in range(KT):
                        mm = nc.tensor.matmul(k.psum[:, 6 + u % 2, 0:P], probs_t[:, u % 2, s * P:(s + 1) * P],
                                              k.v2[:, s, h * P:(h + 1) * P], start=s == 0, stop=s == KT - 1)
                    mm.then_inc(weighed, 1)

                pe.wait_ge(lam_vector, 1)
                nc.tensor.matmul(k.psum[:, 7, 0:2], k.ones[:], lam_prod[:], start=True, stop=True).then_inc(lam_dot, 1)
                pe.wait_ge(lam_scalar, 1)
                for t in range(n + 2):
                    if t < n:
                        score(t, 0)
                        score(t, 1)
                    if 1 <= t <= n:
                        turn(t - 1)
                    if t >= 2:
                        weigh(t - 2)

            @block.vector
            def _(dve):
                step = k.vstep

                def maxima(u):
                    for j in range(2):
                        v = 2 * u + j
                        dve.wait_ge(scored, v + 1)
                        row = k.psum[:, 2 * j:2 * j + 2].rearrange("p b n -> p (b n)")[:, 0:KEYS]
                        nc.vector.tensor_reduce(neg_max[:, v:v + 1], row, AX.X, ALU.max, negate=True).then_inc(maxed, 1)

                def mix(u):
                    dve.wait_ge(exped, 2 * u + 2)
                    step(nc.vector.reciprocal(inv[:, 2 * u:2 * u + 2], total[:, 2 * u:2 * u + 2]))
                    step(nc.vector.tensor_tensor(inv[:, 2 * u + 1:2 * u + 2], inv[:, 2 * u + 1:2 * u + 2], neg_lam[:], ALU.mult))
                    step(nc.vector.tensor_scalar(minus[:], probs[:, u % 2, 1], inv[:, 2 * u + 1:2 * u + 2], None, ALU.mult))
                    nc.vector.scalar_tensor_tensor(probs[:, u % 2, 0], probs[:, u % 2, 0], inv[:, 2 * u:2 * u + 1], minus[:],
                                                   ALU.mult, ALU.add).then_inc(mixed, 1)

                def copy_out(u):
                    i, h = units[u]
                    dve.wait_ge(weighed, u + 1)
                    nc.vector.tensor_copy(k.o[:, i, h * P:(h + 1) * P], k.psum[:, 6 + u % 2, 0:P]).then_inc(out_copied, 1)

                step(nc.vector.memset(lam_prod[:], 0.0))
                nc.vector.tensor_tensor(lam_prod[0:DH], k.vecs[0:DH, LAMBDA:LAMBDA + 4:2], k.vecs[0:DH, LAMBDA + 1:LAMBDA + 4:2],
                                        ALU.mult).then_inc(lam_vector, 1)
                dve.wait_ge(lam_scalar, 1)
                step(nc.vector.tensor_tensor(neg_lam[:], lam_exp[:, 1:2], lam_exp[:, 0:1], ALU.subtract))
                step(nc.vector.tensor_scalar(neg_lam[:], neg_lam[:], LAMBDA_INIT, None, ALU.subtract))
                for t in range(n + 3):
                    if t < n:
                        maxima(t)
                    if 1 <= t <= n:
                        mix(t - 1)
                    if t >= 3:
                        copy_out(t - 3)

            @block.scalar
            def _(act):
                def exp(u):
                    for j in range(2):
                        v = 2 * u + j
                        act.wait_ge(maxed, v + 1)
                        if u >= 2:
                            act.wait_ge(turned, 2 * (u - 1))
                        row = k.psum[:, 2 * j:2 * j + 2].rearrange("p b n -> p (b n)")[:, 0:KEYS]
                        nc.scalar.activation(probs[:, u % 2, j], row, ACT.Exp, bias=neg_max[:, v:v + 1],
                                             accum_out=total[:, v:v + 1]).then_inc(exped, 1)

                def copy_turned(u):
                    for half in range(2):
                        act.wait_ge(turned, 2 * u + half + 1)
                        if u >= 2:
                            act.wait_ge(weighed, u - 1)
                        nc.scalar.activation(probs_t[:, u % 2, half * HALF_KEYS:(half + 1) * HALF_KEYS],
                                             k.psum[:, 4 + half, 0:HALF_KEYS], ACT.Copy).then_inc(turned_copied, 1)

                act.wait_ge(lam_dot, 1)
                nc.scalar.activation(lam_exp[:], k.psum[:, 7, 0:2], ACT.Exp).then_inc(lam_scalar, 1)
                for t in range(n + 1):
                    if t < n:
                        exp(t)
                    if t >= 1:
                        copy_turned(t - 1)


def gates_stage(k):
    nc = k.nc
    done, copied = k.sem("gate2_done"), k.sem("gate2_copied")
    first = FIRST["gate2"]
    with nc.Block(no_gpsimd_drain=True) as block:
        @block.sync
        def _(sp):
            stream(k, sp, first, 8, done, lambda n: 2 * (n + 1))

        @block.tensor
        def _(pe):
            for c in range(2 * KC):
                if c >= 4:
                    pe.wait_ge(copied, c - 3)
                chunk_products(k, pe, k.psum[:, c % 4], first, c, k.h, done)

        @block.scalar
        def _(act):
            for c in range(2 * KC):
                act.wait_ge(done, c + 1)
                nc.scalar.activation(k.gates[:, c], k.psum[:, c % 4], ACT.Sigmoid, bias=k.vecs[:, B_GATE + c:B_GATE + c + 1]).then_inc(
                    copied, 1)


def branches_stage(k):
    nc = k.nc
    done, gated, summed, out_done, out_copied = (k.sem(f"branch_{s}") for s in ("done", "gated", "summed", "out_done", "out_copied"))
    first, first_out = FIRST["branch2"], FIRST["out2"]
    with nc.Block(no_gpsimd_drain=True) as block:
        @block.sync
        def _(sp):
            stream(k, sp, first, 8, done, lambda n: 2 * (n + 1))
            stream(k, sp, first_out, 4, out_done, lambda n: 2 * (n + 1))

        @block.tensor
        def _(pe):
            for c in range(2 * KC):
                if c >= 4:
                    pe.wait_ge(gated, c - 3)
                chunk_products(k, pe, k.psum[:, c % 4], first, c, k.h if c < KC else k.u, done)
            pe.wait_ge(summed, KC)
            for c in range(KC):
                if c >= 4:
                    pe.wait_ge(out_copied, c - 3)
                chunk_products(k, pe, k.psum[:, 4 + c % 4], first_out, c, k.gates, out_done)

        @block.vector
        def _(dve):
            for c in range(2 * KC):
                dve.wait_ge(done, c + 1)
                nc.vector.tensor_tensor(k.gates[:, c], k.gates[:, c], k.psum[:, c % 4], ALU.mult).then_inc(gated, 1)
                if c >= KC:
                    dve.wait_ge(gated, c + 1)
                    nc.vector.tensor_tensor(k.gates[:, c - KC], k.gates[:, c - KC], k.gates[:, c], ALU.add).then_inc(summed, 1)

        @block.scalar
        def _(act):
            for c in range(KC):
                act.wait_ge(out_done, c + 1)
                nc.scalar.activation(k.y2[:, c], k.psum[:, 4 + c % 4], ACT.Copy).then_inc(out_copied, 1)


def query_stage(k):
    nc = k.nc
    done, copied, squared, stat_done, rooted, scored, scaled, loaded, at_vector = (
        k.sem(f"query_{s}") for s in ("done", "copied", "squared", "stat_done", "rooted", "scored", "scaled", "loaded", "vector"))
    first = FIRST["query"]
    n = 2 * PEER_HEADS
    with ExitStack() as scope:
        def sb(name, shape):
            return scope.enter_context(nc.sbuf_tensor(name, shape, F32))

        keys, raw, square = sb("peer_keys", [P, 2, PEER_KEYS]), sb("query_raw", [P, n, SEQ]), sb("query_square", [P, 2, SEQ])
        rstd = sb("query_rstd", [P, TT, n])
        with nc.Block(no_gpsimd_drain=True) as block:
            @block.sync
            def _(sp):
                sp.dma_start(keys[:], k.d["peer_keys"]).then_inc(loaded, 16)
                stream(k, sp, first, 8, done, lambda i: 2 * (i + 1))

            @block.tensor
            def _(pe):
                def stat(c):
                    pe.wait_ge(squared, c + 1)
                    for t in range(TT):
                        mm = nc.tensor.matmul(k.psum[:, 4, t * n + c:t * n + c + 1], square[:, c % 2, t * P:(t + 1) * P],
                                              k.ones[:, 0:1], start=True, stop=True)
                    mm.then_inc(stat_done, 1)

                for c in range(n):
                    if c >= 4:
                        pe.wait_ge(squared, c - 3)
                        pe.wait_ge(copied, c - 3)
                    chunk_products(k, pe, k.psum[:, c % 4], first, c, k.h, done)
                    if c >= 1:
                        stat(c - 1)
                stat(n - 1)
                pe.wait_ge(loaded, 16)
                pe.wait_ge(copied, n)
                for c in range(n):
                    if c >= 3:
                        pe.wait_ge(scaled, c - 2)
                    for t in range(TT):
                        mm = nc.tensor.matmul(k.psum[:, 5 + c % 3, t * P:(t + 1) * P], raw[:, c, t * P:(t + 1) * P], keys[:, c % 2],
                                              start=True, stop=True)
                    mm.then_inc(scored, 1)

            @block.scalar
            def _(act):
                for c in range(n):
                    act.wait_ge(done, c + 1)
                    if c >= 2:
                        act.wait_ge(stat_done, c - 1)
                    nc.scalar.activation(raw[:, c], k.psum[:, c % 4], ACT.Copy).then_inc(copied, 1)
                    nc.scalar.activation(square[:, c % 2], k.psum[:, c % 4], ACT.Square).then_inc(squared, 1)
                act.wait_ge(stat_done, n)
                nc.scalar.activation(rstd[:].rearrange("p t n -> p (t n)"), k.psum[:, 4, 0:TT * n], ACT.Sqrt, bias=k.eps[:, 0:1],
                                     scale=1.0 / P).then_inc(rooted, 1)

            @block.vector
            def _(dve):
                dve.wait_ge(rooted, 1)
                k.vstep(nc.vector.reciprocal(rstd[:], rstd[:]))
                for c in range(n):
                    dve.wait_ge(scored, c + 1)
                    nc.vector.tensor_tensor(k.scores[:, :, c], k.psum[:, 5 + c % 3].rearrange("p (t n) -> p t n", t=TT),
                                            rstd[:, :, c:c + 1].broadcast_to([P, TT, PEER_KEYS]), ALU.mult).then_inc(scaled, 1)


def peer_choice_stage(k):
    nc = k.nc
    loaded, ready, exped, turned, copied = (k.sem(f"choice_{s}") for s in ("loaded", "ready", "exped", "turned", "copied"))
    H, K = PEER_HEADS, PEER_TOPK
    with ExitStack() as scope:
        def sb(name, shape, dt=F32):
            return scope.enter_context(nc.sbuf_tensor(name, shape, dt))

        ramp = sb("choice_ramp", [P, K])
        top, index_u, index = sb("sub_top", [P, 2 * H, K]), sb("sub_index_u", [P, 2 * H, K], U32), sb("sub_index", [P, 2 * H, K])
        cand, best = sb("choice_cand", [P, H, K * K]), sb("choice_best", [P, H, K])
        place, place_a, place_b = (sb(f"choice_place{s}", [P, PAIRS], U32) for s in ("", "_a", "_b"))
        place_f = sb("choice_place_f", [P, PAIRS])
        hot = sb("choice_hot", [P, PAIRS, K])
        picked = sb("choice_picked", [P, 3, 2, PAIRS])
        expo, total = sb("choice_exp", [P, H, K]), sb("choice_total", [P, H])
        with nc.Block(no_gpsimd_drain=True) as block:
            @block.sync
            def _(sp):
                sp.dma_start(ramp[:], k.d["iota"][:, 0:K]).then_inc(loaded, 16)

            @block.vector
            def _(dve):
                step = k.vstep

                def best_of(rows, values, places):
                    for r in range(0, K, 8):
                        for j, row in enumerate(rows):
                            nc.vector.max(values(j)[:, r:r + 8], row).then_inc(step.sem, 1)
                            step.n += 1
                        dve.wait_ge(step.sem, step.n)
                        for j, row in enumerate(rows):
                            nc.vector.max_index(places(j)[:, r:r + 8], values(j)[:, r:r + 8], row).then_inc(step.sem, 1)
                            step.n += 1
                        dve.wait_ge(step.sem, step.n)
                        if r + 8 < K:
                            for j, row in enumerate(rows):
                                nc.vector.match_replace(row, values(j)[:, r:r + 8], row, TAKEN).then_inc(step.sem, 1)
                                step.n += 1
                            dve.wait_ge(step.sem, step.n)

                dve.wait_ge(loaded, 16)
                for t in range(TT):
                    best_of([k.scores[:, t, c] for c in range(2 * H)], lambda j: top[:, j], lambda j: index_u[:, j])
                    step(nc.vector.tensor_copy(index[:], index_u[:]))
                    halves = top[:].rearrange("p (h s) n -> p h s n", s=2)
                    for h in range(H):
                        step(nc.vector.tensor_tensor(cand[:, h].rearrange("p (a b) -> p a b", b=K),
                                                     halves[:, h, 0].unsqueeze(2).broadcast_to([P, K, K]),
                                                     halves[:, h, 1].unsqueeze(1).broadcast_to([P, K, K]), ALU.add))
                    places = place[:].rearrange("p (h n) -> p h n", h=H)
                    best_of([cand[:, h] for h in range(H)], lambda j: best[:, j], lambda j: places[:, j])
                    step(nc.vector.tensor_scalar(place_a[:], place[:], 4, None, ALU.logical_shift_right))
                    step(nc.vector.tensor_scalar(place_b[:], place[:], K - 1, None, ALU.bitwise_and))
                    if t >= 2:
                        dve.wait_ge(copied, t - 1)
                    for s, at in ((0, place_a), (1, place_b)):
                        step(nc.vector.tensor_copy(place_f[:], at[:]))
                        step(nc.vector.tensor_tensor(hot[:], place_f[:].unsqueeze(2).broadcast_to([P, PAIRS, K]),
                                                     ramp[:].unsqueeze(1).broadcast_to([P, PAIRS, K]), ALU.is_equal))
                        hot_h = hot[:].rearrange("p (h n) a -> p h n a", h=H)
                        lists = index[:].rearrange("p (h s) n -> p h s n", s=2)
                        for h in range(H):
                            step(nc.vector.tensor_tensor(hot_h[:, h], hot_h[:, h],
                                                         lists[:, h, s].unsqueeze(1).broadcast_to([P, K, K]), ALU.mult))
                        step(nc.vector.tensor_reduce(picked[:, s, t % 2], hot[:], AX.X, ALU.add))
                    if t >= 1:
                        dve.wait_ge(exped, t)
                    nc.vector.tensor_tensor(expo[:], best[:], best[:, :, 0:1].broadcast_to([P, H, K]), ALU.subtract).then_inc(ready, 1)
                    dve.wait_ge(exped, t + 1)
                    step(nc.vector.tensor_reduce(total[:], expo[:], AX.X, ALU.add))
                    step(nc.vector.reciprocal(total[:], total[:]))
                    nc.vector.tensor_tensor(picked[:, 2, t % 2].rearrange("p (h n) -> p h n", h=H), expo[:],
                                            total[:].unsqueeze(2).broadcast_to([P, H, K]), ALU.mult).then_inc(ready, 1)

            @block.scalar
            def _(act):
                for t in range(TT):
                    act.wait_ge(ready, 2 * t + 1)
                    nc.scalar.activation(expo[:], expo[:], ACT.Exp).then_inc(exped, 1)
                    act.wait_ge(turned, t + 1)
                    nc.scalar.activation(k.pairs[:, :, t * P:(t + 1) * P], k.psum[:, t % 2, 0:3 * P].rearrange("p (s n) -> p s n", s=3),
                                         ACT.Copy).then_inc(copied, 1)

            @block.tensor
            def _(pe):
                for t in range(TT):
                    pe.wait_ge(ready, 2 * t + 2)
                    if t >= 2:
                        pe.wait_ge(copied, t - 1)
                    for s in range(3):
                        mm = nc.tensor.transpose(k.psum[:, t % 2, s * P:(s + 1) * P], picked[:, s, t % 2], k.ident[:])
                    mm.then_inc(turned, 1)


def save_stage(k):
    nc = k.nc
    saved = k.sem("x_saved")
    with nc.Block(no_gpsimd_drain=True) as block:
        @block.sync
        def _(sp):
            sp.dma_start(k.x_dram, k.x[:]).then_inc(saved, 16)
            sp.wait_ge(saved, 16)


def peer_gates_stage(k):
    nc = k.nc
    hot, weighted, used, copied, loaded = (k.sem(f"gates_{s}") for s in ("hot", "weighted", "used", "copied", "loaded"))
    stored = [k.sem(f"gates_stored{i}") for i in range(2)]
    GROUP = 8
    HALF_GROUP = GROUP // 2
    steps = SPAN // GROUP
    turns = SEQ // (2 * SPAN)
    shape = [P, GROUP, P]
    index1, index2, gate = (k.pairs[:, s] for s in range(3))
    with ExitStack() as scope:
        def sb(name, dims):
            return scope.enter_context(nc.sbuf_tensor(name, dims, F32))

        iota, hot1, hot2 = sb("iota", [P, P]), sb("hot1", [P, 2, GROUP, P]), sb("hot2", [P, 2, GROUP, P])
        block_gates = sb("block_gates", [P, 2, PEER_KEYS, SPAN])

        def each_step(eng):
            return [(blk, step, lambda g, at=blk * steps + step: 2 * steps * g + at) for blk in range(2) for step in range(steps)]

        def tokens(vector, n):
            return vector[:, bass.ds(n * GROUP, GROUP)].unsqueeze(2).broadcast_to(shape)

        with nc.Block(no_gpsimd_drain=True) as block:
            @block.sync
            def _(sp):
                sp.dma_start(iota[:], k.d["iota"]).then_inc(loaded, 16)
                for blk in range(2):
                    sp.sem_inc(stored[blk], 16)
                with sp.Fori(0, turns) as g:
                    for blk in range(2):
                        sp.wait_ge(copied, 2 * steps * g + (2 + (blk + 1) * steps))
                        sp.dma_start(k.gates_dram[bass.ds(2 * g + blk, 1)].rearrange("a p j t -> p (a j t)"),
                                     block_gates[:, blk].rearrange("p j t -> p (j t)")).then_inc(stored[blk], 16)
                for blk in range(2):
                    sp.wait_ge(stored[blk], 16 + 16 * turns)

            @block.vector
            def _(dve):
                dve.wait_ge(loaded, 16)
                dve.sem_inc(used, 2)
                with dve.Fori(0, turns) as g:
                    for blk, step, number in each_step(dve):
                        n, b = number(g), step % 2
                        dve.wait_ge(used, n + 1)
                        row = iota[:].unsqueeze(1).broadcast_to(shape)
                        nc.vector.tensor_tensor(hot2[:, b], tokens(index2, n), row, ALU.is_equal).then_inc(hot, 1)
                        nc.vector.tensor_tensor(hot1[:, b], tokens(index1, n), row, ALU.is_equal).then_inc(hot, 1)

            @block.gpsimd
            def _(pool):
                with pool.Fori(0, turns) as g:
                    for blk, step, number in each_step(pool):
                        n, b = number(g), step % 2
                        pool.wait_ge(hot, 2 * n + 1)
                        nc.gpsimd.tensor_tensor(hot2[:, b], hot2[:, b], tokens(gate, n), ALU.mult).then_inc(weighted, 1)

            @block.tensor
            def _(pe):
                with pe.Fori(0, turns) as g:
                    for blk, step, number in each_step(pe):
                        n, b = number(g), step % 2
                        pe.wait_ge(copied, n + 1)
                        pe.wait_ge(hot, 2 * n + 2)
                        pe.wait_ge(weighted, n + 1)
                        for i in range(GROUP):
                            at = (i % HALF_GROUP) * P
                            mm = nc.tensor.matmul(k.psum[:, 2 * b + i // HALF_GROUP, at:at + P], hot1[:, b, i], hot2[:, b, i],
                                                  start=True, stop=True)
                        mm.then_inc(used, 1)

            @block.scalar
            def _(act):
                act.sem_inc(copied, 2)
                with act.Fori(0, turns) as g:
                    for blk, step, number in each_step(act):
                        n, b = number(g), step % 2
                        if step == 0:
                            act.wait_ge(stored[blk], 16 * g + 16)
                        act.wait_ge(used, n + 3)
                        for i in range(2):
                            at = step * GROUP + i * HALF_GROUP
                            ins = nc.scalar.activation(block_gates[:, blk, :, at:at + HALF_GROUP].rearrange("p j t -> p t j"),
                                                       k.psum[:, 2 * b + i].rearrange("p (t j) -> p t j", t=HALF_GROUP), ACT.Copy)
                        ins.then_inc(copied, 1)


def peer_stage(k):
    nc = k.nc
    hid_done, gelu_done, gated, a_high, a_ready, u_high, u_ready, v_high, v_ready, v_done, added, h_high, h_ready = (
        k.sem(f"peer_{s}") for s in ("hid_done", "gelu_done", "gated", "a_high", "a_ready", "u_high", "u_ready", "v_high",
                                     "v_ready", "v_done", "added", "h_high", "h_ready"))
    gate_loaded = [k.sem(f"peer_gate_loaded{i}") for i in range(2)]
    first, batches = FIRST["peer"], PEER_KEYS // 2
    loops = (batches - 4) // 2
    by_batch = k.gates_dram.rearrange("s p (b j) t -> p b s (j t)", j=2)
    spans = SEQ // SPAN

    def tile(r):
        n = first + int(2 * r)
        return n % SLOTS, 16 * (n // SLOTS + 1)

    with ExitStack() as scope:
        def sb(name, dims, kind=F32):
            return scope.enter_context(nc.sbuf_tensor(name, dims, kind))

        gate, acts = sb("gate_tiles", [P, 2, 2 * SEQ]), sb("peer_acts", [P, 2, SEQ])
        a_hi, a_lo = sb("a_hi", [P, 2, 2, SEQ], F32R), sb("a_lo", [P, 2, 2, SEQ], F32R)
        h_hi, h_lo = sb("h_hi", [P, KC, SEQ], F32R), sb("h_lo", [P, KC, SEQ], F32R)
        u_hi, u_lo = sb("u_hi", [P, 2, TILE], F32R), sb("u_lo", [P, 2, TILE], F32R)
        v_hi, v_lo = sb("v_hi", [P, 2, TILE], F32R), sb("v_lo", [P, 2, TILE], F32R)

        def low(lo, source, hi):
            return nc.vector.tensor_tensor(lo, source, hi.bitcast(F32), ALU.subtract)

        def products(out, hi, lo, x_hi, x_lo, start, stop):
            nc.tensor.matmul(out, hi, x_hi, start=start, stop=False)
            nc.tensor.matmul(out, hi, x_lo, start=False, stop=False)
            return nc.tensor.matmul(out, lo, x_hi, start=False, stop=stop)

        with nc.Block(no_gpsimd_drain=True) as block:
            @block.sync
            def _(sp):
                def load_gates(b, r):
                    sp.dma_start(gate[:, r % 2].rearrange("p (s n) -> p s n", s=spans),
                                 by_batch[:, bass.ds(b, 1)].rearrange("p b s n -> p (b s) n")).then_inc(gate_loaded[r % 2], 16)

                def load_tile(b, r, odd):
                    s, _ = tile(r + odd / 2)
                    sp.dma_start(k.ring[:, s, :], k.weights[bass.ds(2 * b + (first + odd), 1)].rearrange("a p n -> p (a n)")).then_inc(
                        k.tile_loaded[s], 16)

                def step(b, r):
                    sp.wait_ge(gated, 2 * b + 2)
                    load_gates(b + 2, r)
                    if r < batches - 4:
                        sp.wait_ge(u_ready, b + 3)
                        load_tile(b + 4, r, 0)
                    sp.wait_ge(v_ready, b + 1)
                    load_tile(b + 2, r, 1)

                for b in range(2):
                    load_gates(b, b)
                for b in range(2):
                    sp.wait_ge(u_ready, b + 1)
                    load_tile(b + 2, b, 0)
                with sp.Fori(0, (batches - 4) // 2) as g:
                    for j in range(2):
                        step(2 * g + j, j)
                for b in range(batches - 4, batches - 2):
                    step(b, b)

            @block.scalar
            def _(act):
                def split_u(r, shift):
                    s, loaded = tile(r)
                    act.wait_ge(k.tile_loaded[s], loaded + shift)
                    nc.scalar.activation(u_hi[:, r % 2], k.ring[:, s], ACT.Copy).then_inc(u_high, 1)

                def step(b, r, shift):
                    if r > 0:
                        act.wait_ge(a_ready, b)
                    for jj in range(2):
                        act.wait_ge(hid_done, 2 * b + (jj + 1))
                        nc.scalar.activation(acts[:, jj], k.psum[:, 2 * (r % 2) + jj], ACT.Gelu).then_inc(gelu_done, 1)
                    if r < batches - 2:
                        split_u(r + 2, shift)
                    act.wait_ge(gated, 2 * b + 2)
                    nc.scalar.activation(a_hi[:, r % 2], acts[:], ACT.Copy).then_inc(a_high, 1)
                    s, loaded = tile(r + 1 / 2)
                    act.wait_ge(k.tile_loaded[s], loaded + shift)
                    nc.scalar.activation(v_hi[:, r % 2], k.ring[:, s], ACT.Copy).then_inc(v_high, 1)

                nc.scalar.activation(h_hi[:], k.h[:], ACT.Copy).then_inc(h_high, 1)
                split_u(0, 0)
                split_u(1, 0)
                step(0, 0, 0)
                with act.Fori(0, loops) as g:
                    for r in (1, 2):
                        step(2 * g + r, r, 16 * g)
                for b in range(2 * loops + 1, batches):
                    step(b, b, 0)

            @block.vector
            def _(dve):
                def split_u(b, r):
                    dve.wait_ge(u_high, b + 1)
                    s, _ = tile(r)
                    low(u_lo[:, r % 2], k.ring[:, s], u_hi[:, r % 2]).then_inc(u_ready, 1)

                def add(b, chunks):
                    for m in chunks:
                        dve.wait_ge(v_done, KC * b + (m + 1))
                        nc.vector.tensor_tensor(k.y3[:, m], k.y3[:, m], k.psum[:, 4 + m % 4], ALU.add).then_inc(added, 1)

                def step(b, r, shift):
                    parity = r % 2
                    dve.wait_ge(gate_loaded[parity], 16 * (r // 2 + 1) + shift)
                    for jj in range(2):
                        dve.wait_ge(gelu_done, 2 * b + (jj + 1))
                        view = acts[:, jj].rearrange("p (s t) -> p s t", s=spans)
                        gates = gate[:, parity].rearrange("p (s j t) -> p s j t", s=spans, j=2)[:, :, jj]
                        nc.vector.tensor_tensor(view, view, gates, ALU.mult).then_inc(gated, 1)
                    if r > 0:
                        add(b - 1, (0,))
                    dve.wait_ge(a_high, b + 1)
                    low(a_lo[:, parity], acts[:], a_hi[:, parity]).then_inc(a_ready, 1)
                    if r > 0:
                        add(b - 1, (1, 2))
                    if r < batches - 2:
                        split_u(b + 2, r + 2)
                    if r > 0:
                        add(b - 1, (3, 4))
                    dve.wait_ge(v_high, b + 1)
                    s, _ = tile(r + 1 / 2)
                    low(v_lo[:, parity], k.ring[:, s], v_hi[:, parity]).then_inc(v_ready, 1)
                    if r > 0:
                        add(b - 1, (5, 6, 7))

                k.vstep(nc.vector.memset(k.y3[:], 0.0))
                dve.wait_ge(h_high, 1)
                low(h_lo[:], k.h[:], h_hi[:]).then_inc(h_ready, 1)
                split_u(0, 0)
                split_u(1, 1)
                step(0, 0, 0)
                with dve.Fori(0, loops) as g:
                    for r in (1, 2):
                        step(2 * g + r, r, 16 * g)
                for b in range(2 * loops + 1, batches):
                    step(b, b, 0)
                add(batches - 1, range(KC))

            @block.tensor
            def _(pe):
                def hidden(b, r):
                    parity = r % 2
                    pe.wait_ge(u_ready, b + 1)
                    if r >= 2:
                        pe.wait_ge(gelu_done, 2 * b - 2)
                    for jj in range(2):
                        for kc in range(KC):
                            at = (jj * KC + kc) * P
                            mm = products(k.psum[:, 2 * parity + jj], u_hi[:, parity, at:at + P], u_lo[:, parity, at:at + P],
                                          h_hi[:, kc], h_lo[:, kc], kc == 0, kc == KC - 1)
                        mm.then_inc(hid_done, 1)

                def out(b, r):
                    parity = r % 2
                    pe.wait_ge(a_ready, b + 1)
                    pe.wait_ge(v_ready, b + 1)
                    for m in range(KC):
                        if r > 0 or m >= 4:
                            pe.wait_ge(added, KC * b + (m - 3))
                        for jj in range(2):
                            at = jj * D + m * P
                            mm = products(k.psum[:, 4 + m % 4], v_hi[:, parity, at:at + P], v_lo[:, parity, at:at + P],
                                          a_hi[:, parity, jj], a_lo[:, parity, jj], jj == 0, jj == 1)
                        mm.then_inc(v_done, 1)

                pe.wait_ge(h_ready, 1)
                hidden(0, 0)
                hidden(1, 1)
                out(0, 0)
                hidden(2, 2)
                with pe.Fori(0, loops) as g:
                    for r in (1, 2):
                        out(2 * g + r, r)
                        hidden(2 * g + (r + 2), r + 2)
                for b in range(2 * loops + 1, batches):
                    out(b, b)
                    if b + 2 < batches:
                        hidden(b + 2, b + 2)


def reload_stage(k):
    nc = k.nc
    loaded = k.sem("x_reloaded")
    with nc.Block(no_gpsimd_drain=True) as block:
        @block.sync
        def _(sp):
            sp.dma_start(k.x2[:], k.x_dram).then_inc(loaded, 16)
            sp.wait_ge(loaded, 16)

        @block.vector
        def _(dve):
            nc.vector.memset(k.ones2[:], 1.0)


def store_stage(k):
    nc = k.nc
    stored = k.sem("out_stored")
    with nc.Block(no_gpsimd_drain=True) as block:
        @block.sync
        def _(sp):
            sp.dma_start(k.d["out"], k.x2[:]).then_inc(stored, 16)
            sp.wait_ge(stored, 16)


def build(nc, d):
    with ExitStack() as whole:
        k = Core()
        k.nc, k.d, k.weights = nc, d, d["weights"]
        k.sem = lambda name: whole.enter_context(nc.semaphore(name))

        def place(scope, kind=F32, **shapes):
            return [scope.enter_context(nc.sbuf_tensor(name, shape, kind)) for name, shape in shapes.items()]

        k.tile_loaded = [k.sem(f"tile_loaded{i}") for i in range(SLOTS)]
        k.loaded = k.sem("vectors_loaded")
        k.norm_sems, k.norms = [k.sem(f"norm_{s}") for s in ("squared", "summed", "std_ready", "scaled")], 0
        k.vstep = Steps(nc.vector, k.sem("vector_step"))
        k.psum = whole.enter_context(nc.psum_tensor("psum", [P, 8, BANK], F32))
        k.h_dram = nc.dram_tensor("h_dram", (SEQ, D), F32, kind="Internal").ap()
        k.y_dram = nc.dram_tensor("y_dram", (EXPERT_TILES * P, D), F32, kind="Internal").ap()
        k.token_dram = nc.dram_tensor("token_dram", (P * EXPERT_TILES, 1), U32, kind="Internal").ap()
        k.gates_dram = nc.dram_tensor("gates_dram", (SEQ // SPAN, P, PEER_KEYS, SPAN), F32, kind="Internal").ap()
        k.x_dram = nc.dram_tensor("x_dram", (P, KC, SEQ), F32, kind="Internal").ap()
        k.ring, k.mod1, k.mod2, k.vecs, k.eps, k.h, k.pairs = place(
            whole, ring=[P, SLOTS, TILE], mod1=[P, N_MOD], mod2=[P, 2, N_MOD], vecs=[P, N_VECS], eps=[P, 2], h=[P, KC, SEQ],
            pairs=[P, 3, SEQ])
        with ExitStack() as main:
            k.x, k.ident, k.ones = place(main, x=[P, KC, SEQ], ident=[P, P], ones=[P, P])
            with ExitStack() as scope:
                k.ada_vecs, k.cond, k.ada_rows = place(scope, ada_vecs=[P, N_ADA], cond=[P, KC, 3], ada_rows=[2, 2, BANK])
                load_stage(k)
                ada_stage(k)
            norm_stage(k, "norm_mix", k.x, k.h, SEQ, k.mod1[:, SCALE_1:SCALE_1 + KC], k.mod1[:, SHIFT_1:SHIFT_1 + KC])
            with ExitStack() as scope:
                (k.proj, k.v_b, k.small, k.causal, k.chosen, k.o, k.neg_cum, k.slope_pos, k.head_rows) = place(
                    scope, proj=[P, FM_CHUNKS, SEQ], v_b=[P, TT, HEADS * DH], small=[P, TT, SMALL], causal=[P, SEQ],
                    chosen=[P, TT, SEQ], o=[P, TT, D], neg_cum=[HEADS, SEQ], slope_pos=[HEADS, SEQ], head_rows=[HEADS, HEADS, P])
                in_projection_stage(k)
                forget_stage(k)
                index_stage(k)
                attention_stage(k)
                head_norm_stage(k, "out1_norm", 2, k.vecs[:, G_OUT:G_OUT + KC])
            out_projection_stage(k)
            norm_stage(k, "norm_ffn", k.x, k.h, SEQ, k.mod1[:, SCALE_2:SCALE_2 + KC], k.mod1[:, SHIFT_2:SHIFT_2 + KC])
            with ExitStack() as scope:
                k.pick, k.pick_weight, k.route_less = place(
                    scope, pick=[P, 2, TT, EXPERTS], pick_weight=[P, 2, TT], route_less=[P, TT, GROUPS])
                k.expert_row, k.slot_token, k.pick_slot = place(
                    scope, U32, expert_row=[P, EXPERT_TILES], slot_token=[P, EXPERT_TILES], pick_slot=[P, 2, TT])
                router_stage(k)
                plan_stage(k)
                moe_stage(k)
                moe_out_stage(k)
            norm_stage(k, "norm_final", k.x, k.x, SEQ, k.vecs[:, G_FINAL:G_FINAL + KC])
            with ExitStack() as scope:
                k.u, k.o = place(scope, u=[P, KC, SEQ], o2=[P, TT, D])
                with ExitStack() as attention:
                    k.q2, k.k2, k.v2 = place(attention, q2=[P, KC, SEQ], k2=[P, KC, KEYS], v2=[P, KT, D])
                    with ExitStack() as inner:
                        k.h_ctx, k.rope, k.swap = place(inner, h_ctx=[P, KC, CTX], rope=[P, 2, SEQ], swap=[P, P])
                        load_context_stage(k)
                        norm_stage(k, "norm_ctx", k.h_ctx, k.h_ctx, CTX, k.mod2[:, 1, SCALE_1:SCALE_1 + KC],
                                   k.mod2[:, 1, SHIFT_1:SHIFT_1 + KC])
                        norm_stage(k, "norm_mix2", k.x, k.h, SEQ, k.mod2[:, 0, SCALE_1:SCALE_1 + KC],
                                   k.mod2[:, 0, SHIFT_1:SHIFT_1 + KC])
                        qk_stage(k)
                        values_stage(k)
                    with ExitStack() as inner:
                        (k.vz,) = place(inner, vz=[P, TT, D])
                        sgu_projection_stage(k)
                        sgu_stage(k)
                    diff_attention_stage(k)
                (k.gates,) = place(scope, gates=[P, 2 * KC, SEQ])
                gates_stage(k)
                head_norm_stage(k, "out2_norm", DIFF_HEADS, k.vecs[:, SUBLN:SUBLN + 1].broadcast_to([P, KC]), 1.0 - LAMBDA_INIT)
                k.y2 = k.o[:].rearrange("p t d -> p (t d)").rearrange("p (c n) -> p c n", c=KC)
                branches_stage(k)
                norm_stage(k, "norm_post_mix", k.y2, k.y2, SEQ, k.mod2[:, 0, GATE_1:GATE_1 + KC], add_to=k.x)
            norm_stage(k, "norm_ffn2", k.x, k.h, SEQ, k.mod2[:, 0, SCALE_2:SCALE_2 + KC], k.mod2[:, 0, SHIFT_2:SHIFT_2 + KC])
            with ExitStack() as scope:
                (k.scores,) = place(scope, scores=[P, TT, 2 * PEER_HEADS, PEER_KEYS])
                query_stage(k)
                peer_choice_stage(k)
            save_stage(k)
        with ExitStack() as tail:
            (k.y3,) = place(tail, y3=[P, KC, SEQ])
            peer_gates_stage(k)
            peer_stage(k)
            k.x2, k.ones2 = place(tail, x2=[P, KC, SEQ], ones2=[P, P])
            k.ones = k.ones2
            reload_stage(k)
            norm_stage(k, "norm_post_ffn", k.y3, k.y3, SEQ, k.mod2[:, 0, GATE_2:GATE_2 + KC], add_to=k.x2)
            store_stage(k)
        return k



def feature_major(w):
    m = w.shape[1]
    return w.reshape(KC, P, m // (2 * P), 2, P).transpose(2, 1, 3, 0, 4).reshape(m // (2 * P), P, TILE)


def token_major(w):
    m = w.shape[1]
    return w.reshape(2, KC // 2, P, m // BANK, BANK).transpose(3, 0, 2, 1, 4).reshape(2 * (m // BANK), P, TILE)


def columns(v):
    return np.ascontiguousarray(v).reshape(-1, P).T


def pack_weights(i):
    w = np.empty((N_TILES, P, TILE), np.float32)

    def put(stage, at, tiles):
        w[FIRST[stage] + at:FIRST[stage] + at + len(tiles)] = tiles

    put("ada1", 0, token_major(i["w_ada"][0]))
    put("ada2", 0, token_major(i["w_ada_2"][0]))
    aq, ak, av, iq, ik, iw, bq, bk, bv, bf = np.split(
        i["w_in"][0], np.cumsum([512, 128, 128, 512, 64, 8, 512, 512, 512]).tolist(), axis=1)
    aq = aq.reshape(D, 2, 4, DH).transpose(0, 2, 1, 3).reshape(D, 512)
    put("in1", 0, feature_major(np.concatenate([aq, iq, bq, bk, ak, ik, ik], axis=1)))
    put("in1", FM_CHUNKS // 2, token_major(bv))
    put("out1", 0, feature_major(i["w_out"][0]))
    w2 = i["w_in_2"][0]
    put("qk2", 0, feature_major(w2[:, 0:2 * D]))
    put("v2", 0, token_major(w2[:, 2 * D:3 * D]))
    put("z2", 0, feature_major(w2[:, 3 * D:4 * D]))
    put("z2", 4, token_major(w2[:, 4 * D:5 * D]))
    put("gate2", 0, feature_major(w2[:, 5 * D:7 * D]))
    put("branch2", 0, feature_major(i["w_branch_attn_2"][0]))
    put("branch2", 4, feature_major(i["w_branch_sgu_2"][0]))
    put("out2", 0, feature_major(i["w_out_2"][0]))
    put("query", 0, feature_major(i["peer_w_query_2"][0]))
    u = i["peer_u_2"][0].reshape(PEER_KEYS, PEER_KEYS // 2, 2, KC, P).transpose(1, 4, 2, 3, 0).reshape(PEER_KEYS // 2, P, TILE)
    v = i["peer_v_2"][0].reshape(PEER_KEYS, PEER_KEYS // 2, TILE).transpose(1, 0, 2)
    w[FIRST["peer"]::2], w[FIRST["peer"] + 1::2] = u, v
    return w


def constants():
    t = np.arange(SEQ)
    q = np.arange(P)
    causal = np.zeros((P, SEQ), np.float32)
    causal[:, SEQ - P:] = np.where(q[None, :] > q[:, None], MASKED, 0.0)
    slopes = 2.0 ** -np.arange(1, HEADS + 1)
    head_rows = np.zeros((HEADS, HEADS, P), np.float32)
    head_rows[np.arange(HEADS), np.arange(HEADS)] = 1.0
    n_freq = DH // 4
    inv = (np.float32(10000.0) ** (-np.arange(n_freq, dtype=np.float32) / np.float32(n_freq))).astype(np.float32)
    f = np.arange(P) % DH
    pos = np.where((f < DH // 2)[:, None], (t // 64)[None, :], (t % 64)[None, :]).astype(np.float32)
    angle = (pos * inv[f % n_freq][:, None]).astype(np.float32)
    sign = np.where(f % (DH // 2) < n_freq, -1.0, 1.0)
    rope = np.stack([np.cos(angle), np.sin(angle) * sign[:, None]], axis=1).astype(np.float32)
    swap = np.zeros((P, P), np.float32)
    swap[np.arange(P) ^ n_freq, np.arange(P)] = 1.0
    return {
        "ident": np.eye(P, dtype=np.float32),
        "iota": np.tile(np.arange(P, dtype=np.float32), (P, 1)),
        "tri": (q[:, None, None] + P * np.arange(TT)[None, :, None] <= t[None, None, :]).astype(np.float32),
        "causal": causal,
        "head_rows": head_rows,
        "slope_pos": (slopes[:, None] * (t - (SEQ - P))[None, :]).astype(np.float32),
        "before": (q[:, None] < q[None, :]).astype(np.float32),
        "token": (q[:, None] + P * np.arange(TT)[None, :]).astype(np.float32),
        "prio": np.tile(np.arange(PER_GROUP, 0, -1).astype(np.float32), (P, 1)),
        "rope": rope,
        "swap": swap,
    }


def lay_out(i):
    lam = np.zeros((P, 4), np.float32)
    for n, name in enumerate(("lambda_q1_2", "lambda_k1_2", "lambda_q2_2", "lambda_k2_2")):
        lam[:DH, n] = i[name][0]
    small = np.split(i["w_in"][0], np.cumsum([512, 128, 128, 512, 64, 8, 1536]).tolist(), axis=1)
    rows = lambda w: w.reshape(KC, P, -1).transpose(1, 0, 2)
    return constants() | {
        "weights": pack_weights(i),
        "x": rows(i["x"][0].T),
        "ctx": rows(i["ctx_2"][0].T),
        "ada_vecs": np.concatenate([columns(i["c"]), columns(i["c_2"]), columns(i["c_ctx_2"]), columns(i["b_ada"]),
                                    columns(i["b_ada_2"])], axis=1),
        "vecs": np.concatenate([columns(i[n]) for n in ("g_mix", "g_out_a", "g_out_b", "g_ffn", "g_final", "g_pre_mix_2", "g_post_mix_2",
                                                        "g_pre_ffn_2", "g_post_ffn_2", "b_gate_2", "subln_g_2")] + [lam], axis=1),
        "w_small": rows(np.concatenate([small[2], small[5], small[7]], axis=1)),
        "b_forget": i["b_forget"],
        "w_route": rows(np.concatenate([i["w_group"][0], i["w_router"][0].transpose(1, 0, 2).reshape(D, EXPERTS)], axis=1)),
        "b_route": np.concatenate([i["b_group"], i["b_router"].reshape(1, EXPERTS)], axis=1),
        "experts_in": np.concatenate([i["w_gate"][0], i["w_up"][0]], axis=2).reshape(EXPERTS, KC, P, 2 * FF).transpose(
            0, 2, 1, 3).reshape(EXPERTS * P, KC * 2 * FF),
        "experts_down": i["w_down"][0].reshape(EXPERTS, FF // P, P, D).transpose(0, 2, 1, 3).reshape(EXPERTS * P, FF // P * D),
        "ln_g": i["sgu_ln_g_2"],
        "ln_b": i["sgu_ln_b_2"],
        "sgu_w": i["sgu_w_2"][0].transpose(2, 0, 1),
        "sgu_b": i["sgu_b_2"].reshape(1, D),
        "peer_keys": i["peer_sub_keys_2"][0].transpose(2, 0, 1),
    }


def program(arrays, nc):
    d = {n: nc.dram_tensor("in_" + n, a.shape, F32, kind="ExternalInput").ap() for n, a in arrays.items()}
    d["out"] = nc.dram_tensor("out", (P, KC, SEQ), F32, kind="ExternalOutput").ap()
    return build(nc, d)


def kernel(**inputs):
    import concourse.bacc as bacc
    from concourse.bass_utils import run_bass_kernel_spmd

    arrays = {n: np.ascontiguousarray(a) for n, a in lay_out({n: np.asarray(a) for n, a in inputs.items()}).items()}
    nc = bacc.Bacc("TRN2", target_bir_lowering=False, num_devices=1)
    program(arrays, nc)
    result = run_bass_kernel_spmd(nc, [{"in_" + n: a for n, a in arrays.items()}], core_ids=[0]).results[0]["out"]
    return np.ascontiguousarray(result.transpose(1, 0, 2).reshape(D, SEQ).T).reshape(1, SEQ, D)
```

```python
from contextlib import ExitStack

import numpy as np

import concourse.bass as bass
import concourse.mybir as mybir

F32 = mybir.dt.float32
F32R = mybir.dt.float32r
U32 = mybir.dt.uint32
ACT = mybir.ActivationFunctionType
ALU = mybir.AluOpType
AX = mybir.AxisListType

P = 128
SEQ, D = 512, 1024
CTX = 256
KC = D // P
TT = SEQ // P
BANK = 512
SLOTS, TILE = 4, 2048
EPS, LN_EPS = 1e-6, 1e-5

HEADS, DH = 8, 64
TOPK = min(256, SEQ // 4)
GROUPS, PER_GROUP = 4, 8
EXPERTS, FF = GROUPS * PER_GROUP, D // 4
EXPERT_TILES = (2 * SEQ + EXPERTS * (P - 1)) // P
DIFF_HEADS = 8
KEYS = CTX + SEQ
KT = KEYS // P
LAMBDA_INIT = 0.2
SGU_GROUPS = 8
PEER_HEADS, PEER_KEYS, PEER_TOPK = 8, 128, 16
PAIRS = PEER_HEADS * PEER_TOPK
BATCHES = PEER_KEYS // 2
SPAN = 64

MASKED, FILL, TAKEN = -1e30, -1e38, -3e38
TAKEN_BELOW = -2e38

AQ, IQ, BQ, BK, AK, IK = 0, 4, 8, 12, 16, 17
FM_CHUNKS = 18
SMALL = 144
G_MIX, G_OUT, G_FFN, G_FINAL, G_PRE_MIX, G_POST_MIX, G_PRE_FFN, G_POST_FFN = range(0, 64, 8)
B_GATE, SUBLN, LAMBDA, N_VECS = 64, 80, 81, 85
N_MOD = 6 * KC
ADA_C, ADA_B1, ADA_B2, N_ADA = 0, 24, 24 + N_MOD, 24 + 2 * N_MOD
SHIFT_1, SCALE_1, GATE_1, SHIFT_2, SCALE_2, GATE_2 = range(0, N_MOD, KC)

STAGES = [("ada1", 8), ("in1", 11), ("out1", 4), ("z2", 8), ("gate2", 8),
          ("qk2", 8), ("v2", 4), ("branch2", 8), ("out2", 4), ("query", 8), ("peer", PEER_KEYS)]
FIRST = {}
N_TILES = 0
for _name, _n in STAGES:
    FIRST[_name] = N_TILES
    N_TILES += _n
COUNT = dict(STAGES)
MOD_SLOTS = 3
SPANS = D // BANK
EARLY_SPANS = [(0,)] * (4 * SPANS) + [(1, 2)] * (2 * SPANS)
LATE_SPANS = [(1,)] * (4 * SPANS)
EARLY_MOD_TILES = 2 * len(EARLY_SPANS)


class Core:
    pass


class Steps:

    def __init__(self, eng, sem):
        self.eng, self.sem, self.n = eng, sem, 0

    def __call__(self, ins):
        ins.then_inc(self.sem, 1)
        self.n += 1
        self.eng.wait_ge(self.sem, self.n)


def wait_tile(k, pe, n):
    pe.wait_ge(k.tile_loaded[n % SLOTS], 16 * (n // SLOTS + 1))


def slot(k, n):
    return k.ring[:, n % SLOTS, :]


def stream(k, sp, first, count):
    for n in range(first, first + count):
        sp.wait_ge(k.w_ready, split_number(n) + 1)
        sp.dma_start(slot(k, n + SLOTS), k.weights[n + SLOTS]).then_inc(k.tile_loaded[n % SLOTS], 16)



def split_number(n):
    return n - FIRST["in1"]


def parts(k, n):
    return k.w_hi[:, split_number(n) % 2], k.w_lo[:, split_number(n) % 2]


def wait_split(k, pe, n):
    pe.wait_ge(k.w_ready, split_number(n) + 1)


def high_part(k, act, n):
    wait_tile(k, act, n)
    k.nc.scalar.activation(parts(k, n)[0], slot(k, n), ACT.Copy).then_inc(k.w_high, 1)


def low_part(k, pool, n):
    hi, lo = parts(k, n)
    pool.wait_ge(k.w_high, split_number(n) + 1)
    k.nc.gpsimd.tensor_tensor(lo, slot(k, n), hi.bitcast(F32), ALU.subtract).then_inc(k.w_ready, 1)


def next_high(k, act, first, i, used):
    if i > 0:
        act.wait_ge(*used(i - 1))
    high_part(k, act, first + i + 1)


def low_parts(k, pool, first, count):
    for i in range(count):
        low_part(k, pool, first + i + 1)


def split_products(k, out, hi, lo, x_hi, x_lo, start, stop):
    k.nc.tensor.matmul(out, hi, x_hi, start=start, stop=False)
    k.nc.tensor.matmul(out, hi, x_lo, start=False, stop=False)
    return k.nc.tensor.matmul(out, lo, x_hi, start=False, stop=stop)


def split_stage(k, source):
    nc = k.nc
    high = k.activation_high
    turn, k.activations = k.activations, k.activations + 1
    with nc.Block(no_gpsimd_drain=True) as block:
        @block.scalar
        def _(act):
            for c in range(KC):
                nc.scalar.activation(k.h_hi[:, c], source[:, c], ACT.Copy).then_inc(high, 1)

        @block.vector
        def _(dve):
            for c in range(KC):
                dve.wait_ge(high, KC * turn + c + 1)
                nc.vector.tensor_tensor(k.h_lo[:, c], source[:, c], k.h_hi[:, c].bitcast(F32), ALU.subtract)


def stage_loads(k, count):
    earlier, k.stage_load_count = k.stage_load_count, k.stage_load_count + 16 * count
    return k.stage_loaded, earlier


def load_stage(k):
    nc = k.nc
    with nc.Block(no_gpsimd_drain=True) as block:
        @block.sync
        def _(sp):
            for n in range(SLOTS):
                sp.dma_start(slot(k, n), k.weights[n]).then_inc(k.tile_loaded[n], 16)

        @block.scalar
        def _(act):
            act.dma_start(k.ada_vecs[:], k.d["ada_vecs"]).then_inc(k.moved, 16)
            act.dma_start(k.ident[:], k.d["ident"]).then_inc(k.moved, 16)
            k.moves = 2
            act.wait_ge(k.moved, 16 * k.moves)
            act.dma_start(k.vecs[:], k.d["vecs"]).then_inc(k.loaded, 16)
            act.dma_start(k.x[:], k.d["x"]).then_inc(k.loaded, 16)

        @block.vector
        def _(dve):
            nc.vector.memset(k.ones[:], 1.0).then_inc(k.vstep.sem, 1)
            nc.vector.memset(k.eps[:, 0:1], EPS).then_inc(k.vstep.sem, 1)
            nc.vector.memset(k.eps[:, 1:2], LN_EPS).then_inc(k.vstep.sem, 1)
            k.vstep.n += 3


def ada_stage(k):
    nc = k.nc
    tile_used, cond_ready, rows_copied, turned, added = (
        k.sem(f"ada_{s}") for s in ("tile_used", "cond_ready", "rows_copied", "turned", "added"))
    n1 = COUNT["ada1"]
    rows = k.ada_rows
    turns, per_span = n1 // SLOTS, BANK // P
    with nc.Block(no_gpsimd_drain=True) as block:
        @block.sync
        def _(sp):
            for n in range(n1):
                sp.wait_ge(tile_used, n + 1)
                sp.dma_start(slot(k, n + SLOTS), k.weights[n + SLOTS]).then_inc(k.tile_loaded[n % SLOTS], 16)
                if n >= n1 - SLOTS and n - (n1 - SLOTS) < MOD_SLOTS:
                    load_mod_tile(k, sp, n - (n1 - SLOTS))

        @block.scalar
        def _(act):
            nc.scalar.activation(k.cond[:].rearrange("p c v -> p v c"), k.ada_vecs[:, ADA_C:ADA_C + 24].rearrange(
                "p (v c) -> p v c", v=3), ACT.Silu).then_inc(cond_ready, 1)
            high_part(k, act, FIRST["in1"])

        @block.gpsimd
        def _(pool):
            low_part(k, pool, FIRST["in1"])

        @block.tensor
        def _(pe):
            pe.wait_ge(cond_ready, 1)
            for g in range(turns):
                for b in range(2):
                    if g > 0:
                        pe.wait_ge(rows_copied, 2 * (g - 1) + b + 1)
                    for n in (4 * g + 2 * b, 4 * g + 2 * b + 1):
                        wait_tile(k, pe, n)
                        for j in range(KC // 2):
                            kc = (n % 2) * (KC // 2) + j
                            mm = nc.tensor.matmul(k.psum[0:1, b], k.cond[:, kc, 0:1], slot(k, n)[:, j * BANK:(j + 1) * BANK],
                                                  start=kc == 0, stop=kc == KC - 1)
                        mm.then_inc(tile_used, 1)
                for b in range(2):
                    pe.wait_ge(rows_copied, 2 * g + b + 1)
                    if g > 0:
                        pe.wait_ge(added, 2 * (g - 1) + b + 1)
                    for c in range(per_span):
                        mm = nc.tensor.matmul(k.psum[:, 2 + b, c:c + 1], rows[0:1, b, c * P:(c + 1) * P], k.ident[0:1, 0:1],
                                              start=True, stop=True)
                    mm.then_inc(turned, 1)

        @block.vector
        def _(dve):
            for g in range(turns):
                for b in range(2):
                    dve.wait_ge(tile_used, 4 * g + 2 * b + 2)
                    nc.vector.tensor_copy(rows[0:1, b], k.psum[0:1, b]).then_inc(rows_copied, 1)
                for b in range(2):
                    dve.wait_ge(turned, 2 * g + b + 1)
                    at = (2 * g + b) * per_span
                    nc.vector.tensor_tensor(k.mod1[:, at:at + per_span], k.psum[:, 2 + b, 0:per_span],
                                            k.ada_vecs[:, ADA_B1 + at:ADA_B1 + at + per_span], ALU.add).then_inc(added, 1)
            dve.wait_ge(added, 2 * turns)
            dve.wait_ge(k.loaded, 32)
            fold(k, k.mod1[:, SCALE_1:SCALE_1 + KC], G_MIX, 1.0)


def fold(k, part, gain, one):
    k.vstep(k.nc.vector.scalar_tensor_tensor(part, part, one, k.vecs[:, gain:gain + KC], ALU.add, ALU.mult))


def load_mod_tile(k, sp, n):
    if n >= MOD_SLOTS:
        sp.wait_ge(k.mod_used, n - MOD_SLOTS + 1)
    sp.dma_start(k.mod_tiles[n % MOD_SLOTS], k.d["ada_later"][n]).then_inc(k.mod_loaded[n % MOD_SLOTS], 16)


def mod_sum(k, dve, spans, first, first_unit, i):
    n, buffers = first + i, k.mod_acc.shape[1]
    vectors, unit = spans[i // 2], sum(len(v) for v in spans[:i // 2])
    dve.wait_ge(k.mod_loaded[n % MOD_SLOTS], 16 * (n // MOD_SLOTS + 1))
    for j in range(KC // 2):
        kc, weights = (i % 2) * (KC // 2) + j, k.mod_tiles[n % MOD_SLOTS][:, j * BANK:(j + 1) * BANK]
        for v, vector in enumerate(vectors):
            acc, c = k.mod_acc[:, (unit + v) % buffers], k.cond[:, kc, vector:vector + 1]
            if kc == 0:
                if unit + v >= buffers:
                    dve.wait_ge(k.mod_turned, first_unit + unit + v - buffers + 1)
                product = k.nc.vector.tensor_scalar(acc, weights, c, None, ALU.mult)
            else:
                dve.wait_ge(k.mod_summed, k.mod_sum_count - len(vectors) + 1)
                product = k.nc.vector.scalar_tensor_tensor(acc, weights, c, acc, ALU.mult, ALU.add)
            product.then_inc(k.mod_summed, 1)
            k.mod_sum_count += 1
    dve.wait_ge(k.mod_summed, k.mod_sum_count)
    dve.sem_inc(k.mod_used, 1)


def mod_turn(k, pe, spans, first_unit, u, bank):
    buffers = k.mod_acc.shape[1]
    span = [i for i, vectors in enumerate(spans) for _ in vectors][u]
    pe.wait_ge(k.mod_used, 2 * (span + 1) + (0 if first_unit == 0 else EARLY_MOD_TILES))
    for m in range(BANK // P):
        at = u * (BANK // P) + m
        mm = k.nc.tensor.matmul(k.psum[:, bank, at:at + 1], k.mod_acc[:, u % buffers, m * P:(m + 1) * P], k.ones[:, 0:1],
                                start=True, stop=True)
    mm.then_inc(k.mod_turned, 1)


def norm_stage(k, name, source, target, width, gain, shift=None, add_to=None, split=None):
    nc = k.nc
    squared, summed, totalled, std_ready, scaled = k.norm_sems
    turn, k.norms = k.norms, k.norms + 1
    before = KC * turn
    shifted, shifts = k.shifted, k.shifts
    k.shifts += KC if shift is not None else 0
    low_ready, lows = k.low_ready, k.lows
    k.lows += KC if split is not None else 0
    with ExitStack() as scope:
        square = scope.enter_context(nc.sbuf_tensor(f"{name}_square", [P, 2, width], F32))
        sums = scope.enter_context(nc.sbuf_tensor(f"{name}_sums", [P, width], F32))
        std = scope.enter_context(nc.sbuf_tensor(f"{name}_std", [P, width], F32))
        rstd = scope.enter_context(nc.sbuf_tensor(f"{name}_rstd", [P, width], F32))
        with nc.Block(no_gpsimd_drain=True) as block:
            @block.scalar
            def _(act):
                for c in range(KC):
                    if c >= 2:
                        act.wait_ge(summed, before + c - 1)
                    nc.scalar.activation(square[:, c % 2], source[:, c], ACT.Square).then_inc(squared, 1)
                act.wait_ge(totalled, turn + 1)
                nc.scalar.activation(std[:], k.psum[:, 0, 0:width], ACT.Sqrt, bias=k.eps[:, 0:1], scale=1.0 / D).then_inc(
                    std_ready, 1)
                if shift is not None:
                    for c in range(KC):
                        act.wait_ge(scaled, before + c + 1)
                        if split is not None:
                            nc.scalar.activation(split[0][:, c], target[:, c], ACT.Identity, bias=shift[:, c:c + 1])
                        nc.scalar.activation(target[:, c], target[:, c], ACT.Identity, bias=shift[:, c:c + 1]).then_inc(shifted, 1)

            @block.gpsimd
            def _(pool):
                if split is not None:
                    for c in range(KC):
                        pool.wait_ge(shifted, shifts + c + 1)
                        nc.gpsimd.tensor_tensor(split[1][:, c], target[:, c], split[0][:, c].bitcast(F32), ALU.subtract).then_inc(
                            low_ready, 1)
                    pool.wait_ge(low_ready, lows + KC)

            @block.tensor
            def _(pe):
                pe.wait_ge(summed, before + KC)
                nc.tensor.matmul(k.psum[:, 0, 0:width], k.ones[:], sums[:], start=True, stop=True).then_inc(totalled, 1)

            @block.vector
            def _(dve):
                for c in range(KC):
                    dve.wait_ge(squared, before + c + 1)
                    if c == 0:
                        nc.vector.tensor_copy(sums[:], square[:, 0]).then_inc(summed, 1)
                    else:
                        dve.wait_ge(summed, before + c)
                        nc.vector.tensor_tensor(sums[:], sums[:], square[:, c % 2], ALU.add).then_inc(summed, 1)
                dve.wait_ge(std_ready, turn + 1)
                k.vstep(nc.vector.reciprocal(rstd[:], std[:]))
                for c in range(KC):
                    nc.vector.scalar_tensor_tensor(target[:, c], source[:, c], gain[:, c:c + 1], rstd[:], ALU.mult,
                                                   ALU.mult).then_inc(scaled, 1)
                if add_to is not None:
                    dve.wait_ge(scaled, before + KC)
                    for c in range(KC):
                        nc.vector.tensor_tensor(add_to[:, c], add_to[:, c], target[:, c], ALU.add)


def chunk_products(k, pe, out, tiles, c, source, done):
    n = tiles + c // 2
    hi, lo = parts(k, n)
    wait_split(k, pe, n)
    for kc in range(KC):
        at = ((c % 2) * KC + kc) * P
        mm = split_products(k, out, hi[:, at:at + P], lo[:, at:at + P], source[0][:, kc], source[1][:, kc], kc == 0, kc == KC - 1)
    mm.then_inc(done, 1)


def row_products(k, pe, outs, tiles, tokens, done, free=None):
    for i in range(2):
        wait_split(k, pe, tiles + i)
        hi, lo = parts(k, tiles + i)
        for t, out in enumerate(outs):
            if i == 0 and free is not None:
                free(t)
            for j in range(KC // 2):
                kc, columns = i * (KC // 2) + j, slice(j * BANK, (j + 1) * BANK)
                x_hi, x_lo = tokens(t, kc)
                mm = split_products(k, out, x_hi, x_lo, hi[:, columns], lo[:, columns], kc == 0, kc == KC - 1)
            mm.then_inc(done, 1)


def token_parts(k, t, kc):
    return k.h_hi[:, kc, t * P:(t + 1) * P], k.h_lo[:, kc, t * P:(t + 1) * P]


def in_projection_stage(k):
    nc = k.nc
    done, copied, rows_done = (k.sem(f"in1_{s}") for s in ("done", "copied", "rows_done"))
    loaded, earlier_loads = stage_loads(k, 1)
    first = FIRST["in1"]
    n_fm = FM_CHUNKS // 2
    units, mod_bank = sum(len(vectors) for vectors in EARLY_SPANS), 4 + TT - 1
    with ExitStack() as scope:
        w_small = scope.enter_context(nc.sbuf_tensor("w_small", [P, KC, SMALL], F32))
        def used(i):
            return (done, 2 * (i + 1)) if i < n_fm else (rows_done, TT * (i - n_fm + 1))

        with nc.Block(no_gpsimd_drain=True) as block:
            @block.sync
            def _(sp):
                sp.dma_start(w_small[:], k.d["w_small"]).then_inc(loaded, 16)
                n = MOD_SLOTS
                for i in range(n_fm + 2):
                    stream(k, sp, first + i, 1)
                    while n < min(EARLY_MOD_TILES, MOD_SLOTS + 3 * (i + 1)):
                        load_mod_tile(k, sp, n)
                        n += 1

            @block.gpsimd
            def _(pool):
                low_parts(k, pool, first, n_fm + 2)

            @block.tensor
            def _(pe):
                for c in range(FM_CHUNKS):
                    if c >= 4:
                        pe.wait_ge(copied, c - 3)
                    chunk_products(k, pe, k.psum[:, c % 4], first, c, (k.h_hi, k.h_lo), done)
                    if c >= FM_CHUNKS - units:
                        mod_turn(k, pe, EARLY_SPANS, 0, c - (FM_CHUNKS - units), mod_bank)

                def free(t):
                    if 4 + t == mod_bank:
                        pe.wait_ge(k.mod_read, 1)

                row_products(k, pe, [k.psum[:, 4 + t] for t in range(TT)], first + n_fm, lambda t, kc: token_parts(k, t, kc), rows_done, free)
                pe.wait_ge(loaded, earlier_loads + 16)
                pe.wait_ge(copied, FM_CHUNKS)
                for t in range(TT):
                    for kc in range(KC):
                        mm = nc.tensor.matmul(k.psum[:, 2 + t // 2, (t % 2) * SMALL:(t % 2 + 1) * SMALL],
                                              k.h[:, kc, t * P:(t + 1) * P], w_small[:, kc], start=kc == 0, stop=kc == KC - 1)
                mm.then_inc(rows_done, 1)

            @block.scalar
            def _(act):
                for c in range(FM_CHUNKS):
                    if c % 2 == 0:
                        next_high(k, act, first, c // 2, used)
                    act.wait_ge(done, c + 1)
                    query = c < IQ or BQ <= c < BK
                    nc.scalar.activation(k.proj[:, c], k.psum[:, c % 4], ACT.Copy, scale=DH ** -0.5 if query else 1.0).then_inc(
                        copied, 1)
                for i in range(n_fm, n_fm + 2):
                    next_high(k, act, first, i, used)

            @block.vector
            def _(dve):
                for i in range(EARLY_MOD_TILES):
                    mod_sum(k, dve, EARLY_SPANS, 0, 0, i)
                dve.wait_ge(k.mod_turned, units)
                at, single = GATE_1, 4 * KC
                nc.vector.tensor_tensor(k.mod1[:, at:at + single], k.psum[:, mod_bank, 0:single],
                                        k.ada_vecs[:, ADA_B1 + at:ADA_B1 + at + single], ALU.add).then_inc(k.vstep.sem, 1)
                per = BANK // P
                both = k.psum[:, mod_bank, single:single + 4 * KC].rearrange("p (s v m) -> p v s m", v=2, m=per)
                for v in range(2):
                    nc.vector.tensor_tensor(k.mod2[:, v, 0:2 * KC].rearrange("p (s m) -> p s m", m=per), both[:, v],
                                            k.ada_vecs[:, ADA_B2:ADA_B2 + 2 * KC].rearrange("p (s m) -> p s m", m=per),
                                            ALU.add).then_inc(k.vstep.sem, 1)
                k.vstep.n += 3
                dve.wait_ge(k.vstep.sem, k.vstep.n)
                dve.sem_inc(k.mod_read, 1)
                fold(k, k.mod1[:, SCALE_2:SCALE_2 + KC], G_FFN, 1.0)
                fold(k, k.mod2[:, 0, SCALE_1:SCALE_1 + KC], G_PRE_MIX, 1.0)
                fold(k, k.mod2[:, 1, SCALE_1:SCALE_1 + KC], G_PRE_MIX, 1.0)
                for t in range(TT):
                    dve.wait_ge(rows_done, TT + t + 1)
                    nc.vector.tensor_copy(k.v_b[:, t], k.psum[:, 4 + t])
                dve.wait_ge(rows_done, 2 * TT + 1)
                for i in range(2):
                    nc.vector.tensor_copy(k.small[:, 2 * i:2 * i + 2], k.psum[:, 2 + i, 0:2 * SMALL].rearrange(
                        "p (t n) -> p t n", t=2))


def forget_stage(k):
    nc = k.nc
    at_vector, at_scalar, summed = (k.sem(f"forget_{s}") for s in ("vector", "scalar", "summed"))
    loaded, earlier_loads = stage_loads(k, 5)
    with ExitStack() as scope:
        tri = scope.enter_context(nc.sbuf_tensor("tri", [P, TT, SEQ], F32))
        head_raw, slope_raw, cum_raw = (scope.enter_context(nc.sbuf_tensor(f"{n}_raw", shape, F32)) for n, shape in (
            ("head_rows", [HEADS, HEADS, P]), ("slope_pos", [HEADS, SEQ]), ("neg_cum", [HEADS, SEQ])))
        b_row = scope.enter_context(nc.sbuf_tensor("b_forget_row", [P, HEADS], F32))
        z, mag, e, log_f = (scope.enter_context(nc.sbuf_tensor(f"forget_{n}", [P, TT, HEADS], F32)) for n in
                            ("z", "mag", "e", "log_f"))
        with nc.Block(no_gpsimd_drain=True) as block:
            @block.sync
            def _(sp):
                sp.dma_start(b_row[:], k.d["b_forget"][0].partition_broadcast(P)).then_inc(loaded, 16)
                sp.dma_start(tri[:], k.d["tri"]).then_inc(loaded, 16)
                sp.dma_start(k.causal[:], k.d["causal"]).then_inc(loaded, 16)
                sp.dma_start(head_raw[:], k.d["head_rows"]).then_inc(loaded, 16)
                sp.dma_start(slope_raw[:], k.d["slope_pos"]).then_inc(loaded, 16)
                sp.wait_ge(loaded, earlier_loads + 80)

            @block.vector
            def _(dve):
                step = k.vstep
                dve.wait_ge(loaded, earlier_loads + 80)
                step(nc.vector.tensor_tensor(z[:], k.small[:, :, 136:144], b_row[:].unsqueeze(1).broadcast_to([P, TT, HEADS]),
                                             ALU.add))
                nc.vector.scalar_tensor_tensor(mag[:], z[:], -1.0, z[:], ALU.mult, ALU.max).then_inc(at_vector, 1)
                dve.wait_ge(at_scalar, 2)
                nc.vector.scalar_tensor_tensor(log_f[:], z[:], 0.0, e[:], ALU.min, ALU.subtract).then_inc(at_vector, 1)
                nc.vector.tensor_copy(k.head_rows[:], head_raw[:])
                nc.vector.tensor_copy(k.slope_pos[:], slope_raw[:])
                dve.wait_ge(at_scalar, 4)
                nc.vector.tensor_tensor(k.neg_cum[:, 1], cum_raw[:], k.neg_cum[:, 0].bitcast(F32), ALU.subtract)

            @block.scalar
            def _(act):
                act.wait_ge(at_vector, 1)
                nc.scalar.activation(e[:], mag[:], ACT.Exp, scale=-1.0).then_inc(at_scalar, 1)
                act.wait_ge(at_scalar, 1)
                nc.scalar.activation(e[:], e[:], ACT.Ln, bias=1.0).then_inc(at_scalar, 1)
                act.wait_ge(summed, 1)
                nc.scalar.activation(cum_raw[:], k.psum[0:HEADS, 0], ACT.Copy, scale=-1.0).then_inc(at_scalar, 1)
                nc.scalar.activation(k.neg_cum[:, 0], k.psum[0:HEADS, 0], ACT.Copy, scale=-1.0).then_inc(at_scalar, 1)

            @block.tensor
            def _(pe):
                pe.wait_ge(loaded, earlier_loads + 80)
                pe.wait_ge(at_vector, 2)
                for t in range(TT):
                    mm = nc.tensor.matmul(k.psum[0:HEADS, 0], log_f[:, t], tri[:, t], start=t == 0, stop=t == TT - 1)
                mm.then_inc(summed, 1)


def head_half(chunk_view, half):
    return chunk_view[half * DH:(half + 1) * DH]


def index_stage(k):
    nc = k.nc
    done, relued, added = (k.sem(f"index_{s}") for s in ("done", "relued", "added"))
    units = [(i, h) for i in range(1, TT) for h in range(HEADS)]
    with ExitStack() as scope:
        score = k.index_score
        relu = scope.enter_context(nc.sbuf_tensor("index_relu", [P, 2, SEQ], F32))
        with nc.Block(no_gpsimd_drain=True) as block:
            @block.tensor
            def _(pe):
                for u, (i, h) in enumerate(units):
                    if u >= 2:
                        pe.wait_ge(relued, u - 1)
                    nc.tensor.matmul(k.psum[:, u % 2, 0:P * (i + 1)],
                                     head_half(k.proj[:, IQ + h // 2, i * P:(i + 1) * P], h % 2),
                                     head_half(k.proj[:, IK, 0:P * (i + 1)], h % 2), start=True, stop=True).then_inc(done, 1)

            @block.scalar
            def _(act):
                for u, (i, h) in enumerate(units):
                    act.wait_ge(done, u + 1)
                    if u >= 2:
                        act.wait_ge(added, u - 1)
                    nc.scalar.activation(relu[:, u % 2, 0:P * (i + 1)], k.psum[:, u % 2, 0:P * (i + 1)], ACT.Relu).then_inc(
                        relued, 1)

            @block.vector
            def _(dve):
                step = k.vstep
                for u, (i, h) in enumerate(units):
                    w = P * (i + 1)
                    weight = k.small[:, i, 128 + h:129 + h]
                    dve.wait_ge(relued, u + 1)
                    if h == 0:
                        nc.vector.tensor_scalar(score[:, i, 0:w], relu[:, u % 2, 0:w], weight, None, ALU.mult).then_inc(added, 1)
                    else:
                        dve.wait_ge(added, u)
                        nc.vector.scalar_tensor_tensor(score[:, i, 0:w], relu[:, u % 2, 0:w], weight, score[:, i, 0:w],
                                                       ALU.mult, ALU.add).then_inc(added, 1)
                dve.wait_ge(added, len(units))
                for i in range(1, TT):
                    part = score[:, i, P * i:P * (i + 1)]
                    step(nc.vector.scalar_tensor_tensor(part, k.causal[:, SEQ - P:SEQ], FILL / MASKED, part, ALU.mult, ALU.add))


def attention_stage(k):
    nc = k.nc
    square_done, scored, masked, exped, turned, turned_copied, weighed, out_copied = (
        k.sem(f"attn_{s}") for s in ("square_done", "scored", "masked", "exped", "turned", "turned_copied", "weighed", "out_copied"))
    units = [(a, i, h) for a in (1, 0) for i in range(TT) for h in range(HEADS)]
    first_sparse = TT * HEADS
    assert TOPK // 8 * 2 <= first_sparse
    n = len(units)
    DEEP = 3
    with ExitStack() as scope:
        def sb(name, shape):
            return scope.enter_context(nc.sbuf_tensor(name, shape, F32))

        logits, probs, probs_t = sb("attn_logits", [P, DEEP, SEQ]), sb("attn_probs", [P, DEEP, SEQ]), sb("attn_probs_t", [P, 2, SEQ])
        top, squared = sb("index_top", [P, TT, 8]), sb("attn_squared", [P, 2, DH])
        neg_max, total, inv = sb("attn_neg_max", [P, n]), sb("attn_total", [P, n]), sb("attn_inv", [P, n])
        with nc.Block(no_gpsimd_drain=True) as block:
            @block.tensor
            def _(pe):
                def score(u):
                    a, i, h = units[u]
                    w = P * (i + 1)
                    if u >= 2:
                        pe.wait_ge(masked, u - 1)
                    if a == 0:
                        q, key, half, rows = AQ + h % 4, AK, h // 4, (k.slope_pos[:, SEQ - w:SEQ],)
                    else:
                        q, key, half, rows = BQ + h // 2, BK + h // 2, h % 2, (k.neg_cum[:, 0, 0:w], k.neg_cum[:, 1, 0:w])
                    out = k.psum[:, u % 2, 0:w]
                    nc.tensor.matmul(out, head_half(k.proj[:, q, i * P:(i + 1) * P], half), head_half(k.proj[:, key, 0:w], half),
                                     start=True, stop=False)
                    for row in rows:
                        mm = nc.tensor.matmul(out, k.head_rows[:, h], row, start=False, stop=row is rows[-1])
                    mm.then_inc(scored, 1)

                def turn(u):
                    i = units[u][1]
                    pe.wait_ge(exped, u + 1)
                    if u >= 2:
                        pe.wait_ge(turned_copied, u - 1)
                    for s in range(i + 1):
                        mm = nc.tensor.transpose(k.psum[:, 2 + u % 2, s * P:(s + 1) * P], probs[:, u % DEEP, s * P:(s + 1) * P],
                                                 k.ident[:])
                    mm.then_inc(turned, 1)

                def weigh(u):
                    a, i, h = units[u]
                    pe.wait_ge(turned_copied, u + 1)
                    if u >= 2:
                        pe.wait_ge(out_copied, u - 1)
                    for s in range(i + 1):
                        v = k.small[:, s, (h // 4) * DH:(h // 4 + 1) * DH] if a == 0 else k.v_b[:, s, h * DH:(h + 1) * DH]
                        mm = nc.tensor.matmul(k.psum[:, 4 + u % 2, 0:DH], probs_t[:, u % 2, s * P:(s + 1) * P], v,
                                              start=s == 0, stop=s == i)
                    mm.then_inc(weighed, 1)

                for t in range(n + DEEP):
                    if t < n:
                        score(t)
                    if 2 <= t < n + 2:
                        turn(t - 2)
                    if t >= DEEP:
                        weigh(t - DEEP)

            @block.vector
            def _(dve):
                def mask(u):
                    a, i, _h = units[u]
                    w = P * (i + 1)
                    dve.wait_ge(scored, u + 1)
                    if u >= DEEP:
                        dve.wait_ge(exped, u - DEEP + 1)
                    mask_rows = k.chosen[:, i, 0:w] if a == 0 else k.causal[:, SEQ - w:SEQ]
                    k.vstep(nc.vector.tensor_tensor(logits[:, u % DEEP, 0:w], k.psum[:, u % 2, 0:w], mask_rows, ALU.add))
                    nc.vector.tensor_reduce(neg_max[:, u:u + 1], logits[:, u % DEEP, 0:w], AX.X, ALU.max, negate=True).then_inc(
                        masked, 1)

                def normalise(u):
                    a, i, h = units[u]
                    dve.wait_ge(exped, u + 1)
                    k.vstep(nc.vector.reciprocal(inv[:, u:u + 1], total[:, u:u + 1]))
                    dve.wait_ge(weighed, u + 1)
                    at = a * HEADS * DH + h * DH
                    nc.vector.tensor_scalar(k.o[:, i, at:at + DH], k.psum[:, 4 + u % 2, 0:DH], inv[:, u:u + 1], None,
                                            ALU.mult).then_inc(out_copied, 1)

                def choose(t):
                    dve.wait_ge(k.vstep.sem, k.vstep.n)
                    for i in range(1, TT):
                        row = k.index_score[:, i, 0:P * (i + 1)]
                        if t % 2 == 0:
                            ins = nc.vector.max(top[:, i], row)
                        else:
                            ins = nc.vector.match_replace(row, top[:, i], row, TAKEN)
                        ins.then_inc(k.vstep.sem, 1)
                        k.vstep.n += 1

                def mark_chosen():
                    dve.wait_ge(k.vstep.sem, k.vstep.n)
                    k.vstep(nc.vector.tensor_copy(k.chosen[:, 0, 0:P], k.causal[:, SEQ - P:SEQ]))
                    for i in range(1, TT):
                        w = P * (i + 1)
                        k.vstep(nc.vector.tensor_scalar(k.chosen[:, i, 0:w], k.index_score[:, i, 0:w], TAKEN_BELOW, MASKED, ALU.is_gt,
                                                        ALU.mult))

                for t in range(n + DEEP + 1):
                    if t == first_sparse:
                        mark_chosen()
                    if t < n:
                        mask(t)
                    if t < TOPK // 8 * 2:
                        choose(t)
                    if t > DEEP:
                        normalise(t - DEEP - 1)

            @block.scalar
            def _(act):
                def exp(u):
                    w = P * (units[u][1] + 1)
                    act.wait_ge(masked, u + 1)
                    if u >= DEEP:
                        act.wait_ge(turned, u - DEEP + 1)
                    nc.scalar.activation(probs[:, u % DEEP, 0:w], logits[:, u % DEEP, 0:w], ACT.Exp, bias=neg_max[:, u:u + 1],
                                         accum_out=total[:, u:u + 1]).then_inc(exped, 1)

                def copy_turned(u):
                    w = P * (units[u][1] + 1)
                    act.wait_ge(turned, u + 1)
                    if u >= 2:
                        act.wait_ge(weighed, u - 1)
                    nc.scalar.activation(probs_t[:, u % 2, 0:w], k.psum[:, 2 + u % 2, 0:w], ACT.Copy).then_inc(turned_copied, 1)

                def square(u):
                    a, i, h = units[u]
                    at = a * HEADS * DH + h * DH
                    act.wait_ge(out_copied, u + 1)
                    if u >= 2:
                        act.wait_ge(square_done, u - 1)
                    nc.scalar.activation(squared[:, u % 2], k.o[:, i, at:at + DH], ACT.Square, accum_out=k.squares[:, i, a, h:h + 1]).then_inc(
                        square_done, 1)

                for t in range(n + DEEP + 2):
                    if t < n:
                        exp(t)
                    if 2 <= t < n + 2:
                        copy_turned(t - 2)
                    if t > DEEP + 1:
                        square(t - DEEP - 2)


def head_norm_stage(k, name, groups, gain, squares, gain_scale=1.0):
    nc = k.nc
    std_ready, scaled, turned, copied, rooted = k.head_norm_sems
    turn, k.head_norms = k.head_norms, k.head_norms + 1
    high = k.activation_high
    high_turn, k.activations = k.activations, k.activations + 1
    width = D // groups
    with ExitStack() as scope:
        total = scope.enter_context(nc.sbuf_tensor(f"{name}_total", [P, TT, groups], F32))
        rstd = scope.enter_context(nc.sbuf_tensor(f"{name}_rstd", [P, TT, groups], F32))
        gains = scope.enter_context(nc.sbuf_tensor(f"{name}_gains", [P, KC], F32))
        with nc.Block(no_gpsimd_drain=True) as block:
            @block.vector
            def _(dve):
                step = k.vstep
                step(nc.vector.tensor_scalar(gains[:], gain, gain_scale, None, ALU.mult))
                if squares.shape[-1] > 1:
                    step(nc.vector.tensor_reduce(total[:], squares, AX.X, ALU.add))
                else:
                    step(nc.vector.tensor_copy(total[:], squares.rearrange("p t g n -> p t (g n)")))
                nc.vector.tensor_scalar(total[:], total[:], 1.0 / width, EPS, ALU.mult, ALU.add).then_inc(std_ready, 1)
                dve.wait_ge(rooted, turn + 1)
                step(nc.vector.reciprocal(rstd[:], total[:]))
                for t in range(TT):
                    rows = k.o[:, t].rearrange("p (g n) -> p g n", g=groups)
                    nc.vector.tensor_tensor(rows, rows, rstd[:, t].unsqueeze(2).broadcast_to([P, groups, width]),
                                            ALU.mult).then_inc(scaled, 1)
                for c in range(KC):
                    dve.wait_ge(high, KC * high_turn + c + 1)
                    nc.vector.scalar_tensor_tensor(k.h_lo[:, c], k.psum[:, c % 4], gains[:, c:c + 1], k.h_hi[:, c].bitcast(F32), ALU.mult,
                                                   ALU.subtract).then_inc(copied, 1)

            @block.tensor
            def _(pe):
                pe.wait_ge(scaled, TT * turn + TT)
                for c in range(KC):
                    if c >= 4:
                        pe.wait_ge(copied, KC * turn + c - 3)
                    for t in range(TT):
                        mm = nc.tensor.transpose(k.psum[:, c % 4, t * P:(t + 1) * P], k.o[:, t, c * P:(c + 1) * P], k.ident[:])
                    mm.then_inc(turned, 1)

            @block.scalar
            def _(act):
                act.wait_ge(std_ready, turn + 1)
                nc.scalar.activation(total[:], total[:], ACT.Sqrt).then_inc(rooted, 1)
                for c in range(KC):
                    act.wait_ge(turned, KC * turn + c + 1)
                    nc.scalar.activation(k.h_hi[:, c], k.psum[:, c % 4], ACT.Copy, scale=gains[:, c:c + 1]).then_inc(high, 1)


def out_projection_stage(k):
    nc = k.nc
    done, added = k.sem("out1_done"), k.sem("out1_added")
    first = FIRST["out1"]
    def used(i):
        return (done, 2 * (i + 1))

    with nc.Block(no_gpsimd_drain=True) as block:
        @block.sync
        def _(sp):
            stream(k, sp, first, COUNT["out1"])

        @block.gpsimd
        def _(pool):
            low_parts(k, pool, first, COUNT["out1"])

        @block.scalar
        def _(act):
            for i in range(COUNT["out1"]):
                next_high(k, act, first, i, used)

        @block.tensor
        def _(pe):
            for c in range(KC):
                if c >= 4:
                    pe.wait_ge(added, c - 3)
                chunk_products(k, pe, k.psum[:, c % 4], first, c, (k.h_hi, k.h_lo), done)

        @block.vector
        def _(dve):
            for c in range(KC):
                dve.wait_ge(done, c + 1)
                nc.vector.scalar_tensor_tensor(k.x[:, c], k.psum[:, c % 4], k.mod1[:, GATE_1 + c:GATE_1 + c + 1], k.x[:, c],
                                               ALU.mult, ALU.add).then_inc(added, 1)


def first_of_largest(k, sb, name, values, n, prio):
    nc, step = k.nc, k.vstep
    shape = [P, TT, n]
    top, less, mark, best, hot = (sb(f"{name}_{s}", [P, TT] if s in ("top", "best") else shape) for s in
                                  ("top", "less", "mark", "best", "hot"))
    step(nc.vector.tensor_reduce(top[:], values, AX.X, ALU.max))
    step(nc.vector.tensor_tensor(less[:], values, top[:].unsqueeze(2).broadcast_to(shape), ALU.subtract))
    step(nc.vector.tensor_scalar(mark[:], less[:], 0.0, None, ALU.is_equal))
    step(nc.vector.tensor_tensor(mark[:], mark[:], prio[:, 0:n].unsqueeze(1).broadcast_to(shape), ALU.mult))
    step(nc.vector.tensor_reduce(best[:], mark[:], AX.X, ALU.max))
    step(nc.vector.tensor_tensor(hot[:], mark[:], best[:].unsqueeze(2).broadcast_to(shape), ALU.is_equal))
    return top, less, hot


def router_stage(k):
    nc = k.nc
    routed, at_vector, at_scalar, turned, copied, stored = (
        k.sem(f"route_{s}") for s in ("routed", "vector", "scalar", "turned", "copied", "stored"))
    loaded, earlier_loads = stage_loads(k, 3)
    n = GROUPS + EXPERTS
    with ExitStack() as scope:
        def sb(name, shape):
            return scope.enter_context(nc.sbuf_tensor(name, shape, F32))

        w_route, b_route, prio = sb("w_route", [P, KC, n]), sb("b_route", [P, n]), sb("prio", [P, PER_GROUP])
        logits, picked = sb("route_logits", [P, TT, n]), sb("route_picked", [P, TT, GROUPS, PER_GROUP])
        expert, second = sb("route_expert", [P, TT, PER_GROUP]), sb("route_second", [P, TT, PER_GROUP])
        exp_group, group_sum, p_group = sb("exp_group", [P, TT, GROUPS]), sb("group_sum", [P, TT]), sb("p_group", [P, TT])
        delta, w_first, w_second = sb("route_delta", [P, TT]), sb("w_first", [P, TT]), sb("w_second", [P, TT])
        h_rows = sb("h_rows", [P, TT, D])
        with nc.Block(no_gpsimd_drain=True) as block:
            @block.sync
            def _(sp):
                sp.dma_start(w_route[:], k.d["w_route"]).then_inc(loaded, 16)
                sp.dma_start(b_route[:], k.d["b_route"][0].partition_broadcast(P)).then_inc(loaded, 16)
                sp.dma_start(prio[:], k.d["prio"]).then_inc(loaded, 16)
                sp.wait_ge(copied, 2 * TT)
                sp.dma_start(k.h_dram.rearrange("(t p) d -> p t d", p=P), h_rows[:]).then_inc(stored, 16)
                sp.wait_ge(stored, 16)

            @block.tensor
            def _(pe):
                pe.wait_ge(loaded, earlier_loads + 48)
                for t in range(TT):
                    for kc in range(KC):
                        mm = nc.tensor.matmul(k.psum[:, 0, t * n:(t + 1) * n], k.h[:, kc, t * P:(t + 1) * P], w_route[:, kc],
                                              start=kc == 0, stop=kc == KC - 1)
                mm.then_inc(routed, 1)
                for half in range(2 * TT):
                    if half >= 4:
                        pe.wait_ge(copied, half - 3)
                    for c in range(KC // 2):
                        mm = nc.tensor.transpose(k.psum[:, 1 + half % 4, c * P:(c + 1) * P],
                                                 k.h[:, (half % 2) * (KC // 2) + c, (half // 2) * P:(half // 2 + 1) * P], k.ident[:])
                    mm.then_inc(turned, 1)

            @block.scalar
            def _(act):
                act.wait_ge(at_vector, 1)
                nc.scalar.activation(exp_group[:], k.route_less[:], ACT.Exp).then_inc(at_scalar, 1)
                act.wait_ge(at_vector, 2)
                nc.scalar.activation(w_second[:], delta[:], ACT.Exp).then_inc(at_scalar, 1)
                for half in range(2 * TT):
                    act.wait_ge(turned, half + 1)
                    nc.scalar.activation(h_rows[:, half // 2, (half % 2) * BANK:(half % 2 + 1) * BANK], k.psum[:, 1 + half % 4], ACT.Copy).then_inc(
                        copied, 1)

            @block.vector
            def _(dve):
                step = k.vstep
                dve.wait_ge(loaded, earlier_loads + 48)
                dve.wait_ge(routed, 1)
                step(nc.vector.tensor_tensor(logits[:], k.psum[:, 0, 0:TT * n].rearrange("p (t n) -> p t n", n=n),
                                             b_route[:].unsqueeze(1).broadcast_to([P, TT, n]), ALU.add))
                _top, less, group = first_of_largest(k, sb, "group", logits[:, :, 0:GROUPS], GROUPS, prio)
                nc.vector.tensor_copy(k.route_less[:], less[:]).then_inc(at_vector, 1)
                for g in range(GROUPS):
                    step(nc.vector.tensor_tensor(picked[:, :, g], logits[:, :, GROUPS + g * PER_GROUP:GROUPS + (g + 1) * PER_GROUP],
                                                 group[:, :, g:g + 1].broadcast_to([P, TT, PER_GROUP]), ALU.mult))
                step(nc.vector.tensor_reduce(expert[:], picked[:].rearrange("p t g e -> p t e g"), AX.X, ALU.add))
                top1, _less1, hot1 = first_of_largest(k, sb, "best1", expert[:], PER_GROUP, prio)
                step(nc.vector.scalar_tensor_tensor(second[:], hot1[:], MASKED, expert[:], ALU.mult, ALU.add))
                top2, _less2, hot2 = first_of_largest(k, sb, "best2", second[:], PER_GROUP, prio)
                nc.vector.tensor_tensor(delta[:], top2[:], top1[:], ALU.subtract).then_inc(at_vector, 1)
                dve.wait_ge(at_scalar, 2)
                step(nc.vector.tensor_reduce(group_sum[:], exp_group[:], AX.X, ALU.add))
                step(nc.vector.reciprocal(p_group[:], group_sum[:]))
                step(nc.vector.tensor_scalar(w_first[:], w_second[:], 1.0, None, ALU.add))
                step(nc.vector.reciprocal(w_first[:], w_first[:]))
                step(nc.vector.tensor_tensor(k.pick_weight[:, 0], w_first[:], p_group[:], ALU.mult))
                step(nc.vector.tensor_tensor(k.pick_weight[:, 1], w_second[:], k.pick_weight[:, 0], ALU.mult))
                for choice, hot in enumerate((hot1, hot2)):
                    for g in range(GROUPS):
                        step(nc.vector.tensor_tensor(k.pick[:, choice, :, g * PER_GROUP:(g + 1) * PER_GROUP], hot[:],
                                                     group[:, :, g:g + 1].broadcast_to([P, TT, PER_GROUP]), ALU.mult))


def plan_stage(k):
    nc = k.nc
    picks_ready, counted, slots_ready, zeroed, cleared, scattered = (
        k.sem(f"plan_{s}") for s in ("picks_ready", "counted", "slots_ready", "zeroed", "cleared", "scattered"))
    loaded, earlier_loads = stage_loads(k, 4)
    T, E = EXPERT_TILES, EXPERTS
    PAD = E // 2
    with ExitStack() as scope:
        def sb(name, shape, kind=F32):
            return scope.enter_context(nc.sbuf_tensor(name, shape, kind))

        before, iota, token = sb("before", [P, P]), sb("tile_iota", [P, P]), sb("token", [P, TT])
        both, ranked, based = sb("both_picks", [P, TT, E]), sb("ranked", [P, 2, TT, E]), sb("based", [P, 2, TT, E])
        count, tiles, base = sb("expert_count", [P, E]), sb("expert_tiles", [P, E]), sb("expert_base", [P, E])
        sums = [sb(f"tile_sums{i}", [P, PAD + E]) for i in range(2)]
        passed, owner = sb("passed", [P, T, E]), sb("tile_owner", [P, T])
        rank, first, carry, slot_f = (sb(n, [P, 2, TT]) for n in ("pick_rank", "pick_base", "pick_carry", "pick_slot_f"))
        token_u, place_u, zero = sb("token_u", [P, TT], U32), sb("pick_place", [P, 2, TT], U32), sb("no_token", [P, T], U32)
        with nc.Block(no_gpsimd_drain=True) as block:
            @block.sync
            def _(sp):
                for part, name in ((before, "before"), (iota, "iota"), (token, "token")):
                    sp.dma_start(part[:], k.d[name]).then_inc(loaded, 16)
                sp.wait_ge(zeroed, 1)
                sp.dma_start(k.token_dram.rearrange("(p t) o -> p (t o)", p=P), zero[:]).then_inc(cleared, 16)
                sp.wait_ge(scattered, 16 * 2 * TT)
                sp.dma_start(k.slot_token[:], k.token_dram.rearrange("(p t) o -> p (t o)", p=P)).then_inc(loaded, 16)
                sp.wait_ge(loaded, earlier_loads + 64)

            @block.gpsimd
            def _(pool):
                pool.wait_ge(cleared, 16)
                pool.wait_ge(slots_ready, 1)
                for choice in range(2):
                    for t in range(TT):
                        pool.indirect_dma_start(k.token_dram, bass.IndirectOffsetOnAxis(ap=place_u[:, choice, t:t + 1], axis=0),
                                                token_u[:, t:t + 1], None).then_inc(scattered, 16)
                pool.wait_ge(scattered, 16 * 2 * TT)

            @block.tensor
            def _(pe):
                pe.wait_ge(loaded, earlier_loads + 48)
                pe.wait_ge(picks_ready, 1)
                for t in range(TT):
                    for i in range(t + 1):
                        nc.tensor.matmul(k.psum[:, 0, t * E:(t + 1) * E], k.ones[:] if i < t else before[:], both[:, i],
                                         start=i == 0, stop=i == t)
                for i in range(TT):
                    mm = nc.tensor.matmul(k.psum[:, 1, 0:E], k.ones[:], both[:, i], start=i == 0, stop=i == TT - 1)
                mm.then_inc(counted, 1)

            @block.vector
            def _(dve):
                step = k.vstep
                nc.vector.memset(zero[:], 0).then_inc(zeroed, 1)
                nc.vector.tensor_tensor(both[:], k.pick[:, 0], k.pick[:, 1], ALU.add).then_inc(picks_ready, 1)
                for part in sums:
                    step(nc.vector.memset(part[:, 0:PAD], 0.0))
                dve.wait_ge(loaded, earlier_loads + 48)
                step(nc.vector.tensor_copy(token_u[:], token[:]))
                dve.wait_ge(counted, 1)
                step(nc.vector.tensor_copy(count[:], k.psum[:, 1, 0:E]))
                step(nc.vector.tensor_scalar(tiles[:], count[:], 0.0, None, ALU.is_gt))
                for m in range(1, TT):
                    step(nc.vector.scalar_tensor_tensor(tiles[:], count[:], float(m * P), tiles[:], ALU.is_gt, ALU.add))
                step(nc.vector.tensor_copy(sums[0][:, PAD:], tiles[:]))
                shift, at = 1, 0
                while shift < E:
                    step(nc.vector.tensor_tensor(sums[1 - at][:, PAD:], sums[at][:, PAD:], sums[at][:, PAD - shift:PAD - shift + E], ALU.add))
                    shift, at = 2 * shift, 1 - at
                total = sums[at][:, PAD:]
                step(nc.vector.tensor_tensor(base[:], total, tiles[:], ALU.subtract))
                step(nc.vector.tensor_tensor(passed[:], total.unsqueeze(1).broadcast_to([P, T, E]),
                                             iota[:, 0:T].unsqueeze(2).broadcast_to([P, T, E]), ALU.is_le))
                step(nc.vector.tensor_reduce(owner[:], passed[:], AX.X, ALU.add))
                step(nc.vector.tensor_scalar(owner[:], owner[:], float(E - 1), float(P), ALU.min, ALU.mult))
                step(nc.vector.tensor_scalar(owner[:], owner[:], token[:, 0:1], None, ALU.add))
                step(nc.vector.tensor_copy(k.expert_row[:], owner[:]))
                ranks = k.psum[:, 0, 0:TT * E].rearrange("p (t e) -> p t e", e=E)
                for choice in range(2):
                    step(nc.vector.tensor_tensor(ranked[:, choice], k.pick[:, choice], ranks, ALU.mult))
                    step(nc.vector.tensor_tensor(based[:, choice], k.pick[:, choice], base[:].unsqueeze(1).broadcast_to([P, TT, E]),
                                                 ALU.mult))
                step(nc.vector.tensor_reduce(rank[:], ranked[:], AX.X, ALU.add))
                step(nc.vector.tensor_reduce(first[:], based[:], AX.X, ALU.add))
                step(nc.vector.scalar_tensor_tensor(slot_f[:], first[:], float(P), rank[:], ALU.mult, ALU.add))
                step(nc.vector.tensor_copy(k.pick_slot[:], slot_f[:]))
                step(nc.vector.tensor_scalar(carry[:], rank[:], float(P), None, ALU.is_ge))
                for m in range(2, TT):
                    step(nc.vector.scalar_tensor_tensor(carry[:], rank[:], float(m * P), carry[:], ALU.is_ge, ALU.add))
                step(nc.vector.scalar_tensor_tensor(rank[:], carry[:], float(-P), rank[:], ALU.mult, ALU.add))
                step(nc.vector.tensor_tensor(first[:], first[:], carry[:], ALU.add))
                step(nc.vector.scalar_tensor_tensor(slot_f[:], rank[:], float(T), first[:], ALU.mult, ALU.add))
                nc.vector.tensor_copy(place_u[:], slot_f[:]).then_inc(slots_ready, 1)


def moe_stage(k):
    nc = k.nc
    x_turned, x_ready, in_done, silu_done, a_ready, a_turned, at_ready, down_done, y_ready = (
        k.sem(f"moe_{s}") for s in ("x_turned", "x_ready", "in_done", "silu_done", "a_ready", "a_turned", "at_ready", "down_done", "y_ready"))
    x_loaded, in_loaded, down_loaded, y_stored = (
        [k.sem(f"moe_{s}{i}") for i in range(2)] for s in ("x_loaded", "in_loaded", "down_loaded", "y_stored"))
    T = EXPERT_TILES
    loops = (T - 3) // 2
    with ExitStack() as scope:
        def sb(name, shape):
            return scope.enter_context(nc.sbuf_tensor(name, shape, F32))

        w_in, w_down = sb("w_expert_in", [P, 2, KC, 2 * FF]), sb("w_expert_down", [P, 2, 2, D])
        x_rows, x_turn = sb("x_rows", [P, 2, D]), sb("x_turn", [P, 2, KC, P])
        silu, a, a_turn, y_rows = sb("moe_silu", [P, 2, FF]), sb("moe_a", [P, 2, FF]), sb("a_turn", [P, 2, P]), sb("y_rows", [P, 2, D])
        x_banks, in_banks, a_bank, y_banks = (0, 1), (2, 3), 4, (5, 6)
        with nc.Block(no_gpsimd_drain=True) as block:
            @block.gpsimd
            def _(pool):
                def gather(out, table, rows, m, done):
                    pool.indirect_dma_start(out, None, table, bass.IndirectOffsetOnAxis(ap=rows[:, m:m + 1], axis=0)).then_inc(done, 16)

                def tokens(m):
                    if m >= 2:
                        pool.wait_ge(x_turned, m - 1)
                    gather(x_rows[:, m % 2], k.h_dram, k.slot_token, m, x_loaded[m % 2])

                def gate_up(m):
                    if m >= 2:
                        pool.wait_ge(in_done, m - 1)
                    gather(w_in[:, m % 2].rearrange("p c n -> p (c n)"), k.d["experts_in"], k.expert_row, m, in_loaded[m % 2])

                def down(m):
                    if m >= 2:
                        pool.wait_ge(down_done, m - 1)
                    gather(w_down[:, m % 2].rearrange("p c n -> p (c n)"), k.d["experts_down"], k.expert_row, m, down_loaded[m % 2])

                tokens(0)
                gate_up(0)
                for m in range(1, T):
                    tokens(m)
                    gate_up(m)
                    down(m - 1)
                down(T - 1)

            @block.tensor
            def _(pe):
                def turn_x(m, r):
                    pe.wait_ge(x_loaded[r % 2], turns(m, r))
                    if r > 0:
                        pe.wait_ge(x_ready, m)
                    for c in range(KC):
                        at = (c % 4) * P
                        mm = nc.tensor.transpose(k.psum[:, x_banks[c // 4], at:at + P], x_rows[:, r % 2, c * P:(c + 1) * P], k.ident[:])
                    mm.then_inc(x_turned, 1)

                def gate_up(m, r):
                    pe.wait_ge(x_ready, m + 1)
                    pe.wait_ge(in_loaded[r % 2], turns(m, r))
                    if r >= 2:
                        pe.wait_ge(a_ready, m - 1)
                    for c in range(KC):
                        mm = nc.tensor.matmul(k.psum[:, in_banks[r % 2]], x_turn[:, r % 2, c], w_in[:, r % 2, c], start=c == 0, stop=c == KC - 1)
                    mm.then_inc(in_done, 1)

                def turn_a(n, r):
                    pe.wait_ge(a_ready, n + 1)
                    if r > 0:
                        pe.wait_ge(at_ready, n)
                    for c in range(2):
                        mm = nc.tensor.transpose(k.psum[:, a_bank, c * P:(c + 1) * P], a[:, r % 2, c * P:(c + 1) * P], k.ident[:])
                    mm.then_inc(a_turned, 1)

                def down(n, r):
                    pe.wait_ge(at_ready, n + 1)
                    pe.wait_ge(down_loaded[r % 2], turns(n, r))
                    if r > 0:
                        pe.wait_ge(y_ready, n)
                    for half, bank in enumerate(y_banks):
                        for c in range(2):
                            mm = nc.tensor.matmul(k.psum[:, bank], a_turn[:, c], w_down[:, r % 2, c, half * BANK:(half + 1) * BANK],
                                                  start=c == 0, stop=c == 1)
                    mm.then_inc(down_done, 1)

                def step(n, r):
                    if r + 1 < T:
                        gate_up(n + 1, r + 1)
                    turn_a(n, r)
                    if r + 2 < T:
                        turn_x(n + 2, r + 2)
                    down(n, r)

                turn_x(0, 0)
                turn_x(1, 1)
                gate_up(0, 0)
                step(0, 0)
                with pe.Fori(0, loops) as g:
                    for r in (1, 2):
                        step(2 * g + r, r)
                for n in range(2 * loops + 1, T):
                    step(n, n)

            @block.scalar
            def _(act):
                def copy_x(m, r):
                    act.wait_ge(x_turned, m + 1)
                    if r >= 2:
                        act.wait_ge(in_done, m - 1)
                    for i in range(2):
                        ins = nc.scalar.activation(x_turn[:, r % 2, 4 * i:4 * i + 4].rearrange("p c n -> p (c n)"), k.psum[:, x_banks[i]], ACT.Copy)
                    ins.then_inc(x_ready, 1)

                def gate(m, r):
                    act.wait_ge(in_done, m + 1)
                    if r >= 2:
                        act.wait_ge(a_ready, m - 1)
                    nc.scalar.activation(silu[:, r % 2], k.psum[:, in_banks[r % 2], 0:FF], ACT.Silu).then_inc(silu_done, 1)

                def step(n, r):
                    if r + 1 < T:
                        gate(n + 1, r + 1)
                    act.wait_ge(a_turned, n + 1)
                    if r > 0:
                        act.wait_ge(down_done, n)
                    nc.scalar.activation(a_turn[:].rearrange("p c n -> p (c n)"), k.psum[:, a_bank, 0:FF], ACT.Copy).then_inc(at_ready, 1)
                    if r + 2 < T:
                        copy_x(n + 2, r + 2)

                copy_x(0, 0)
                copy_x(1, 1)
                gate(0, 0)
                step(0, 0)
                with act.Fori(0, loops) as g:
                    for r in (1, 2):
                        step(2 * g + r, r)
                for n in range(2 * loops + 1, T):
                    step(n, n)

            @block.vector
            def _(dve):
                def up(m, r):
                    dve.wait_ge(silu_done, m + 1)
                    if r >= 2:
                        dve.wait_ge(a_turned, m - 1)
                    nc.vector.tensor_tensor(a[:, r % 2], silu[:, r % 2], k.psum[:, in_banks[r % 2], FF:2 * FF], ALU.mult).then_inc(a_ready, 1)

                def step(n, r):
                    if r + 1 < T:
                        up(n + 1, r + 1)
                    dve.wait_ge(down_done, n + 1)
                    if r >= 2:
                        dve.wait_ge(y_stored[r % 2], turns(n, r) - 16)
                    for half, bank in enumerate(y_banks):
                        ins = nc.vector.tensor_copy(y_rows[:, r % 2, half * BANK:(half + 1) * BANK], k.psum[:, bank])
                    ins.then_inc(y_ready, 1)

                up(0, 0)
                step(0, 0)
                step(1, 1)
                step(2, 2)
                with dve.Fori(1, loops) as g:
                    for r in (1, 2):
                        step(2 * g + r, r + 2)
                for n in range(2 * loops + 1, T):
                    step(n, n)

            @block.sync
            def _(sp):
                def store(n, r):
                    sp.wait_ge(y_ready, n + 1)
                    sp.dma_start(k.y_dram.rearrange("(n p) d -> n p d", p=P)[bass.ds(n, 1)].rearrange("n p d -> p (n d)"),
                                 y_rows[:, r % 2]).then_inc(y_stored[r % 2], 16)

                with sp.Fori(0, T // 2) as g:
                    for r in range(2):
                        store(2 * g + r, r)
                if T % 2:
                    store(T - 1, T - 1)
                for i in range(2):
                    sp.wait_ge(y_stored[i], 16 * ((T + 1 - i) // 2))


def turns(n, r):
    return (n - r % 2) * 8 + 16


def moe_out_stage(k):
    nc = k.nc
    summed, turned, added = (k.sem(f"moe_out_{s}") for s in ("summed", "turned", "added"))
    got = [k.sem(f"moe_out_got{i}") for i in range(2)]
    gate = k.mod1[:, GATE_2:GATE_2 + KC]
    with ExitStack() as scope:
        picked, y_sum = (scope.enter_context(nc.sbuf_tensor(n, shape, F32)) for n, shape in (
            ("picked_rows", [P, 2, 2, D]), ("y_sum", [P, 2, D])))
        with nc.Block(no_gpsimd_drain=True) as block:
            @block.gpsimd
            def _(pool):
                for t in range(TT):
                    if t >= 2:
                        pool.wait_ge(summed, t - 1)
                    for choice in range(2):
                        pool.indirect_dma_start(picked[:, t % 2, choice], None, k.y_dram, bass.IndirectOffsetOnAxis(
                            ap=k.pick_slot[:, choice, t:t + 1], axis=0)).then_inc(got[t % 2], 16)

            @block.vector
            def _(dve):
                def add(t):
                    for c in range(KC):
                        dve.wait_ge(turned, 2 * t + c // 4 + 1)
                        part = k.x[:, c, t * P:(t + 1) * P]
                        nc.vector.scalar_tensor_tensor(part, k.psum[:, 2 * (t % 2) + c // 4, (c % 4) * P:(c % 4 + 1) * P], gate[:, c:c + 1],
                                                       part, ALU.mult, ALU.add).then_inc(added, 1)

                for t in range(TT):
                    dve.wait_ge(got[t % 2], 32 * (t // 2 + 1))
                    if t >= 2:
                        dve.wait_ge(turned, 2 * (t - 1))
                    k.vstep(nc.vector.tensor_scalar(y_sum[:, t % 2], picked[:, t % 2, 0], k.pick_weight[:, 0, t:t + 1], None, ALU.mult))
                    nc.vector.scalar_tensor_tensor(y_sum[:, t % 2], picked[:, t % 2, 1], k.pick_weight[:, 1, t:t + 1], y_sum[:, t % 2],
                                                   ALU.mult, ALU.add).then_inc(summed, 1)
                    if t > 0:
                        add(t - 1)
                add(TT - 1)

            @block.tensor
            def _(pe):
                for t in range(TT):
                    pe.wait_ge(summed, t + 1)
                    if t >= 2:
                        pe.wait_ge(added, KC * (t - 1))
                    for c in range(KC):
                        mm = nc.tensor.transpose(k.psum[:, 2 * (t % 2) + c // 4, (c % 4) * P:(c % 4 + 1) * P],
                                                 y_sum[:, t % 2, c * P:(c + 1) * P], k.ident[:])
                        if c % 4 == 3:
                            mm.then_inc(turned, 1)


def load_context_stage(k):
    nc = k.nc
    with nc.Block(no_gpsimd_drain=True) as block:
        @block.sync
        def _(sp):
            sp.dma_start(k.rope[:], k.d["rope"]).then_inc(k.rope_loaded, 16)
            sp.dma_start(k.swap[:], k.d["swap"]).then_inc(k.rope_loaded, 16)
            sp.wait_ge(k.ctx_loaded, 16)


def qk_stage(k):
    nc = k.nc
    done, copied, swapped, rotated, ctx_done, ctx_copied = (
        k.sem(f"qk_{s}") for s in ("done", "copied", "swapped", "rotated", "ctx_done", "ctx_copied"))
    first = FIRST["qk2"]
    n = 2 * KC
    units, mod_bank, first_unit = len(LATE_SPANS), 6, sum(len(vectors) for vectors in EARLY_SPANS)
    mod_tiles = 2 * units

    def summed(c):
        return min(mod_tiles, 4 * max(0, c - 1) // 3)

    assert summed(n - 1) == mod_tiles
    with ExitStack() as scope:
        spare = k.h[:].rearrange("p c n -> p (c n)")[:, KC * CTX:].rearrange("p (s b n) -> p s b n", s=2, b=2)
        raw, with_cos = spare[:, 0], spare[:, 1]
        with_sin = scope.enter_context(nc.sbuf_tensor("qk_with_sin", [P, 2, SEQ], F32))

        def used(i):
            return (done, 2 * (i + 1)) if i < KC // 2 else (ctx_done, 2 * (i - KC // 2 + 1))

        with nc.Block(no_gpsimd_drain=True) as block:
            @block.sync
            def _(sp):
                stream(k, sp, first, 1)
                sp.wait_ge(k.moved, 16 * k.moves)
                for i in range(MOD_SLOTS):
                    load_mod_tile(k, sp, EARLY_MOD_TILES + i)
                for i in range(1, KC):
                    stream(k, sp, first + i, 1)
                    for j in range(MOD_SLOTS + 3 * (i - 1), min(mod_tiles, MOD_SLOTS + 3 * i)):
                        load_mod_tile(k, sp, EARLY_MOD_TILES + j)

            @block.gpsimd
            def _(pool):
                low_parts(k, pool, first, KC)

            @block.tensor
            def _(pe):
                def swap(c):
                    pe.wait_ge(copied, c + 1)
                    if c >= 2:
                        pe.wait_ge(rotated, c - 1)
                    nc.tensor.matmul(k.psum[:, 2 + c % 2], k.swap[:], raw[:, c % 2], start=True, stop=True).then_inc(swapped, 1)

                pe.wait_ge(k.rope_loaded, 32)
                for c in range(n):
                    if c >= 2:
                        pe.wait_ge(copied, c - 1)
                    chunk_products(k, pe, k.psum[:, c % 2], first, c, (k.h_hi, k.h_lo), done)
                    if c >= KC:
                        i = c - KC
                        if i >= 2:
                            pe.wait_ge(ctx_copied, i - 1)
                        chunk_products(k, pe, k.psum[:, 4 + i % 2, 0:CTX], first, c, (k.ctx_hi, k.ctx_lo), ctx_done)
                    if c >= 1:
                        swap(c - 1)
                    if c >= 2:
                        for u in range(summed(c - 3) // 2, summed(c - 2) // 2):
                            mod_turn(k, pe, LATE_SPANS, first_unit, u, mod_bank)
                swap(n - 1)

            @block.scalar
            def _(act):
                act.wait_ge(k.moved, 16 * k.moves)
                for c in range(n):
                    if c % 2 == 0:
                        next_high(k, act, first, c // 2, used)
                    act.wait_ge(done, c + 1)
                    if c >= 2:
                        act.wait_ge(swapped, c - 1)
                        act.wait_ge(rotated, c - 1)
                    nc.scalar.activation(raw[:, c % 2], k.psum[:, c % 2], ACT.Copy, scale=DH ** -0.5 if c < KC else 1.0).then_inc(
                        copied, 1)
                    if c >= KC:
                        i = c - KC
                        act.wait_ge(ctx_done, i + 1)
                        nc.scalar.activation(k.k2[:, i, 0:CTX], k.psum[:, 4 + i % 2, 0:CTX], ACT.Copy).then_inc(ctx_copied, 1)

            @block.vector
            def _(dve):
                dve.wait_ge(k.moved, 16 * k.moves)
                dve.wait_ge(k.rope_loaded, 32)
                for c in range(n):
                    target = k.q2[:, c] if c < KC else k.k2[:, c - KC, CTX:KEYS]
                    dve.wait_ge(copied, c + 1)
                    nc.vector.tensor_tensor(with_cos[:, c % 2], raw[:, c % 2], k.rope[:, 0], ALU.mult)
                    dve.wait_ge(swapped, c + 1)
                    k.vstep(nc.vector.tensor_tensor(with_sin[:, c % 2], k.psum[:, 2 + c % 2], k.rope[:, 1], ALU.mult))
                    nc.vector.tensor_tensor(target, with_cos[:, c % 2], with_sin[:, c % 2], ALU.add).then_inc(rotated, 1)
                    for i in range(summed(c - 1), summed(c)):
                        mod_sum(k, dve, LATE_SPANS, EARLY_MOD_TILES, first_unit, i)
                dve.wait_ge(k.mod_turned, first_unit + units)
                k.vstep(nc.vector.tensor_tensor(k.mod2[:, 0, GATE_1:N_MOD], k.psum[:, mod_bank, 0:4 * KC],
                                                k.ada_vecs[:, ADA_B2 + GATE_1:ADA_B2 + N_MOD], ALU.add))
                fold(k, k.mod2[:, 0, SCALE_2:SCALE_2 + KC], G_PRE_FFN, 1.0)
                fold(k, k.mod2[:, 0, GATE_1:GATE_1 + KC], G_POST_MIX, 0.0)
                fold(k, k.mod2[:, 0, GATE_2:GATE_2 + KC], G_POST_FFN, 0.0)


def values_stage(k):
    nc = k.nc
    done, copied = k.sem("v2_done"), k.sem("v2_copied")
    first = FIRST["v2"]
    def used(i):
        return (done, KT * (i + 1))

    with nc.Block(no_gpsimd_drain=True) as block:
        @block.sync
        def _(sp):
            stream(k, sp, first, 4)

        @block.gpsimd
        def _(pool):
            low_parts(k, pool, first, 4)

        @block.tensor
        def _(pe):
            def tokens(t, kc):
                if t >= CTX // P:
                    return token_parts(k, t - CTX // P, kc)
                return k.ctx_hi[:, kc, t * P:(t + 1) * P], k.ctx_lo[:, kc, t * P:(t + 1) * P]

            for half in range(2):
                def free(t):
                    if half * KT + t >= 8:
                        pe.wait_ge(copied, half * KT + t - 7)

                row_products(k, pe, [k.psum[:, (half * KT + t) % 8] for t in range(KT)], first + 2 * half, tokens, done, free)

        @block.scalar
        def _(act):
            for u in range(2 * KT):
                if u % KT == 0:
                    for i in range(2):
                        next_high(k, act, first, 2 * (u // KT) + i, used)
                act.wait_ge(done, KT * (u // KT + 1) + u + 1)
                nc.scalar.activation(k.v2[:, u % KT, (u // KT) * BANK:(u // KT + 1) * BANK], k.psum[:, u % 8], ACT.Copy).then_inc(
                    copied, 1)


def sgu_projection_stage(k):
    nc = k.nc
    done, copied, rows_done = k.sem("z_done"), k.sem("z_copied"), k.sem("z_rows_done")
    first = FIRST["z2"]
    def used(i):
        return (done, 2 * (i + 1)) if i < 4 else (rows_done, TT * (i - 4 + 1))

    with nc.Block(no_gpsimd_drain=True) as block:
        @block.sync
        def _(sp):
            stream(k, sp, first, 8)

        @block.gpsimd
        def _(pool):
            low_parts(k, pool, first, 8)

        @block.tensor
        def _(pe):
            for c in range(KC):
                if c >= 4:
                    pe.wait_ge(copied, c - 3)
                chunk_products(k, pe, k.psum[:, c % 4], first, c, (k.h_hi, k.h_lo), done)
            for half in range(2):
                row_products(k, pe, [k.psum[:, (4 + half * TT + t) % 8] for t in range(TT)], first + 4 + 2 * half,
                             lambda t, kc: token_parts(k, t, kc), rows_done,
                             lambda t: pe.wait_ge(copied, KC + t + half * TT - 7))

        @block.scalar
        def _(act):
            for c in range(KC):
                if c % 2 == 0:
                    next_high(k, act, first, c // 2, used)
                act.wait_ge(done, c + 1)
                nc.scalar.activation(k.u[:, c], k.psum[:, c % 4], ACT.Gelu).then_inc(copied, 1)
            for u in range(2 * TT):
                if u % TT == 0:
                    for i in range(2):
                        next_high(k, act, first, 4 + 2 * (u // TT) + i, used)
                act.wait_ge(rows_done, TT * (u // TT + 1) + u + 1)
                nc.scalar.activation(k.vz[:, u % TT, (u // TT) * BANK:(u // TT + 1) * BANK], k.psum[:, (4 + u) % 8],
                                     ACT.Gelu).then_inc(copied, 1)


def sgu_stage(k):
    nc = k.nc
    normed, mixed, used, at_scalar = (k.sem(f"sgu_{s}") for s in ("normed", "mixed", "used", "scalar"))
    loaded, earlier_loads = stage_loads(k, 4)
    with ExitStack() as scope:
        def sb(name, shape):
            return scope.enter_context(nc.sbuf_tensor(name, shape, F32))

        w_s, b_s = sb("sgu_w", [P, SGU_GROUPS, P]), sb("sgu_b", [P, SGU_GROUPS, P])
        ln = sb("sgu_ln", [P, 2, D])
        stats, moments = sb("sgu_stats", [P, TT, 2, 6]), sb("sgu_moments", [P, TT, 2])
        std, with_bias = sb("sgu_std", [P, TT]), sb("sgu_with_bias", [P, 2, SEQ])
        with nc.Block(no_gpsimd_drain=True) as block:
            @block.sync
            def _(sp):
                sp.dma_start(ln[:, 0], k.d["ln_g"][0].partition_broadcast(P)).then_inc(loaded, 16)
                sp.dma_start(ln[:, 1], k.d["ln_b"][0].partition_broadcast(P)).then_inc(loaded, 16)
                sp.dma_start(b_s[:].rearrange("p g n -> p (g n)"), k.d["sgu_b"][0].partition_broadcast(P)).then_inc(loaded, 16)
                sp.dma_start(w_s[:], k.d["sgu_w"]).then_inc(loaded, 16)

            @block.vector
            def _(dve):
                step = k.vstep
                for t in range(TT):
                    for i in range(2):
                        step(nc.vector.bn_stats(stats[:, t, i], k.vz[:, t, i * BANK:(i + 1) * BANK]))
                    step(nc.vector.bn_aggr(moments[:, t], stats[:, t].rearrange("p i n -> p (i n)")))
                nc.vector.tensor_copy(std[:], moments[:, :, 1]).then_inc(normed, 1)
                dve.wait_ge(at_scalar, 1)
                step(nc.vector.reciprocal(std[:], std[:]))
                dve.wait_ge(loaded, earlier_loads + 64)
                for t in range(TT):
                    step(nc.vector.tensor_scalar(k.vz[:, t], k.vz[:, t], moments[:, t, 0:1], std[:, t:t + 1], ALU.subtract, ALU.mult))
                for t in range(TT):
                    step(nc.vector.tensor_tensor(k.vz[:, t], k.vz[:, t], ln[:, 0], ALU.mult))
                for t in range(TT):
                    nc.vector.tensor_tensor(k.vz[:, t], k.vz[:, t], ln[:, 1], ALU.add).then_inc(normed, 1)
                for g in range(SGU_GROUPS):
                    dve.wait_ge(mixed, g + 1)
                    part = with_bias[:, g % 2].rearrange("p (t n) -> p t n", t=TT)
                    k.vstep(nc.vector.tensor_tensor(part, k.psum[:, g % 4].rearrange("p (t n) -> p t n", t=TT),
                                                    b_s[:, g].unsqueeze(1).broadcast_to([P, TT, P]), ALU.add))
                    nc.vector.tensor_tensor(k.u[:, g], k.u[:, g], with_bias[:, g % 2], ALU.mult).then_inc(used, 1)

            @block.scalar
            def _(act):
                act.wait_ge(normed, 1)
                nc.scalar.activation(std[:], std[:], ACT.Sqrt, bias=k.eps[:, 1:2]).then_inc(at_scalar, 1)

            @block.tensor
            def _(pe):
                pe.wait_ge(loaded, earlier_loads + 64)
                pe.wait_ge(normed, 1 + TT)
                for g in range(SGU_GROUPS):
                    if g >= 4:
                        pe.wait_ge(used, g - 3)
                    for t in range(TT):
                        mm = nc.tensor.matmul(k.psum[:, g % 4, t * P:(t + 1) * P], k.vz[:, t, g * P:(g + 1) * P], w_s[:, g],
                                              start=True, stop=True)
                    mm.then_inc(mixed, 1)


def diff_attention_stage(k):
    nc = k.nc
    square_done, scored, maxed, exped, mixed, turned, turned_copied, weighed, out_copied, lam_step = (
        k.sem(f"diff_{s}") for s in ("square_done", "scored", "maxed", "exped", "mixed", "turned", "turned_copied", "weighed", "out_copied",
                                     "lam_step"))
    pair_high, pair_low = k.sem("diff_pair_high"), k.sem("diff_pair_low")
    units = [(i, h) for h in range(DIFF_HEADS) for i in range(TT)]
    pairs_hi, pairs_lo = (part[:].rearrange("p c n -> p (c n)")[:, 0:2 * (KEYS + SEQ)].rearrange("p (b n) -> p b n", b=2)
                          for part in (k.h_hi, k.h_lo))

    def sources(h):
        return (k.k2[:, h], slice(0, KEYS)), (k.q2[:, h], slice(KEYS, KEYS + SEQ))

    n = len(units)
    DEEP = 3
    HALF_KEYS = KEYS // 2
    with ExitStack() as scope:
        def sb(name, shape):
            return scope.enter_context(nc.sbuf_tensor(name, shape, F32))

        probs, minus, probs_t = sb("diff_probs", [P, DEEP, 2, KEYS]), sb("diff_minus", [P, KEYS]), sb("diff_probs_t", [P, 2, KEYS])
        neg_max, total, inv = sb("diff_neg_max", [P, 2 * n]), sb("diff_total", [P, 2 * n]), sb("diff_inv", [P, 2 * n])
        squared = sb("diff_squared", [P, 2, P])
        lam_prod, lam_exp, neg_lam = sb("lam_prod", [P, 2]), sb("lam_exp", [P, 2]), sb("neg_lam", [P, 1])
        with nc.Block(no_gpsimd_drain=True) as block:
            @block.tensor
            def _(pe):
                def score(u, j):
                    i, h = units[u]
                    v = 2 * u + j
                    if v >= 2:
                        pe.wait_ge(exped, v - 1)
                    pe.wait_ge(pair_low, 2 * (h + 1))
                    hi, lo = (head_half(part[:, h % 2], j) for part in (pairs_hi, pairs_lo))
                    queries = slice(KEYS + i * P, KEYS + (i + 1) * P)
                    split_products(k, k.psum[:, 2 * j, :], hi[:, queries], lo[:, queries], hi[:, 0:BANK], lo[:, 0:BANK], True, True)
                    split_products(k, k.psum[:, 2 * j + 1, 0:KEYS - BANK], hi[:, queries], lo[:, queries], hi[:, BANK:KEYS],
                                   lo[:, BANK:KEYS], True, True).then_inc(scored, 1)

                def turn(u):
                    pe.wait_ge(mixed, u + 1)
                    for half in range(2):
                        if u >= 1:
                            pe.wait_ge(turned_copied, 2 * u + half - 1)
                        for s in range(3):
                            at = half * HALF_KEYS + s * P
                            mm = nc.tensor.transpose(k.psum[:, 4 + half, s * P:(s + 1) * P], probs[:, u % DEEP, 0, at:at + P], k.ident[:])
                        mm.then_inc(turned, 1)

                def weigh(u):
                    h = units[u][1]
                    pe.wait_ge(turned_copied, 2 * u + 2)
                    if u >= 2:
                        pe.wait_ge(out_copied, u - 1)
                    for s in range(KT):
                        mm = nc.tensor.matmul(k.psum[:, 6 + u % 2, 0:P], probs_t[:, u % 2, s * P:(s + 1) * P],
                                              k.v2[:, s, h * P:(h + 1) * P], start=s == 0, stop=s == KT - 1)
                    mm.then_inc(weighed, 1)

                pe.wait_ge(lam_step, 1)
                nc.tensor.matmul(k.psum[:, 7, 0:2], k.ones[:], lam_prod[:], start=True, stop=True).then_inc(lam_step, 1)
                pe.wait_ge(lam_step, 3)
                for t in range(n + DEEP):
                    if t < n:
                        score(t, 0)
                        score(t, 1)
                    if 2 <= t < n + 2:
                        turn(t - 2)
                    if t >= DEEP:
                        weigh(t - DEEP)

            @block.vector
            def _(dve):
                step = k.vstep

                def maxima(u):
                    for j in range(2):
                        v = 2 * u + j
                        dve.wait_ge(scored, v + 1)
                        row = k.psum[:, 2 * j:2 * j + 2].rearrange("p b n -> p (b n)")[:, 0:KEYS]
                        nc.vector.tensor_reduce(neg_max[:, v:v + 1], row, AX.X, ALU.max, negate=True).then_inc(maxed, 1)

                def mix(u):
                    dve.wait_ge(exped, 2 * u + 2)
                    step(nc.vector.reciprocal(inv[:, 2 * u:2 * u + 2], total[:, 2 * u:2 * u + 2]))
                    step(nc.vector.tensor_tensor(inv[:, 2 * u + 1:2 * u + 2], inv[:, 2 * u + 1:2 * u + 2], neg_lam[:], ALU.mult))
                    step(nc.vector.tensor_scalar(minus[:], probs[:, u % DEEP, 1], inv[:, 2 * u + 1:2 * u + 2], None, ALU.mult))
                    nc.vector.scalar_tensor_tensor(probs[:, u % DEEP, 0], probs[:, u % DEEP, 0], inv[:, 2 * u:2 * u + 1], minus[:],
                                                   ALU.mult, ALU.add).then_inc(mixed, 1)

                def copy_out(u):
                    i, h = units[u]
                    dve.wait_ge(weighed, u + 1)
                    nc.vector.tensor_copy(k.o[:, i, h * P:(h + 1) * P], k.psum[:, 6 + u % 2, 0:P]).then_inc(out_copied, 1)

                step(nc.vector.memset(lam_prod[:], 0.0))
                nc.vector.tensor_tensor(lam_prod[0:DH], k.vecs[0:DH, LAMBDA:LAMBDA + 4:2], k.vecs[0:DH, LAMBDA + 1:LAMBDA + 4:2],
                                        ALU.mult).then_inc(lam_step, 1)
                dve.wait_ge(lam_step, 3)
                step(nc.vector.tensor_tensor(neg_lam[:], lam_exp[:, 1:2], lam_exp[:, 0:1], ALU.subtract))
                step(nc.vector.tensor_scalar(neg_lam[:], neg_lam[:], LAMBDA_INIT, None, ALU.subtract))
                for t in range(n + DEEP + 1):
                    if t < n:
                        maxima(t)
                    if 1 <= t <= n:
                        mix(t - 1)
                    if t > DEEP:
                        copy_out(t - DEEP - 1)

            @block.gpsimd
            def _(pool):
                for h in range(DIFF_HEADS):
                    for s, (source, at_columns) in enumerate(sources(h)):
                        pool.wait_ge(pair_high, 2 * h + s + 1)
                        nc.gpsimd.tensor_tensor(pairs_lo[:, h % 2, at_columns], source, pairs_hi[:, h % 2, at_columns].bitcast(F32),
                                                ALU.subtract).then_inc(pair_low, 1)

            @block.scalar
            def _(act):
                def split(h):
                    if h >= 2:
                        act.wait_ge(scored, 2 * TT * (h - 1))
                    for source, at_columns in sources(h):
                        nc.scalar.activation(pairs_hi[:, h % 2, at_columns], source, ACT.Copy).then_inc(pair_high, 1)

                def exp(u):
                    for j in range(2):
                        v = 2 * u + j
                        act.wait_ge(maxed, v + 1)
                        if u >= DEEP:
                            act.wait_ge(turned, 2 * (u - DEEP + 1))
                        row = k.psum[:, 2 * j:2 * j + 2].rearrange("p b n -> p (b n)")[:, 0:KEYS]
                        nc.scalar.activation(probs[:, u % DEEP, j], row, ACT.Exp, bias=neg_max[:, v:v + 1],
                                             accum_out=total[:, v:v + 1]).then_inc(exped, 1)

                def copy_turned(u):
                    for half in range(2):
                        act.wait_ge(turned, 2 * u + half + 1)
                        if u >= 2:
                            act.wait_ge(weighed, u - 1)
                        nc.scalar.activation(probs_t[:, u % 2, half * HALF_KEYS:(half + 1) * HALF_KEYS],
                                             k.psum[:, 4 + half, 0:HALF_KEYS], ACT.Copy).then_inc(turned_copied, 1)

                split(0)
                split(1)
                act.wait_ge(lam_step, 2)
                nc.scalar.activation(lam_exp[:], k.psum[:, 7, 0:2], ACT.Exp).then_inc(lam_step, 1)
                def square(u):
                    i, h = units[u]
                    act.wait_ge(out_copied, u + 1)
                    if u >= 2:
                        act.wait_ge(square_done, u - 1)
                    nc.scalar.activation(squared[:, u % 2], k.o[:, i, h * P:(h + 1) * P], ACT.Square,
                                         accum_out=k.squares2[:, i, h]).then_inc(square_done, 1)

                for t in range(n + DEEP + 2):
                    if t < n:
                        exp(t)
                        i, h = units[t]
                        if i == 1 and 1 <= h < DIFF_HEADS - 1:
                            split(h + 1)
                    if 2 <= t < n + 2:
                        copy_turned(t - 2)
                    if t > DEEP + 1:
                        square(t - DEEP - 2)


def gates_stage(k):
    nc = k.nc
    done, copied = k.sem("gate2_done"), k.sem("gate2_copied")
    first = FIRST["gate2"]
    def used(i):
        return (done, 2 * (i + 1))

    with nc.Block(no_gpsimd_drain=True) as block:
        @block.sync
        def _(sp):
            sp.dma_start(k.h_ctx, k.d["ctx"]).then_inc(k.ctx_loaded, 16)
            stream(k, sp, first, 8)

        @block.gpsimd
        def _(pool):
            low_parts(k, pool, first, 8)

        @block.tensor
        def _(pe):
            for c in range(2 * KC):
                if c >= 4:
                    pe.wait_ge(copied, c - 3)
                chunk_products(k, pe, k.psum[:, c % 4], first, c, (k.h_hi, k.h_lo), done)

        @block.scalar
        def _(act):
            for c in range(2 * KC):
                if c % 2 == 0:
                    next_high(k, act, first, c // 2, used)
                act.wait_ge(done, c + 1)
                nc.scalar.activation(k.gates[:, c], k.psum[:, c % 4], ACT.Sigmoid, bias=k.vecs[:, B_GATE + c:B_GATE + c + 1]).then_inc(
                    copied, 1)


def branch_stage(k, branch):
    nc = k.nc
    done, gated = k.branch_sems
    first, before = FIRST["branch2"] + branch * KC // 2, branch * KC
    def used(i):
        return (done, before + 2 * (i + 1))

    with nc.Block(no_gpsimd_drain=True) as block:
        @block.sync
        def _(sp):
            stream(k, sp, first, KC // 2)

        @block.gpsimd
        def _(pool):
            low_parts(k, pool, first, KC // 2)

        @block.scalar
        def _(act):
            for i in range(KC // 2):
                next_high(k, act, first, i, used)

        @block.tensor
        def _(pe):
            for c in range(KC):
                if c >= 4:
                    pe.wait_ge(gated, before + c - 3)
                chunk_products(k, pe, k.psum[:, c % 4], first, c, (k.h_hi, k.h_lo), done)

        @block.vector
        def _(dve):
            dve.wait_ge(k.moved, 16 * k.moves)
            for c in range(KC):
                part = k.gates[:, before + c]
                dve.wait_ge(done, before + c + 1)
                nc.vector.tensor_tensor(part, part, k.psum[:, c % 4], ALU.mult).then_inc(gated, 1)
                if branch == 1:
                    dve.wait_ge(gated, before + c + 1)
                    nc.vector.tensor_tensor(k.gates[:, c], k.gates[:, c], part, ALU.add)


def out2_stage(k):
    nc = k.nc
    done, copied = k.sem("out2_done"), k.sem("out2_copied")
    first = FIRST["out2"]
    def used(i):
        return (done, 2 * (i + 1))

    with nc.Block(no_gpsimd_drain=True) as block:
        @block.sync
        def _(sp):
            stream(k, sp, first, KC // 2)

        @block.gpsimd
        def _(pool):
            low_parts(k, pool, first, KC // 2)

        @block.tensor
        def _(pe):
            for c in range(KC):
                if c >= 4:
                    pe.wait_ge(copied, c - 3)
                chunk_products(k, pe, k.psum[:, c % 4], first, c, (k.h_hi, k.h_lo), done)

        @block.scalar
        def _(act):
            for c in range(KC):
                if c % 2 == 0:
                    next_high(k, act, first, c // 2, used)
                act.wait_ge(done, c + 1)
                nc.scalar.activation(k.y2[:, c], k.psum[:, c % 4], ACT.Copy).then_inc(copied, 1)


def query_stage(k):
    nc = k.nc
    done, copied, squared, stat_done, rooted, scored, scaled, at_vector = (
        k.sem(f"query_{s}") for s in ("done", "copied", "squared", "stat_done", "rooted", "scored", "scaled", "vector"))
    loaded, earlier_loads = stage_loads(k, 1)
    first = FIRST["query"]
    n = 2 * PEER_HEADS
    with ExitStack() as scope:
        def sb(name, shape):
            return scope.enter_context(nc.sbuf_tensor(name, shape, F32))

        keys, raw, square = sb("peer_keys", [P, 2, PEER_KEYS]), sb("query_raw", [P, n, SEQ]), sb("query_square", [P, 2, SEQ])
        rstd, ones = sb("query_rstd", [P, TT, n]), sb("query_ones", [P, 1])
        def used(i):
            return (done, 2 * (i + 1))

        with nc.Block(no_gpsimd_drain=True) as block:
            @block.sync
            def _(sp):
                sp.dma_start(keys[:], k.d["peer_keys"]).then_inc(loaded, 16)
                stream(k, sp, first, 8)

            @block.gpsimd
            def _(pool):
                low_parts(k, pool, first, 8)

            @block.tensor
            def _(pe):
                def stat(c):
                    pe.wait_ge(squared, c + 1)
                    if c == 0:
                        pe.wait_ge(at_vector, 1)
                    for t in range(TT):
                        mm = nc.tensor.matmul(k.psum[:, 4, t * n + c:t * n + c + 1], square[:, c % 2, t * P:(t + 1) * P],
                                              ones[:], start=True, stop=True)
                    mm.then_inc(stat_done, 1)

                for c in range(n):
                    if c >= 4:
                        pe.wait_ge(squared, c - 3)
                        pe.wait_ge(copied, c - 3)
                    chunk_products(k, pe, k.psum[:, c % 4], first, c, (k.h_hi, k.h_lo), done)
                    if c >= 1:
                        stat(c - 1)
                stat(n - 1)
                pe.wait_ge(loaded, earlier_loads + 16)
                pe.wait_ge(copied, n)
                for c in range(n):
                    if c >= 3:
                        pe.wait_ge(scaled, c - 2)
                    for t in range(TT):
                        mm = nc.tensor.matmul(k.psum[:, 5 + c % 3, t * P:(t + 1) * P], raw[:, c, t * P:(t + 1) * P], keys[:, c % 2],
                                              start=True, stop=True)
                    mm.then_inc(scored, 1)

            @block.scalar
            def _(act):
                for c in range(n):
                    if c % 2 == 0:
                        next_high(k, act, first, c // 2, used)
                    act.wait_ge(done, c + 1)
                    if c >= 2:
                        act.wait_ge(stat_done, c - 1)
                    nc.scalar.activation(raw[:, c], k.psum[:, c % 4], ACT.Copy).then_inc(copied, 1)
                    nc.scalar.activation(square[:, c % 2], k.psum[:, c % 4], ACT.Square).then_inc(squared, 1)
                act.wait_ge(stat_done, n)
                nc.scalar.activation(rstd[:].rearrange("p t n -> p (t n)"), k.psum[:, 4, 0:TT * n], ACT.Sqrt, bias=k.eps[:, 0:1],
                                     scale=1.0 / P).then_inc(rooted, 1)

            @block.vector
            def _(dve):
                nc.vector.memset(ones[:], 1.0).then_inc(at_vector, 1)
                dve.wait_ge(rooted, 1)
                k.vstep(nc.vector.reciprocal(rstd[:], rstd[:]))
                for c in range(n):
                    dve.wait_ge(scored, c + 1)
                    nc.vector.tensor_tensor(k.scores[:, :, c], k.psum[:, 5 + c % 3].rearrange("p (t n) -> p t n", t=TT),
                                            rstd[:, :, c:c + 1].broadcast_to([P, TT, PEER_KEYS]), ALU.mult).then_inc(scaled, 1)


def split_high(k, act, m, r):
    n = FIRST["peer"] + r
    act.wait_ge(k.tile_loaded[n % SLOTS], (m - r) * (16 // SLOTS) + 16 * (n // SLOTS + 1))
    k.nc.scalar.activation(parts(k, n)[0], slot(k, n), ACT.Copy).then_inc(k.w_high, 1)


def split_low(k, pool, m, r):
    n = FIRST["peer"] + r
    hi, lo = parts(k, n)
    pool.wait_ge(k.w_high, m + (split_number(FIRST["peer"]) + 1))
    k.nc.gpsimd.tensor_tensor(lo, slot(k, n), hi.bitcast(F32), ALU.subtract).then_inc(k.w_ready, 1)


def wait_parts(k, eng, m):
    eng.wait_ge(k.w_ready, m + (split_number(FIRST["peer"]) + 1))


def refill(k, sp, m, r):
    n = FIRST["peer"] + r
    wait_parts(k, sp, m)
    source = k.weights[n + SLOTS] if isinstance(m, int) else k.weights[bass.ds(m + (n - r + SLOTS), 1)].rearrange("a p n -> p (a n)")
    sp.dma_start(slot(k, n), source).then_inc(k.tile_loaded[n % SLOTS], 16)



def hidden_sync(k, sp, b, r):
    sp.wait_ge(k.gelu_done, 2 * b + 6)
    sp.dma_start(k.hid_dram[bass.ds(b, 1)].rearrange("b p n -> p (b n)"), k.acts[:, r % 2].rearrange("p j t -> p (j t)")).then_inc(
        k.hid_stored[r % 2], 16)
    refill(k, sp, b + 2, r + 2)


def hidden_scalar(k, act, b, r, between=None):
    act.wait_ge(k.hid_stored[r % 2], turns(b, r))
    for jj in range(2):
        act.wait_ge(k.hid_done, 2 * b + (jj + 1))
        k.nc.scalar.activation(k.acts[:, r % 2, jj], k.psum[:, 2 * (r % 2) + jj], ACT.Gelu).then_inc(k.gelu_done, 1)
        if jj == 0 and between is not None:
            between()
    split_high(k, act, b + 2, r + 2)


def hidden_tensor(k, pe, b, r, between=None):
    parity = r % 2
    wait_parts(k, pe, b)
    w_hi, w_lo = parts(k, FIRST["peer"] + r)
    pe.wait_ge(k.gelu_done, 2 * b + 2)
    for jj in range(2):
        for kc in range(KC):
            at = (jj * KC + kc) * P
            mm = split_products(k, k.psum[:, 2 * parity + jj], w_hi[:, at:at + P], w_lo[:, at:at + P],
                                k.h_hi[:, kc], k.h_lo[:, kc], kc == 0, kc == KC - 1)
        mm.then_inc(k.hid_done, 1)
        if jj == 0 and between is not None:
            between()


def peer_choice_stage(k):
    nc = k.nc
    ready, exped, turned, copied = (k.sem(f"choice_{s}") for s in ("ready", "exped", "turned", "copied"))
    loaded, earlier_loads = stage_loads(k, 2)
    quarter = BATCHES // 2 // TT
    loops = quarter // SLOTS
    H, K = PEER_HEADS, PEER_TOPK
    with ExitStack() as scope:
        def sb(name, shape, dt=F32):
            return scope.enter_context(nc.sbuf_tensor(name, shape, dt))

        ramp, ident = sb("choice_ramp", [P, K]), sb("choice_ident", [P, P])
        top, index_u, index = sb("sub_top", [P, 2 * H, K]), sb("sub_index_u", [P, 2 * H, K], U32), sb("sub_index", [P, 2 * H, K])
        cand, best = sb("choice_cand", [P, H, K * K]), sb("choice_best", [P, H, K])
        place, place_a, place_b = (sb(f"choice_place{s}", [P, PAIRS], U32) for s in ("", "_a", "_b"))
        place_f = sb("choice_place_f", [P, PAIRS])
        hot = sb("choice_hot", [P, PAIRS, K])
        picked = sb("choice_picked", [P, 3, 2, PAIRS])
        expo, total = sb("choice_exp", [P, H, K]), sb("choice_total", [P, H])
        with nc.Block(no_gpsimd_drain=True) as block:
            @block.sync
            def _(sp):
                sp.dma_start(ramp[:], k.d["iota"][:, 0:K]).then_inc(loaded, 16)
                sp.dma_start(ident[:], k.d["ident"]).then_inc(loaded, 16)
                for i in range(2):
                    sp.sem_inc(k.hid_stored[i], 16)
                    refill(k, sp, i, i)
                with sp.Fori(0, TT * loops) as g:
                    for r in range(SLOTS):
                        hidden_sync(k, sp, SLOTS * g + r, r)

            @block.gpsimd
            def _(pool):
                split_low(k, pool, 1, 1)
                with pool.Fori(0, TT * loops) as g:
                    for r in range(SLOTS):
                        split_low(k, pool, SLOTS * g + (r + 2), r + 2)

            @block.vector
            def _(dve):
                step = k.vstep

                def best_of(rows, values, places):
                    for r in range(0, K, 8):
                        for j, row in enumerate(rows):
                            nc.vector.max(values(j)[:, r:r + 8], row).then_inc(step.sem, 1)
                            step.n += 1
                        dve.wait_ge(step.sem, step.n)
                        for j, row in enumerate(rows):
                            nc.vector.max_index(places(j)[:, r:r + 8], values(j)[:, r:r + 8], row).then_inc(step.sem, 1)
                            step.n += 1
                        dve.wait_ge(step.sem, step.n)
                        if r + 8 < K:
                            for j, row in enumerate(rows):
                                nc.vector.match_replace(row, values(j)[:, r:r + 8], row, TAKEN).then_inc(step.sem, 1)
                                step.n += 1
                            dve.wait_ge(step.sem, step.n)

                dve.wait_ge(loaded, earlier_loads + 32)
                for t in range(TT):
                    best_of([k.scores[:, t, c] for c in range(2 * H)], lambda j: top[:, j], lambda j: index_u[:, j])
                    step(nc.vector.tensor_copy(index[:], index_u[:]))
                    halves = top[:].rearrange("p (h s) n -> p h s n", s=2)
                    for h in range(H):
                        step(nc.vector.tensor_tensor(cand[:, h].rearrange("p (a b) -> p a b", b=K),
                                                     halves[:, h, 0].unsqueeze(2).broadcast_to([P, K, K]),
                                                     halves[:, h, 1].unsqueeze(1).broadcast_to([P, K, K]), ALU.add))
                    places = place[:].rearrange("p (h n) -> p h n", h=H)
                    best_of([cand[:, h] for h in range(H)], lambda j: best[:, j], lambda j: places[:, j])
                    step(nc.vector.tensor_scalar(place_a[:], place[:], 4, None, ALU.logical_shift_right))
                    step(nc.vector.tensor_scalar(place_b[:], place[:], K - 1, None, ALU.bitwise_and))
                    if t >= 2:
                        dve.wait_ge(copied, t - 1)
                    for s, at in ((0, place_a), (1, place_b)):
                        step(nc.vector.tensor_copy(place_f[:], at[:]))
                        step(nc.vector.tensor_tensor(hot[:], place_f[:].unsqueeze(2).broadcast_to([P, PAIRS, K]),
                                                     ramp[:].unsqueeze(1).broadcast_to([P, PAIRS, K]), ALU.is_equal))
                        hot_h = hot[:].rearrange("p (h n) a -> p h n a", h=H)
                        lists = index[:].rearrange("p (h s) n -> p h s n", s=2)
                        for h in range(H):
                            step(nc.vector.tensor_tensor(hot_h[:, h], hot_h[:, h],
                                                         lists[:, h, s].unsqueeze(1).broadcast_to([P, K, K]), ALU.mult))
                        step(nc.vector.tensor_reduce(picked[:, s, t % 2], hot[:], AX.X, ALU.add))
                    if t >= 1:
                        dve.wait_ge(exped, t)
                    nc.vector.tensor_tensor(expo[:], best[:], best[:, :, 0:1].broadcast_to([P, H, K]), ALU.subtract).then_inc(ready, 1)
                    dve.wait_ge(exped, t + 1)
                    step(nc.vector.tensor_reduce(total[:], expo[:], AX.X, ALU.add))
                    step(nc.vector.reciprocal(total[:], total[:]))
                    nc.vector.tensor_tensor(picked[:, 2, t % 2].rearrange("p (h n) -> p h n", h=H), expo[:],
                                            total[:].unsqueeze(2).broadcast_to([P, H, K]), ALU.mult).then_inc(ready, 1)

            @block.scalar
            def _(act):
                def exp(t):
                    act.wait_ge(ready, 2 * t + 1)
                    nc.scalar.activation(expo[:], expo[:], ACT.Exp).then_inc(exped, 1)

                def copy(t):
                    act.wait_ge(turned, t + 1)
                    nc.scalar.activation(k.pairs[:, :, t * P:(t + 1) * P], k.psum[:, 4 + t % 2, 0:3 * P].rearrange("p (s n) -> p s n", s=3),
                                         ACT.Copy).then_inc(copied, 1)

                act.sem_inc(k.gelu_done, 4)
                split_high(k, act, 1, 1)
                for t in range(TT):
                    with act.Fori(t * loops, (t + 1) * loops) as g:
                        for r in range(SLOTS):
                            hidden_scalar(k, act, SLOTS * g + r, r)
                    exp(t)
                    if t >= 1:
                        copy(t - 1)
                copy(TT - 1)

            @block.tensor
            def _(pe):
                def turn(t):
                    pe.wait_ge(ready, 2 * t + 2)
                    if t >= 2:
                        pe.wait_ge(copied, t - 1)
                    for s in range(3):
                        mm = nc.tensor.transpose(k.psum[:, 4 + t % 2, s * P:(s + 1) * P], picked[:, s, t % 2], ident[:])
                    mm.then_inc(turned, 1)

                pe.wait_ge(loaded, earlier_loads + 32)
                for t in range(TT):
                    with pe.Fori(t * loops, (t + 1) * loops) as g:
                        for r in range(SLOTS):
                            hidden_tensor(k, pe, SLOTS * g + r, r)
                    if t >= 1:
                        turn(t - 1)
                turn(TT - 1)


def move_stage(k, *moves, wait=True):
    nc = k.nc
    k.moves += len(moves)
    with nc.Block(no_gpsimd_drain=True) as block:
        @block.sync
        def _(sp):
            for to, source in moves:
                sp.dma_start(to, source).then_inc(k.moved, 16)
            if wait:
                sp.wait_ge(k.moved, 16 * k.moves)


def peer_gates_stage(k):
    nc = k.nc
    hot, weighted, used, copied = (k.sem(f"gates_{s}") for s in ("hot", "weighted", "used", "copied"))
    loaded, earlier_loads = stage_loads(k, 1)
    stored = [k.sem(f"gates_stored{i}") for i in range(2)]
    GROUP = 8
    HALF_GROUP = GROUP // 2
    steps = SPAN // GROUP
    turns = SEQ // (2 * SPAN)
    within, behind = (0, 1, 1, 1, 1, 1, 0, 0), (2, 2, 2, 2, 2, 1, 0, 0)
    body = len(behind)
    g0 = BATCHES // 2 // body
    assert body % SLOTS == 0 and sum(within + behind) == 2 * steps and BATCHES == (g0 + turns) * body
    shape = [P, GROUP, P]
    index1, index2, gate = (k.pairs[:, s] for s in range(3))
    with ExitStack() as scope:
        def sb(name, dims):
            return scope.enter_context(nc.sbuf_tensor(name, dims, F32))

        iota, hot1, hot2 = sb("iota", [P, P]), sb("hot1", [P, 2, GROUP, P]), sb("hot2", [P, 2, GROUP, P])
        block_gates = sb("block_gates", [P, 2, PEER_KEYS, SPAN])

        def steps_of(first, count):
            return [(at // steps, at % steps, at) for at in range(first, first + count)]

        def steps_within(r):
            return steps_of(sum(within[:r] + behind[:r]), within[r])

        def steps_behind(r):
            return steps_of(sum(within[:r + 1] + behind[:r]), behind[r])

        def tokens(vector, n):
            return vector[:, bass.ds(n * GROUP, GROUP)].unsqueeze(2).broadcast_to(shape)

        with nc.Block(no_gpsimd_drain=True) as block:
            @block.sync
            def _(sp):
                sp.dma_start(iota[:], k.d["iota"]).then_inc(loaded, 16)
                for blk in range(2):
                    sp.sem_inc(stored[blk], 16)
                with sp.Fori(g0, g0 + turns) as g:
                    for r in range(body):
                        hidden_sync(k, sp, body * g + r, r)
                        for blk, step, at in steps_within(r) + steps_behind(r):
                            if step == steps - 1:
                                sp.wait_ge(copied, 2 * steps * g + (3 + at - 2 * steps * g0))
                                sp.dma_start(k.gates_dram[bass.ds(2 * g + (blk - 2 * g0), 1)].rearrange("a p j t -> p (a j t)"),
                                             block_gates[:, blk].rearrange("p j t -> p (j t)")).then_inc(stored[blk], 16)
                for i in range(2):
                    sp.wait_ge(stored[i], 16 + 16 * turns)
                    sp.wait_ge(k.hid_stored[i], 16 + 16 * (BATCHES // 2))

            @block.vector
            def _(dve):
                dve.wait_ge(loaded, earlier_loads + 16)
                dve.sem_inc(used, 2)
                with dve.Fori(0, SEQ // (2 * GROUP)) as g:
                    for b in range(2):
                        n = 2 * g + b
                        dve.wait_ge(used, n + 1)
                        row = iota[:].unsqueeze(1).broadcast_to(shape)
                        nc.vector.tensor_tensor(hot2[:, b], tokens(index2, n), row, ALU.is_equal).then_inc(hot, 1)
                        nc.vector.tensor_tensor(hot1[:, b], tokens(index1, n), row, ALU.is_equal).then_inc(hot, 1)

            @block.gpsimd
            def _(pool):
                with pool.Fori(g0, g0 + turns) as g:
                    for r in range(body):
                        for blk, step, at in steps_behind(r) + (steps_within(r + 1) if r + 1 < body else []):
                            n, b = 2 * steps * g + (at - 2 * steps * g0), step % 2
                            pool.wait_ge(hot, 2 * n + 1)
                            nc.gpsimd.tensor_tensor(hot2[:, b], hot2[:, b], tokens(gate, n), ALU.mult).then_inc(weighted, 1)
                        split_low(k, pool, body * g + (r + 2), r + 2)

            @block.tensor
            def _(pe):
                def sum_gates(g, chosen):
                    for blk, step, at in chosen:
                        n, b = 2 * steps * g + (at - 2 * steps * g0), step % 2
                        pe.wait_ge(copied, n + 1)
                        pe.wait_ge(hot, 2 * n + 2)
                        pe.wait_ge(weighted, n + 1)
                        for i in range(GROUP):
                            column = (i % HALF_GROUP) * P
                            mm = nc.tensor.matmul(k.psum[:, 4 + 2 * b + i // HALF_GROUP, column:column + P], hot1[:, b, i], hot2[:, b, i],
                                                  start=True, stop=True)
                        mm.then_inc(used, 1)

                with pe.Fori(g0, g0 + turns) as g:
                    for r in range(body):
                        hidden_tensor(k, pe, body * g + r, r, lambda: sum_gates(g, steps_within(r)))
                        sum_gates(g, steps_behind(r))

            @block.scalar
            def _(act):
                def copy_gates(g, chosen):
                    for blk, step, at in chosen:
                        n, b = 2 * steps * g + (at - 2 * steps * g0), step % 2
                        if step == 0:
                            act.wait_ge(stored[blk], 16 * g + (16 - 16 * g0))
                        act.wait_ge(used, n + 3)
                        for i in range(2):
                            token = step * GROUP + i * HALF_GROUP
                            ins = nc.scalar.activation(block_gates[:, blk, :, token:token + HALF_GROUP].rearrange("p j t -> p t j"),
                                                       k.psum[:, 4 + 2 * b + i].rearrange("p (t j) -> p t j", t=HALF_GROUP), ACT.Copy)
                        ins.then_inc(copied, 1)

                act.sem_inc(copied, 2)
                with act.Fori(g0, g0 + turns) as g:
                    for r in range(body):
                        hidden_scalar(k, act, body * g + r, r, lambda: copy_gates(g, steps_within(r)))
                        copy_gates(g, steps_behind(r))


def peer_out_stage(k):
    nc = k.nc
    gated, a_high, a_ready, v_done, added, reloaded = (
        k.sem(f"out_{s}") for s in ("gated", "a_high", "a_ready", "v_done", "added", "reloaded"))
    hid_loaded, gate_loaded = ([k.sem(f"out_{s}{i}") for i in range(2)] for s in ("hid_loaded", "gate_loaded"))
    by_batch = k.gates_dram.rearrange("s p (b j) t -> p b s (j t)", j=2)
    spans = SEQ // SPAN
    loops = (BATCHES - 6) // SLOTS
    with ExitStack() as scope:
        def sb(name, dims, kind=F32):
            return scope.enter_context(nc.sbuf_tensor(name, dims, kind))

        gate, hid = sb("gate_tiles", [P, 2, 2 * SEQ]), sb("hid_tiles", [P, 2, 2 * SEQ])
        a_hi, a_lo = sb("a_hi", [P, 2, 2, SEQ], F32R), sb("a_lo", [P, 2, 2, SEQ], F32R)
        flat = "p j t -> p (j t)"

        def each_step(eng, step):
            with eng.Fori(0, loops) as g:
                for r in range(SLOTS):
                    step(SLOTS * g + r, r)
            for b in range(SLOTS * loops, BATCHES):
                step(b, b)

        with nc.Block(no_gpsimd_drain=True) as block:
            @block.sync
            def _(sp):
                def load(b, r):
                    sp.dma_start(hid[:, r % 2], k.hid_dram[bass.ds(b, 1)].rearrange("b p n -> p (b n)")).then_inc(hid_loaded[r % 2], 16)
                    sp.dma_start(gate[:, r % 2].rearrange("p (s n) -> p s n", s=spans),
                                 by_batch[:, bass.ds(b, 1)].rearrange("p b s n -> p (b s) n")).then_inc(gate_loaded[r % 2], 16)

                def step(b, r):
                    if r + 2 < BATCHES:
                        sp.wait_ge(a_ready, b + 1)
                        load(b + 2, r)
                    if r + 1 + SLOTS < BATCHES:
                        refill(k, sp, b + (BATCHES + 1), r + (BATCHES + 1))

                for b in range(2):
                    load(b, b)
                refill(k, sp, BATCHES, BATCHES)
                sp.dma_start(k.x2[:], k.x_dram).then_inc(reloaded, 16)
                each_step(sp, step)
                sp.wait_ge(reloaded, 16)

            @block.scalar
            def _(act):
                def high(b, r):
                    act.wait_ge(gated, 2 * b + 2)
                    nc.scalar.activation(a_hi[:, r % 2].rearrange(flat), hid[:, r % 2], ACT.Copy).then_inc(a_high, 1)

                def step(b, r):
                    if r + 1 < BATCHES:
                        high(b + 1, r + 1)
                    if r + 2 < BATCHES:
                        act.wait_ge(v_done, KC * b + KC)
                        split_high(k, act, b + (BATCHES + 2), r + (BATCHES + 2))

                high(0, 0)
                each_step(act, step)

            @block.gpsimd
            def _(pool):
                def step(b, r):
                    if r + 2 < BATCHES:
                        split_low(k, pool, b + (BATCHES + 2), r + (BATCHES + 2))

                each_step(pool, step)

            @block.vector
            def _(dve):
                def multiply(b, r):
                    parity = r % 2
                    dve.wait_ge(hid_loaded[parity], turns(b, r))
                    dve.wait_ge(gate_loaded[parity], turns(b, r))
                    for jj in range(2):
                        view = hid[:, parity, jj * SEQ:(jj + 1) * SEQ].rearrange("p (s t) -> p s t", s=spans)
                        gates = gate[:, parity].rearrange("p (s j t) -> p s j t", s=spans, j=2)[:, :, jj]
                        nc.vector.tensor_tensor(view, view, gates, ALU.mult).then_inc(gated, 1)

                def low(b, r):
                    dve.wait_ge(a_high, b + 1)
                    nc.vector.tensor_tensor(a_lo[:, r % 2].rearrange(flat), hid[:, r % 2], a_hi[:, r % 2].rearrange(flat).bitcast(F32),
                                            ALU.subtract).then_inc(a_ready, 1)

                def add(b, chunks):
                    for m in chunks:
                        dve.wait_ge(v_done, KC * b + (m + 1))
                        nc.vector.tensor_tensor(k.y3[:, m], k.y3[:, m], k.psum[:, m % 4], ALU.add).then_inc(added, 1)

                def step(b, r):
                    if r + 1 < BATCHES:
                        multiply(b + 1, r + 1)
                    add(b, (0, 1))
                    if r + 1 < BATCHES:
                        low(b + 1, r + 1)
                    add(b, range(2, KC))

                nc.vector.memset(k.ones2[:], 1.0)
                k.vstep(nc.vector.memset(k.y3[:], 0.0))
                dve.sem_inc(added, 4)
                multiply(0, 0)
                low(0, 0)
                each_step(dve, step)

            @block.tensor
            def _(pe):
                def step(b, r):
                    parity = r % 2
                    pe.wait_ge(a_ready, b + 1)
                    wait_parts(k, pe, b + BATCHES)
                    w_hi, w_lo = parts(k, FIRST["peer"] + BATCHES + r)
                    for m in range(KC):
                        pe.wait_ge(added, KC * b + (m + 1))
                        for jj in range(2):
                            at = jj * D + m * P
                            mm = split_products(k, k.psum[:, m % 4], w_hi[:, at:at + P], w_lo[:, at:at + P],
                                                a_hi[:, parity, jj], a_lo[:, parity, jj], jj == 0, jj == 1)
                        mm.then_inc(v_done, 1)

                each_step(pe, step)


def store_stage(k):
    nc = k.nc
    stored = k.sem("out_stored")
    with nc.Block(no_gpsimd_drain=True) as block:
        @block.sync
        def _(sp):
            sp.dma_start(k.d["out"], k.x2[:]).then_inc(stored, 16)
            sp.wait_ge(stored, 16)


def build(nc, d):
    with ExitStack() as whole:
        k = Core()
        k.nc, k.d, k.weights = nc, d, d["weights"]
        k.sem = lambda name: whole.enter_context(nc.semaphore(name))

        def place(scope, kind=F32, **shapes):
            return [scope.enter_context(nc.sbuf_tensor(name, shape, kind)) for name, shape in shapes.items()]

        k.tile_loaded = [k.sem(f"tile_loaded{i}") for i in range(SLOTS)]
        k.loaded = k.sem("vectors_loaded")
        k.moved, k.moves = k.sem("moved"), 0
        k.stage_loaded, k.stage_load_count = k.sem("stage_loaded"), 0
        k.head_norm_sems, k.head_norms = [k.sem(f"head_norm_{s}") for s in ("std_ready", "scaled", "turned", "copied", "rooted")], 0
        k.norm_sems, k.norms = [k.sem(f"norm_{s}") for s in ("squared", "summed", "totalled", "std_ready", "scaled")], 0
        k.vstep = Steps(nc.vector, k.sem("vector_step"))
        k.psum = whole.enter_context(nc.psum_tensor("psum", [P, 8, BANK], F32))
        k.h_dram = nc.dram_tensor("h_dram", (SEQ, D), F32, kind="Internal").ap()
        k.y_dram = nc.dram_tensor("y_dram", (EXPERT_TILES * P, D), F32, kind="Internal").ap()
        k.token_dram = nc.dram_tensor("token_dram", (P * EXPERT_TILES, 1), U32, kind="Internal").ap()
        k.gates_dram = nc.dram_tensor("gates_dram", (SEQ // SPAN, P, PEER_KEYS, SPAN), F32, kind="Internal").ap()
        k.hid_dram = nc.dram_tensor("hid_dram", (BATCHES, P, 2 * SEQ), F32, kind="Internal").ap()
        k.x_dram = nc.dram_tensor("x_dram", (P, KC, SEQ), F32, kind="Internal").ap()
        k.ring, k.mod1, k.mod2, k.vecs, k.eps, k.h = place(
            whole, ring=[P, SLOTS, TILE], mod1=[P, N_MOD], mod2=[P, 2, N_MOD], vecs=[P, N_VECS], eps=[P, 2], h=[P, KC, SEQ])
        k.mod_loaded = [k.sem(f"mod_loaded{i}") for i in range(MOD_SLOTS)]
        k.mod_used, k.mod_summed, k.mod_turned, k.mod_read = (k.sem(f"mod_{s}") for s in ("used", "summed", "turned", "read"))
        k.mod_sum_count = 0
        k.w_hi, k.w_lo = place(whole, F32R, w_hi=[P, 2, TILE], w_lo=[P, 2, TILE])
        k.w_high, k.w_ready = k.sem("tile_high"), k.sem("tile_split")
        k.activation_high, k.activations = k.sem("activation_high"), 0
        k.shifted, k.shifts, k.low_ready, k.lows = k.sem("norm_shifted"), 0, k.sem("norm_low_ready"), 0
        k.branch_sems = k.sem("branch_done"), k.sem("branch_gated")
        k.u_dram = nc.dram_tensor("u_dram", (P, KC, SEQ), F32, kind="Internal").ap()
        k.branch_gates_dram = nc.dram_tensor("branch_gates_dram", (P, 2 * KC, SEQ), F32, kind="Internal").ap()

        def place_parts(scope):
            k.h_hi, k.h_lo = place(scope, F32R, **{f"h_hi_{len(k.part_scopes)}": [P, KC, SEQ], f"h_lo_{len(k.part_scopes)}": [P, KC, SEQ]})
            k.part_scopes.append(scope)

        k.part_scopes = []
        with ExitStack() as main:
            k.x, k.ident, k.ones = place(main, x=[P, KC, SEQ], ident=[P, P], ones=[P, P])
            k.ada_vecs, k.cond = place(main, ada_vecs=[P, N_ADA], cond=[P, KC, 3])
            with ExitStack() as scope:
                k.o, k.squares = place(scope, o=[P, TT, D], squares=[P, TT, 2, HEADS])
                with ExitStack() as attention:
                    k.proj, k.v_b, k.small = place(attention, proj=[P, FM_CHUNKS, SEQ], v_b=[P, TT, HEADS * DH], small=[P, TT, SMALL])
                    flat = k.o[:].rearrange("p t d -> p (t d)")
                    k.mod_tiles = [flat[:, 0:TILE], flat[:, TILE:2 * TILE], k.v_b[:].rearrange("p t d -> p (t d)")]
                    with ExitStack() as starting:
                        (k.ada_rows,) = place(starting, ada_rows=[1, 2, BANK])
                        load_stage(k)
                        ada_stage(k)
                    with ExitStack() as inner:
                        place_parts(inner)
                        norm_stage(k, "norm_mix", k.x, k.h, SEQ, k.mod1[:, SCALE_1:SCALE_1 + KC], k.mod1[:, SHIFT_1:SHIFT_1 + KC],
                                   split=(k.h_hi, k.h_lo))
                        (k.mod_acc,) = place(inner, mod_acc=[P, 5, BANK])
                        in_projection_stage(k)
                    k.causal, k.chosen, k.index_score = place(
                        attention, causal=[P, SEQ], chosen=[P, TT, SEQ], index_score=[P, TT, SEQ])
                    k.neg_cum, k.slope_pos, k.head_rows = place(
                        attention, F32R, neg_cum=[HEADS, 2, SEQ], slope_pos=[HEADS, SEQ], head_rows=[HEADS, HEADS, P])
                    forget_stage(k)
                    index_stage(k)
                    attention_stage(k)
                place_parts(scope)
                head_norm_stage(k, "out1_norm", 2, k.vecs[:, G_OUT:G_OUT + KC], k.squares[:])
                out_projection_stage(k)
            norm_stage(k, "norm_ffn", k.x, k.h, SEQ, k.mod1[:, SCALE_2:SCALE_2 + KC], k.mod1[:, SHIFT_2:SHIFT_2 + KC])
            with ExitStack() as scope:
                k.pick, k.pick_weight, k.route_less = place(
                    scope, pick=[P, 2, TT, EXPERTS], pick_weight=[P, 2, TT], route_less=[P, TT, GROUPS])
                k.expert_row, k.slot_token, k.pick_slot = place(
                    scope, U32, expert_row=[P, EXPERT_TILES], slot_token=[P, EXPERT_TILES], pick_slot=[P, 2, TT])
                router_stage(k)
                plan_stage(k)
                moe_stage(k)
                moe_out_stage(k)
            norm_stage(k, "norm_final", k.x, k.x, SEQ, k.vecs[:, G_FINAL:G_FINAL + KC])
            with ExitStack() as scope:
                place_parts(scope)
                (k.squares2,) = place(scope, squares2=[P, TT, DIFF_HEADS, 1])
                norm_stage(k, "norm_mix2", k.x, k.h, SEQ, k.mod2[:, 0, SCALE_1:SCALE_1 + KC], k.mod2[:, 0, SHIFT_1:SHIFT_1 + KC],
                           split=(k.h_hi, k.h_lo))
                with ExitStack() as early:
                    (k.u,) = place(early, u=[P, KC, SEQ])
                    with ExitStack() as inner:
                        (k.vz,) = place(inner, vz=[P, TT, D])
                        sgu_projection_stage(k)
                        sgu_stage(k)
                    k.h_ctx = k.h[:].rearrange("p c n -> p (c n)")[:, 0:KC * CTX].rearrange("p (c n) -> p c n", c=KC)
                    move_stage(k, (k.u_dram, k.u[:]), (k.x_dram, k.x[:]), wait=False)
                    k.ctx_loaded, k.rope_loaded = k.sem("context_loaded"), k.sem("rope_loaded")
                    (k.gates,) = place(early, gates=[P, 2 * KC, SEQ])
                    gates_stage(k)
                    move_stage(k, (k.branch_gates_dram, k.gates[:]), wait=False)
                k.q2 = k.x
                k.o = k.h[:].rearrange("p c n -> p (c n)").rearrange("p (t d) -> p t d", t=TT)
                with ExitStack() as attention:
                    k.k2, k.v2 = place(attention, k2=[P, KC, KEYS], v2=[P, KT, D])
                    with ExitStack() as inner:
                        k.ctx_hi, k.ctx_lo = place(inner, F32R, ctx_hi=[P, KC, CTX], ctx_lo=[P, KC, CTX])
                        k.rope, k.swap = place(inner, rope=[P, 2, SEQ], swap=[P, P])
                        load_context_stage(k)
                        norm_stage(k, "norm_ctx", k.h_ctx, k.h_ctx, CTX, k.mod2[:, 1, SCALE_1:SCALE_1 + KC],
                                   k.mod2[:, 1, SHIFT_1:SHIFT_1 + KC], split=(k.ctx_hi, k.ctx_lo))
                        (k.mod_acc,) = place(inner, mod_acc_late=[P, 2, BANK])
                        flat = k.v2[:].rearrange("p t d -> p (t d)")
                        k.mod_tiles = [flat[:, i * TILE:(i + 1) * TILE] for i in range(MOD_SLOTS)]
                        qk_stage(k)
                        values_stage(k)
                    diff_attention_stage(k)
                k.u, k.gates = place(scope, u_again=[P, KC, SEQ], gates_again=[P, 2 * KC, SEQ])
                move_stage(k, (k.gates[:], k.branch_gates_dram), (k.u[:], k.u_dram), (k.x[:], k.x_dram), wait=False)
                head_norm_stage(k, "out2_norm", DIFF_HEADS, k.vecs[:, SUBLN:SUBLN + 1].broadcast_to([P, KC]), k.squares2[:],
                                1.0 - LAMBDA_INIT)
                branch_stage(k, 0)
                split_stage(k, k.u)
                branch_stage(k, 1)
                split_stage(k, k.gates)
                k.y2 = k.h
                out2_stage(k)
                norm_stage(k, "norm_post_mix", k.y2, k.y2, SEQ, k.mod2[:, 0, GATE_1:GATE_1 + KC], add_to=k.x)
            norm_stage(k, "norm_ffn2", k.x, k.h, SEQ, k.mod2[:, 0, SCALE_2:SCALE_2 + KC], k.mod2[:, 0, SHIFT_2:SHIFT_2 + KC])
            move_stage(k, (k.x_dram, k.x[:]))
        with ExitStack() as tail:
            with ExitStack() as scope:
                place_parts(scope)
                k.acts, k.pairs = place(scope, hid_acts=[P, 2, 2, SEQ], pairs=[P, 3, SEQ])
                k.hid_done, k.gelu_done = k.sem("memory_hid_done"), k.sem("memory_gelu_done")
                k.hid_stored = [k.sem(f"memory_hid_stored{i}") for i in range(2)]
                with ExitStack() as choice:
                    (k.scores,) = place(choice, scores=[P, TT, 2 * PEER_HEADS, PEER_KEYS])
                    split_stage(k, k.h)
                    query_stage(k)
                    peer_choice_stage(k)
                peer_gates_stage(k)
            k.y3, k.x2, k.ones2 = place(tail, y3=[P, KC, SEQ], x2=[P, KC, SEQ], ones2=[P, P])
            peer_out_stage(k)
            k.ones = k.ones2
            norm_stage(k, "norm_post_ffn", k.y3, k.y3, SEQ, k.mod2[:, 0, GATE_2:GATE_2 + KC], add_to=k.x2)
            store_stage(k)
        return k



def feature_major(w):
    m = w.shape[1]
    return w.reshape(KC, P, m // (2 * P), 2, P).transpose(2, 1, 3, 0, 4).reshape(m // (2 * P), P, TILE)


def token_major(w):
    m = w.shape[1]
    return w.reshape(2, KC // 2, P, m // BANK, BANK).transpose(3, 0, 2, 1, 4).reshape(2 * (m // BANK), P, TILE)


def columns(v):
    return np.ascontiguousarray(v).reshape(-1, P).T


def pack_weights(i):
    w = np.empty((N_TILES, P, TILE), np.float32)

    def put(stage, at, tiles):
        w[FIRST[stage] + at:FIRST[stage] + at + len(tiles)] = tiles

    put("ada1", 0, token_major(i["w_ada"][0][:, 0:2 * D]))
    aq, ak, av, iq, ik, iw, bq, bk, bv, bf = np.split(
        i["w_in"][0], np.cumsum([512, 128, 128, 512, 64, 8, 512, 512, 512]).tolist(), axis=1)
    aq = aq.reshape(D, 2, 4, DH).transpose(0, 2, 1, 3).reshape(D, 512)
    put("in1", 0, feature_major(np.concatenate([aq, iq, bq, bk, ak, ik, ik], axis=1)))
    put("in1", FM_CHUNKS // 2, token_major(bv))
    put("out1", 0, feature_major(i["w_out"][0]))
    w2 = i["w_in_2"][0]
    put("qk2", 0, feature_major(w2[:, 0:2 * D]))
    put("v2", 0, token_major(w2[:, 2 * D:3 * D]))
    put("z2", 0, feature_major(w2[:, 3 * D:4 * D]))
    put("z2", 4, token_major(w2[:, 4 * D:5 * D]))
    put("gate2", 0, feature_major(w2[:, 5 * D:7 * D]))
    put("branch2", 0, feature_major(i["w_branch_attn_2"][0]))
    put("branch2", 4, feature_major(i["w_branch_sgu_2"][0]))
    put("out2", 0, feature_major(i["w_out_2"][0]))
    put("query", 0, feature_major(i["peer_w_query_2"][0]))
    u = i["peer_u_2"][0].reshape(PEER_KEYS, PEER_KEYS // 2, 2, KC, P).transpose(1, 4, 2, 3, 0).reshape(PEER_KEYS // 2, P, TILE)
    v = i["peer_v_2"][0].reshape(PEER_KEYS, PEER_KEYS // 2, TILE).transpose(1, 0, 2)
    put("peer", 0, u)
    put("peer", BATCHES, v)
    return w


def constants():
    t = np.arange(SEQ)
    q = np.arange(P)
    causal = np.zeros((P, SEQ), np.float32)
    causal[:, SEQ - P:] = np.where(q[None, :] > q[:, None], MASKED, 0.0)
    slopes = 2.0 ** -np.arange(1, HEADS + 1)
    head_rows = np.zeros((HEADS, HEADS, P), np.float32)
    head_rows[np.arange(HEADS), np.arange(HEADS)] = 1.0
    n_freq = DH // 4
    inv = (np.float32(10000.0) ** (-np.arange(n_freq, dtype=np.float32) / np.float32(n_freq))).astype(np.float32)
    f = np.arange(P) % DH
    pos = np.where((f < DH // 2)[:, None], (t // 64)[None, :], (t % 64)[None, :]).astype(np.float32)
    angle = (pos * inv[f % n_freq][:, None]).astype(np.float32)
    sign = np.where(f % (DH // 2) < n_freq, -1.0, 1.0)
    rope = np.stack([np.cos(angle), np.sin(angle) * sign[:, None]], axis=1).astype(np.float32)
    swap = np.zeros((P, P), np.float32)
    swap[np.arange(P) ^ n_freq, np.arange(P)] = 1.0
    return {
        "ident": np.eye(P, dtype=np.float32),
        "iota": np.tile(np.arange(P, dtype=np.float32), (P, 1)),
        "tri": (q[:, None, None] + P * np.arange(TT)[None, :, None] <= t[None, None, :]).astype(np.float32),
        "causal": causal,
        "head_rows": head_rows,
        "slope_pos": (slopes[:, None] * (t - (SEQ - P))[None, :]).astype(np.float32),
        "before": (q[:, None] < q[None, :]).astype(np.float32),
        "token": (q[:, None] + P * np.arange(TT)[None, :]).astype(np.float32),
        "prio": np.tile(np.arange(PER_GROUP, 0, -1).astype(np.float32), (P, 1)),
        "rope": rope,
        "swap": swap,
    }


def lay_out(i):
    lam = np.zeros((P, 4), np.float32)
    for n, name in enumerate(("lambda_q1_2", "lambda_k1_2", "lambda_q2_2", "lambda_k2_2")):
        lam[:DH, n] = i[name][0]
    small = np.split(i["w_in"][0], np.cumsum([512, 128, 128, 512, 64, 8, 1536]).tolist(), axis=1)
    rows = lambda w: w.reshape(KC, P, -1).transpose(1, 0, 2)
    return constants() | {
        "weights": pack_weights(i),
        "ada_later": np.concatenate([token_major(i["w_ada"][0][:, 2 * D:]), token_major(i["w_ada_2"][0])]),
        "x": rows(i["x"][0].T),
        "ctx": rows(i["ctx_2"][0].T),
        "ada_vecs": np.concatenate([columns(i["c"]), columns(i["c_2"]), columns(i["c_ctx_2"]), columns(i["b_ada"]),
                                    columns(i["b_ada_2"])], axis=1),
        "vecs": np.concatenate([columns(i[n]) for n in ("g_mix", "g_out_a", "g_out_b", "g_ffn", "g_final", "g_pre_mix_2", "g_post_mix_2",
                                                        "g_pre_ffn_2", "g_post_ffn_2", "b_gate_2", "subln_g_2")] + [lam], axis=1),
        "w_small": rows(np.concatenate([small[2], small[5], small[7]], axis=1)),
        "b_forget": i["b_forget"],
        "w_route": rows(np.concatenate([i["w_group"][0], i["w_router"][0].transpose(1, 0, 2).reshape(D, EXPERTS)], axis=1)),
        "b_route": np.concatenate([i["b_group"], i["b_router"].reshape(1, EXPERTS)], axis=1),
        "experts_in": np.concatenate([i["w_gate"][0], i["w_up"][0]], axis=2).reshape(EXPERTS, KC, P, 2 * FF).transpose(
            0, 2, 1, 3).reshape(EXPERTS * P, KC * 2 * FF),
        "experts_down": i["w_down"][0].reshape(EXPERTS, FF // P, P, D).transpose(0, 2, 1, 3).reshape(EXPERTS * P, FF // P * D),
        "ln_g": i["sgu_ln_g_2"],
        "ln_b": i["sgu_ln_b_2"],
        "sgu_w": i["sgu_w_2"][0].transpose(2, 0, 1),
        "sgu_b": i["sgu_b_2"].reshape(1, D),
        "peer_keys": i["peer_sub_keys_2"][0].transpose(2, 0, 1),
    }


def program(arrays, nc):
    d = {n: nc.dram_tensor("in_" + n, a.shape, F32, kind="ExternalInput").ap() for n, a in arrays.items()}
    d["out"] = nc.dram_tensor("out", (P, KC, SEQ), F32, kind="ExternalOutput").ap()
    return build(nc, d)


def kernel(**inputs):
    import concourse.bacc as bacc
    from concourse.bass_utils import run_bass_kernel_spmd

    arrays = {n: np.ascontiguousarray(a) for n, a in lay_out({n: np.asarray(a) for n, a in inputs.items()}).items()}
    nc = bacc.Bacc("TRN2", target_bir_lowering=False, num_devices=1)
    program(arrays, nc)
    result = run_bass_kernel_spmd(nc, [{"in_" + n: a for n, a in arrays.items()}], core_ids=[0]).results[0]["out"]
    return np.ascontiguousarray(result.transpose(1, 0, 2).reshape(D, SEQ).T).reshape(1, SEQ, D)
```
